# Optimizing a Trainium2 kernel written in Bass

```python
import math
import jax, jax.numpy as jnp
from jax import lax
import numpy as np

D_MODEL = 1024
BATCH = 1
SEQ = 2048
DEPTH = 2
DEC_BATCH = 1
DEC_SEQ = 64
PAST_LEN = 2048

F32 = jnp.float32
CHUNK = 64
Q_BLOCK = 128
EPS = 1e-6
N_EVEN = (DEPTH + 1) // 2
N_ODD = DEPTH // 2
H_A = 4
DK_A = 128
DV_A = 128
CONV_W = 4
H_B = 8
Q_LORA = 384
KV_LORA = 256
D_NOPE = 64
D_ROPE = 32
DV_B = 64
ROPE_THETA = 10000.0
H_C = 8
DK_C = 128
DV_C = 128

W_A = H_A * DV_A
W_B = H_B * DV_B
W_C = H_C * DV_C
QKV_A = H_A * (2 * DK_A + DV_A)
IN_E_SPLITS = (QKV_A, H_A, H_A, W_A, Q_LORA, KV_LORA + D_ROPE, W_B)
IN_E = QKV_A + 2 * H_A + W_A + Q_LORA + KV_LORA + D_ROPE + W_B
IN_O = 2 * H_C * DK_C + 2 * W_C

kernel_name = 'hybrid_streaming_gdn_mla_hgrn2_step'

def split_last(x, sizes):
    return jnp.split(x, np.cumsum(sizes)[:-1].tolist(), axis=-1)

def rmsnorm(x, g):
    xf = x.astype(F32)
    y = xf * lax.rsqrt(jnp.mean(xf * xf, axis=-1, keepdims=True) + EPS)
    return (y * g.astype(F32)).astype(x.dtype)

def l2norm(x):
    xf = x.astype(F32)
    return xf * lax.rsqrt(jnp.sum(xf * xf, axis=-1, keepdims=True) + EPS)

def rope(x, pos):
    half = D_ROPE // 2
    inv = ROPE_THETA ** (-jnp.arange(half, dtype=F32) / half)
    ang = pos.astype(F32)[:, None] * inv[None, :]
    cos, sin = jnp.cos(ang)[:, None, :], jnp.sin(ang)[:, None, :]
    xf = x.astype(F32)
    x1, x2 = xf[..., :half], xf[..., half:]
    return jnp.concatenate([x1 * cos - x2 * sin, x1 * sin + x2 * cos], axis=-1).astype(x.dtype)

def causal_dwconv(x, buf, w):
    xp = jnp.concatenate([buf.astype(x.dtype), x], axis=1)
    y = lax.conv_general_dilated(xp, w[:, None, :].astype(x.dtype), window_strides=(1,), padding='VALID',
                                 dimension_numbers=('NWC', 'WIO', 'NWC'), feature_group_count=x.shape[-1])
    return y, xp[:, -(CONV_W - 1):]

def scan_chunks(chunk_fn, S0, seqs):
    T = seqs[0].shape[2]
    L = CHUNK if T % CHUNK == 0 else T
    n = T // L

    def split(a):
        return jnp.moveaxis(a.reshape(a.shape[:2] + (n, L) + a.shape[3:]), 2, 0)

    S, o = lax.scan(lambda S, xs: chunk_fn(S, *xs), S0, tuple(split(a) for a in seqs))
    o = jnp.moveaxis(o, 0, 2)
    return o.reshape(o.shape[:2] + (T,) + o.shape[4:]), S

def gdn_chunk(S, q, k, v, beta, g):
    L = q.shape[2]
    tril = jnp.tril(jnp.ones((L, L), bool))
    strict = jnp.tril(jnp.ones((L, L), bool), -1)
    gc = jnp.cumsum(g, axis=-1)
    decay = jnp.exp(jnp.where(tril, gc[..., :, None] - gc[..., None, :], -jnp.inf))
    kb = k * beta[..., None]
    M = jnp.einsum('bhid,bhjd->bhij', kb, k) * jnp.where(strict, decay, 0.0)
    rhs = jnp.concatenate([v * beta[..., None], kb * jnp.exp(gc)[..., None]], axis=-1)
    uw = lax.linalg.triangular_solve(M + jnp.eye(L, dtype=F32), rhs, left_side=True, lower=True, unit_diagonal=True)
    u, w = uw[..., :DV_A], uw[..., DV_A:]
    v_new = u - jnp.einsum('bhld,bhde->bhle', w, S)
    attn = jnp.einsum('bhid,bhjd->bhij', q, k) * decay
    o = jnp.einsum('bhld,bhde->bhle', q * jnp.exp(gc)[..., None], S) + jnp.einsum('bhij,bhje->bhie', attn, v_new)
    gl = gc[..., -1:]
    S_new = S * jnp.exp(gl)[..., None] + jnp.einsum('bhld,bhle->bhde', k * jnp.exp(gl - gc)[..., None], v_new)
    return S_new, o

def hgrn_chunk(S, q, k, i, logf):
    L = q.shape[2]
    G = jnp.cumsum(logf, axis=2)
    causal = jnp.tril(jnp.ones((L, L), bool))
    rel = jnp.exp(jnp.where(causal[None, None, :, :, None], G[:, :, :, None, :] - G[:, :, None, :, :], -jnp.inf))
    scores = jnp.einsum('bhtd,bhsd,bhtsd->bhts', q, k, rel)
    o = jnp.einsum('bhtd,bhde->bhte', q * jnp.exp(G), S) + jnp.einsum('bhts,bhse->bhte', scores, i)
    GL = G[:, :, -1:, :]
    S_new = S * jnp.exp(GL[:, :, 0, :])[..., None] + jnp.einsum('bhsd,bhse->bhde', k * jnp.exp(GL - G), i)
    return S_new, o

def chunk_causal_attention(q, k, v, q_pos, k_pos):
    B, Tq, H, Dq = q.shape
    Dv = v.shape[-1]
    scale = (D_NOPE + D_ROPE) ** -0.5
    k_chunk = k_pos // CHUNK

    def block(args):
        qb, pb = args
        s = jnp.einsum('bqhd,bkhd->bhqk', qb, k, preferred_element_type=F32) * scale
        mask = k_chunk[None, :] <= (pb // CHUNK)[:, None]
        p = jax.nn.softmax(jnp.where(mask[None, None], s, -jnp.inf), axis=-1)
        return jnp.einsum('bhqk,bkhd->bqhd', p.astype(v.dtype), v)

    if Tq > Q_BLOCK and Tq % Q_BLOCK == 0:
        nb = Tq // Q_BLOCK
        qb = q.reshape(B, nb, Q_BLOCK, H, Dq).transpose(1, 0, 2, 3, 4)
        o = lax.map(block, (qb, q_pos.reshape(nb, Q_BLOCK)))
        return o.transpose(1, 0, 2, 3, 4).reshape(B, Tq, H, Dv)
    return block((q, q_pos))

def even_mixer(h, pos, k_pos, conv_buf, s_delta, ckv_past, kr_past, w_in, conv_w, a_log, dt_bias,
               g_norm_a, g_q, w_uq, g_kv, w_ukv, w_out):
    B, T, _ = h.shape
    qkv, b_logit, a_logit, z_a, cq, ckv_kr, z_b = split_last(h @ w_in, IN_E_SPLITS)
    qkv_c, conv_new = causal_dwconv(qkv, conv_buf, conv_w)
    qa, ka, va = split_last(jax.nn.silu(qkv_c), (H_A * DK_A, H_A * DK_A, H_A * DV_A))
    qa = (l2norm(qa.reshape(B, T, H_A, DK_A)) * DK_A ** -0.5).transpose(0, 2, 1, 3)
    ka = l2norm(ka.reshape(B, T, H_A, DK_A)).transpose(0, 2, 1, 3)
    va = va.reshape(B, T, H_A, DV_A).astype(F32).transpose(0, 2, 1, 3)
    beta = jax.nn.sigmoid(b_logit.astype(F32)).transpose(0, 2, 1)
    g = (-jnp.exp(a_log.astype(F32)) * jax.nn.softplus(a_logit.astype(F32) + dt_bias.astype(F32))).transpose(0, 2, 1)
    o_a, S_new = scan_chunks(gdn_chunk, s_delta.astype(F32), (qa, ka, va, beta, g))
    o_a = rmsnorm(o_a.transpose(0, 2, 1, 3), g_norm_a).astype(h.dtype)
    o_a = (o_a * jax.nn.silu(z_a).reshape(B, T, H_A, DV_A)).reshape(B, T, W_A)
    q_b = (rmsnorm(cq, g_q) @ w_uq).reshape(B, T, H_B, D_NOPE + D_ROPE)
    q_b = jnp.concatenate([q_b[..., :D_NOPE], rope(q_b[..., D_NOPE:], pos)], axis=-1)
    c_kv = rmsnorm(ckv_kr[..., :KV_LORA], g_kv)
    k_pe = rope(ckv_kr[..., KV_LORA:][:, :, None, :], pos)[:, :, 0, :]
    ckv_all = jnp.concatenate([ckv_past.astype(h.dtype), c_kv], axis=1)
    kr_all = jnp.concatenate([kr_past.astype(h.dtype), k_pe], axis=1)
    Tk = ckv_all.shape[1]
    kv = (ckv_all @ w_ukv).reshape(B, Tk, H_B, D_NOPE + DV_B)
    k_b = jnp.concatenate([kv[..., :D_NOPE], jnp.broadcast_to(kr_all[:, :, None, :], (B, Tk, H_B, D_ROPE))], axis=-1)
    o_b = chunk_causal_attention(q_b, k_b, kv[..., D_NOPE:], pos, k_pos)
    o_b = o_b.reshape(B, T, W_B) * jax.nn.silu(z_b)
    out = jnp.concatenate([o_a, o_b], axis=-1) @ w_out
    return (out, S_new.astype(s_delta.dtype), conv_new.astype(conv_buf.dtype),
            c_kv.astype(ckv_past.dtype), k_pe.astype(kr_past.dtype))

def odd_mixer(h, s_hgrn, lb, w_in, g_norm_c, w_out):
    B, T, _ = h.shape
    q, f, i, z = split_last(h @ w_in, (H_C * DK_C, H_C * DK_C, W_C, W_C))
    fg = lb + (1.0 - lb) * jax.nn.sigmoid(f.astype(F32))

    def heads(a, d):
        return a.reshape(B, T, H_C, d).transpose(0, 2, 1, 3)

    qh = heads(jax.nn.silu(q.astype(F32)), DK_C)
    kh = heads(1.0 - fg, DK_C)
    lh = heads(jnp.log(fg), DK_C)
    ih = heads(i.astype(F32), DV_C)
    o, S_new = scan_chunks(hgrn_chunk, s_hgrn.astype(F32), (qh, kh, ih, lh))
    o = rmsnorm(o.transpose(0, 2, 1, 3), g_norm_c).astype(h.dtype)
    o = (o * jax.nn.silu(z).reshape(B, T, H_C, DV_C)).reshape(B, T, W_C)
    return o @ w_out, S_new.astype(s_hgrn.dtype)

def trunk(x, c, ckv_past, kr_past, s_delta, s_conv, s_hgrn, w_ada, b_ada, g_pre, g_post, w_in_e, conv_w,
          a_log, dt_bias, g_norm_a, g_q, w_uq, g_kv, w_ukv, w_out_e, w_in_o, lb_logits, g_norm_c, w_out_o):
    T = x.shape[1]
    past = ckv_past.shape[2]
    pos = past + jnp.arange(T, dtype=jnp.int32)
    k_pos = jnp.arange(past + T, dtype=jnp.int32)
    mod = jnp.einsum('bd,lde->lbe', jax.nn.silu(c), w_ada) + b_ada[:, None, :]
    p_lb = jax.nn.softmax(lb_logits.astype(F32), axis=0)
    lbs = jnp.cumsum(p_lb, axis=0) - p_lb[0]
    nd, nc, nk, nr, nh = [], [], [], [], []
    for l in range(DEPTH):
        shift, scale, gate = jnp.split(mod[l], 3, axis=-1)
        h = rmsnorm(x, g_pre[l]) * (1.0 + scale[:, None, :]) + shift[:, None, :]
        if l % 2 == 0:
            e = l // 2
            o, S, cb, ck, kr = even_mixer(h, pos, k_pos, s_conv[e], s_delta[e], ckv_past[e], kr_past[e],
                                          w_in_e[e], conv_w[e], a_log[e], dt_bias[e], g_norm_a[e],
                                          g_q[e], w_uq[e], g_kv[e], w_ukv[e], w_out_e[e])
            nd.append(S)
            nc.append(cb)
            nk.append(ck)
            nr.append(kr)
        else:
            j = l // 2
            o, S = odd_mixer(h, s_hgrn[j], lbs[l], w_in_o[j], g_norm_c[j], w_out_o[j])
            nh.append(S)
        x = x + gate[:, None, :] * rmsnorm(o, g_post[l])
    return (x, jnp.stack(nd), jnp.stack(nc), jnp.stack(nk), jnp.stack(nr), jnp.stack(nh))

def setup_inputs(seed: int = 0) -> dict:
    key = jax.random.key(seed)
    ks = jax.random.split(key, 32)
    D = D_MODEL

    def nrm(k, shape, s):
        return jax.random.normal(k, shape, F32) * s

    dt0 = jnp.exp(jax.random.uniform(ks[16], (N_EVEN, H_A), F32, math.log(1e-3), math.log(1e-1)))
    return {
        'x_prompt': nrm(ks[0], (BATCH, SEQ, D), 1.0),
        'x_sample': nrm(ks[1], (DEC_BATCH, DEC_SEQ, D), 1.0),
        'c_prompt': nrm(ks[2], (BATCH, D), 1.0),
        'c_sample': nrm(ks[3], (DEC_BATCH, D), 1.0),
        'cache_ckv': nrm(ks[4], (N_EVEN, DEC_BATCH, PAST_LEN, KV_LORA), 1.0),
        'cache_kr': nrm(ks[5], (N_EVEN, DEC_BATCH, PAST_LEN, D_ROPE), 1.0),
        'state_delta': nrm(ks[6], (N_EVEN, DEC_BATCH, H_A, DK_A, DV_A), 0.1),
        'state_conv': nrm(ks[7], (N_EVEN, DEC_BATCH, CONV_W - 1, QKV_A), 1.0),
        'state_hgrn': nrm(ks[8], (N_ODD, DEC_BATCH, H_C, DK_C, DV_C), 0.1),
        'w_ada': nrm(ks[9], (DEPTH, D, 3 * D), 0.5 * D ** -0.5),
        'b_ada': nrm(ks[10], (DEPTH, 3 * D), 0.01),
        'g_pre': 1.0 + nrm(ks[11], (DEPTH, D), 0.01),
        'g_post': 1.0 + nrm(ks[12], (DEPTH, D), 0.01),
        'w_in_e': nrm(ks[13], (N_EVEN, D, IN_E), D ** -0.5),
        'conv_w': nrm(ks[14], (N_EVEN, CONV_W, QKV_A), CONV_W ** -0.5),
        'a_log': jnp.log(jax.random.uniform(ks[15], (N_EVEN, H_A), F32, 1.0, 16.0)),
        'dt_bias': dt0 + jnp.log(-jnp.expm1(-dt0)),
        'g_norm_a': 1.0 + nrm(ks[17], (N_EVEN, DV_A), 0.01),
        'g_q': 1.0 + nrm(ks[18], (N_EVEN, Q_LORA), 0.01),
        'w_uq': nrm(ks[19], (N_EVEN, Q_LORA, H_B * (D_NOPE + D_ROPE)), Q_LORA ** -0.5),
        'g_kv': 1.0 + nrm(ks[20], (N_EVEN, KV_LORA), 0.01),
        'w_ukv': nrm(ks[21], (N_EVEN, KV_LORA, H_B * (D_NOPE + DV_B)), KV_LORA ** -0.5),
        'w_out_e': nrm(ks[22], (N_EVEN, W_A + W_B, D), (W_A + W_B) ** -0.5),
        'w_in_o': nrm(ks[23], (N_ODD, D, IN_O), D ** -0.5),
        'lb_logits': nrm(ks[24], (DEPTH, H_C * DK_C), 0.1),
        'g_norm_c': 1.0 + nrm(ks[25], (N_ODD, DV_C), 0.01),
        'w_out_o': nrm(ks[26], (N_ODD, W_C, D), W_C ** -0.5),
    }

def reference(x_prompt, x_sample, c_prompt, c_sample, cache_ckv, cache_kr, state_delta, state_conv, state_hgrn,
              w_ada, b_ada, g_pre, g_post, w_in_e, conv_w, a_log, dt_bias, g_norm_a, g_q, w_uq, g_kv, w_ukv,
              w_out_e, w_in_o, lb_logits, g_norm_c, w_out_o):
    Bp = x_prompt.shape[0]
    dt = x_prompt.dtype
    y_prompt, p_delta, p_conv, p_ckv, p_kr, p_hgrn = trunk(
        x_prompt, c_prompt,
        jnp.zeros((N_EVEN, Bp, 0, KV_LORA), dt), jnp.zeros((N_EVEN, Bp, 0, D_ROPE), dt),
        jnp.zeros((N_EVEN, Bp, H_A, DK_A, DV_A), dt), jnp.zeros((N_EVEN, Bp, CONV_W - 1, QKV_A), dt),
        jnp.zeros((N_ODD, Bp, H_C, DK_C, DV_C), dt),
        w_ada, b_ada, g_pre, g_post, w_in_e, conv_w, a_log, dt_bias, g_norm_a, g_q, w_uq, g_kv, w_ukv,
        w_out_e, w_in_o, lb_logits, g_norm_c, w_out_o)
    y_sample, s_delta, s_conv, s_ckv, s_kr, s_hgrn = trunk(
        x_sample, c_sample, cache_ckv, cache_kr, state_delta, state_conv, state_hgrn,
        w_ada, b_ada, g_pre, g_post, w_in_e, conv_w, a_log, dt_bias, g_norm_a, g_q, w_uq, g_kv, w_ukv,
        w_out_e, w_in_o, lb_logits, g_norm_c, w_out_o)
    return (y_prompt, y_sample, p_delta, p_conv, p_ckv, p_kr, p_hgrn, s_delta, s_conv, s_ckv, s_kr, s_hgrn)


_drawn_inputs = setup_inputs


def setup_inputs(seed=0):
    import zlib

    import numpy as np

    out = dict(_drawn_inputs(seed))
    spreads = {}
    factors = {'cache_ckv': 4.759,
     'cache_kr': 8.0,
     'state_hgrn': 33.696,
     'g_pre': 3.876,
     'g_post': 147.438,
     'g_norm_a': 200.0,
     'g_q': 48.417,
     'g_kv': 32.091,
     'g_norm_c': 200.0,
     'a_log': 2.97}
    for name, (base, spread) in spreads.items():
        noise = np.random.default_rng([zlib.crc32(name.encode()), seed]).standard_normal(out[name].shape)
        drawn = base * np.exp(spread * noise) if base else spread * noise
        out[name] = __import__('jax').numpy.asarray(drawn.astype(out[name].dtype))
    for name, factor in factors.items():
        out[name] = (out[name] * factor).astype(out[name].dtype)
    return out
```

```python
from contextlib import ExitStack

import concourse.bass as bass
from concourse import mybir

F32 = mybir.dt.float32
I32 = mybir.dt.int32
ALU = mybir.AluOpType
ACT = mybir.ActivationFunctionType
AX = mybir.AxisListType.X

P = 128
D = 1024
KD = D // P
SEQ = 2048
NT = SEQ // P
TILES = NT + 1
SAMPLE = NT
DEC = 64
CH = 64
PAST = 2048
EPS = 1e-6
HA, DK = 4, 128
QKV = 3 * HA * DK
NCT = QKV // P
HB, NOPE, ROPE, DV = 8, 64, 32, 64
HQ = NOPE + ROPE
QL, KL = 384, 256
IN_E = 3240
HC = 8
IN_O = 4096
LEVELS = (1, 2, 4, 8, 16, 32)
TOK = QKV
EVEN_GROUPS = ((1536, 2048), (2048, 2440), (2440, 2728), (2728, 3240))


class Links:

    def __init__(self, eng, sem, per, tile):
        self.eng, self.sem, self.per, self.k = eng, sem, per, 0
        self.base = tile * per

    def did(self, ins):
        ins.then_inc(self.sem, 1)
        self.k += 1
        return self.k

    def need(self, k):
        self.eng.wait_ge(self.sem, self.base + k)

    def link(self, ins):
        self.need(self.did(ins))

    def end(self):
        assert self.k == self.per, self.k


def stage(nc, ctx):
    def sb(name, shape, dt=F32):
        return ctx.enter_context(nc.sbuf_tensor(name, shape, dt))

    def ps(name, shape=(P, 512)):
        return ctx.enter_context(nc.psum_tensor(name, list(shape), F32))

    sems = []

    def sem(name):
        sems.append(nc.alloc_semaphore(name))
        return sems[-1]

    def clear():
        nc.clear_and_free_semaphores(sems)
        nc.all_engine_barrier()

    ctx.callback(clear)
    return sb, ps, sem


def tiles_of(eng, body):
    with eng.Fori(0, NT // 2 - 1) as i:
        body(i * 2, 0, i)
        body(i * 2 + 1, 1, i)
    body(NT - 2, 0, NT // 2 - 1)
    body(NT - 1, 1, NT // 2 - 1)
    body(SAMPLE, 0, NT // 2)


def last(t):
    return isinstance(t, int) and t == SAMPLE


def cond(t):
    return 1 if last(t) else 0


def modulation(nc, io, keep):
    with ExitStack() as ctx:
        sb, ps, sem = stage(nc, ctx)
        cT = sb("cT", [P, 2, KD])
        scT = sb("scT", [P, KD, 2])
        wa = sb("wa", [P, 2, 3 * D])
        bT = sb("bT", [P, 2, 24])
        gpre = sb("gpre", [P, 2, KD])
        gpost = sb("gpost", [P, 2, KD])
        lb = sb("lbl", [P, 2, KD])
        lt = sb("lt", [P, 4, KD])
        md = sb("md", [P, 2, 24, 2])
        mps = ps("mps", [P, 2, 512])
        consts = sem("m_consts")
        weights = sem("m_weights")
        w_in = [sem("m_w0"), sem("m_w1")]
        silu = sem("m_silu")
        zeroed = sem("m_zeroed")
        used = sem("m_used")
        link = sem("m_link")
        lexp = sem("m_lexp")
        lmax = sem("m_lmax")
        block = ctx.enter_context(nc.Block())

        @block.sync
        def _(sp):
            for j, c in enumerate((io["c_prompt"], io["c_sample"])):
                sp.dma_start(cT[:, j, :], c.rearrange("a (k p) -> p (a k)", p=P), allow_slow_non_contiguous=True).then_inc(consts, 16)
            sp.dma_start(keep["ident"][:, :], io["c_ident"]).then_inc(consts, 16)
            sp.dma_start(keep["cums"][:, :], io["c_cums"]).then_inc(consts, 16)
            sp.dma_start(keep["blk"][:, :], io["c_blk"]).then_inc(consts, 16)
            sp.dma_start(keep["low1"][:, :], io["c_low1"]).then_inc(consts, 16)
            sp.dma_start(keep["strict"][:, :], io["c_strict"]).then_inc(consts, 16)
            sp.dma_start(keep["levels"][:, :, :], io["c_levels"]).then_inc(consts, 16)
            strips = io["w_ada"].rearrange("l (k p) n -> (l k) p n", p=P)
            for p in range(2):
                sp.dma_start(wa[:, p, :], strips[p]).then_inc(w_in[p], 16)
            with sp.Fori(0, KD - 1) as i:
                for p in range(2):
                    sp.wait_ge(used, i * 2 + (p + 1))
                    sp.dma_start(wa[:, p, :], strips[i * 2 + (p + 2)]).then_inc(w_in[p], 16)

        @block.gpsimd
        def _(pool):
            for l in range(2):
                pool.dma_start(gpre[:, l, :], io["g_pre"][l].rearrange("(k p) -> p k", p=P), allow_slow_non_contiguous=True).then_inc(weights, 16)
                pool.dma_start(gpost[:, l, :], io["g_post"][l].rearrange("(k p) -> p k", p=P), allow_slow_non_contiguous=True).then_inc(weights, 16)
                pool.dma_start(bT[:, l, :], io["b_ada"][l].rearrange("(k p) -> p k", p=P), allow_slow_non_contiguous=True).then_inc(weights, 16)
                pool.dma_start(lb[:, l, :], io["lb_logits"][l].rearrange("(k p) -> p k", p=P), allow_slow_non_contiguous=True).then_inc(weights, 16)
            pool.memset(keep["ones"][:, :], 1.0)
            pool.memset(keep["mhalf"][:, :], -0.5).then_inc(silu, 1)

        @block.scalar
        def _(act):
            act.wait_ge(consts, 8 * 16)
            for j in range(2):
                act.activation(scT[:, :, j], cT[:, j, :], ACT.Silu).then_inc(silu, 1)
            act.wait_ge(lmax, 1)
            act.activation(lt[:, 1:3, :], lt[:, 1:3, :], ACT.Exp).then_inc(lexp, 1)

        @block.tensor
        def _(pe):
            pe.wait_ge(silu, 3)
            pe.wait_ge(zeroed, 1)
            for l in range(2):
                with pe.Fori(0, KD // 2) as i:
                    for p in range(2):
                        pe.wait_ge(w_in[p], (i + (l * KD // 2 + 1)) * 16)
                        for ct in range(24):
                            mm = pe.matmul(mps[:, l, 2 * ct:2 * ct + 2], wa[:, p, ct * P:(ct + 1) * P],
                                           scT[:, i * 2 + p, :], start=False, stop=False, skip_group_check=True)
                        mm.then_inc(used, 1)

        @block.vector
        def _(dve):
            ln = Links(dve, link, 11, 0)
            dve.memset(mps[:, :, :], 0.0).then_inc(zeroed, 1)
            dve.wait_ge(weights, 8 * 16)
            dve.wait_ge(consts, 8 * 16)
            ln.link(dve.tensor_tensor(lt[:, 0, :], lb[:, 0, :], lb[:, 1, :], ALU.max))
            for l in range(2):
                t = dve.tensor_tensor(lt[:, 1 + l, :], lb[:, l, :], lt[:, 0, :], ALU.subtract)
            t.then_inc(lmax, 1)
            dve.wait_ge(lexp, 1)
            ln.link(dve.tensor_tensor(lt[:, 0, :], lt[:, 1, :], lt[:, 2, :], ALU.add))
            ln.link(dve.reciprocal(lt[:, 3, :], lt[:, 0, :]))
            ln.link(dve.tensor_tensor(lt[:, 1, :], lt[:, 1, :], lt[:, 3, :], ALU.mult))
            ln.link(dve.tensor_tensor(lt[:, 2, :], lt[:, 2, :], lt[:, 3, :], ALU.mult))
            ln.link(dve.tensor_tensor(lt[:, 2, :], lt[:, 2, :], lt[:, 1, :], ALU.add))
            ln.link(dve.tensor_tensor(keep["lb"][:, 0, :], lt[:, 2, :], lt[:, 1, :], ALU.subtract))
            ln.link(dve.tensor_scalar(keep["lb"][:, 1, :], keep["lb"][:, 0, :], -1.0, 1.0, ALU.mult, ALU.add))
            dve.wait_ge(used, 2 * KD)
            for l in range(2):
                t = dve.tensor_tensor(md[:, l, :, :], mps[:, l, 0:48].rearrange("p (a b) -> p a b", b=2),
                                      bT[:, l, :].unsqueeze(2).to_broadcast([P, 24, 2]), ALU.add)
            ln.link(t)
            for l in range(2):
                for c in range(2):
                    t = dve.tensor_scalar(keep["mA"][:, l, c, :], md[:, l, 8:16, c], 1.0, None, ALU.add)
                    dve.tensor_copy(keep["mB"][:, l, c, :], md[:, l, 0:8, c])
                    u = dve.tensor_tensor(keep["gg"][:, l, c, :], md[:, l, 16:24, c], gpost[:, l, :], ALU.mult)
            ln.link(u)
            for l in range(2):
                for c in range(2):
                    t = dve.tensor_tensor(keep["mA"][:, l, c, :], keep["mA"][:, l, c, :], gpre[:, l, :], ALU.mult)
            ln.link(t)
            ln.end()


def norm_transpose(layer, keep, xt, xn, ms, rs, hT, xps, S):

    def dve_norm(dve, t, p, i):
        dve.wait_ge(S["x_in"][p], (i + 1) * 16)
        dve.wait_ge(S["xT"], t * 2)
        dve.tensor_tensor_reduce(xn[:, :], xt[:, p, :], xt[:, p, :], 1.0 / D, EPS,
                                 ALU.mult, ALU.add, ms[:, 0:1]).then_inc(S["x_ms"], 1)
        dve.wait_ge(S["x_rs"], t + 1)
        dve.tensor_scalar(xn[:, :], xt[:, p, :], rs[:, 0:1], None, ALU.mult).then_inc(S["xn"], 1)

    def pool_norm(pool, t):
        pool.wait_ge(S["x_ms"], t + 1)
        pool.tensor_tensor(rs[:, 0:1], ms[:, 0:1], keep["mhalf"][:, 0:1], ALU.pow).then_inc(S["x_rs"], 1)

    def pe_transposes(pe, t):
        pe.wait_ge(S["xn"], t + 1)
        pe.wait_ge(S["hT_a"], t)
        pe.wait_ge(S["hT_v"], t)
        for k in range(KD):
            mm = pe.transpose(xps[k // 4][:, (k % 4) * P:(k % 4 + 1) * P], xn[:, k * P:(k + 1) * P], keep["ident"][:, :])
            if k % 4 == 3:
                mm.then_inc(S["xT"], 1)

    def act_hT(act, t, p):
        act.wait_ge(S["xT"], t * 2 + 1)
        for k in range(4):
            u = act.activation(hT[:, p, k, :], xps[0][:, k * P:(k + 1) * P], ACT.Identity,
                               bias=keep["mB"][:, layer, cond(t), k:k + 1], scale=keep["mA"][:, layer, cond(t), k:k + 1])
        u.then_inc(S["hT_a"], 1)

    def dve_hT(dve, t, p):
        dve.wait_ge(S["xT"], t * 2 + 2)
        for k in range(4, 8):
            u = dve.tensor_scalar(hT[:, p, k, :], xps[1][:, (k - 4) * P:(k - 3) * P],
                                  keep["mA"][:, layer, cond(t), k:k + 1], keep["mB"][:, layer, cond(t), k:k + 1],
                                  ALU.mult, ALU.add)
        u.then_inc(S["hT_v"], 1)

    return dve_norm, pool_norm, pe_transposes, act_hT, dve_hT


def norm_sems(sem, tag):
    S = {n: sem(f"{tag}_{n}") for n in ("x_ms", "x_rs", "xn", "xT", "hT_a", "hT_v")}
    S["x_in"] = [sem(f"{tag}_x_in0"), sem(f"{tag}_x_in1")]
    return S


def in_even(nc, io, keep, scr):
    with ExitStack() as ctx:
        sb, ps, sem = stage(nc, ctx)
        w = sb("a_w", [P, KD, IN_E])
        xt = sb("a_xt", [P, 2, D])
        xn = sb("a_xn", [P, D])
        hT = sb("a_hT", [P, 2, KD, P])
        xp = sb("a_xp", [P, NCT, P + 3])
        cv = sb("a_cv", [P, 2, NCT, P])
        z = sb("a_z", [P, 2, D])
        ba = sb("a_ba", [P, 2, 8])
        cq = sb("a_cq", [P, QL])
        kv = sb("a_kv", [P, KL + ROPE])
        cqn = sb("a_cqn", [P, 2, QL])
        kvn = sb("a_kvn", [P, 2, KL + ROPE])
        junk = sb("a_junk", [P, QL + KL])
        cs = sb("a_cs", [P, 2, 64])
        rt = sb("a_rt", [P, 2, ROPE])
        cw = sb("a_cw", [P, 4, NCT])
        gq = sb("a_gq", [P, QL])
        gkv = sb("a_gkv", [P, KL])
        ms = sb("a_ms", [P, 1])
        rs = sb("a_rs", [P, 1])
        ms2 = sb("a_ms2", [P, 2])
        rs2 = sb("a_rs2", [P, 2])
        xps = [ps("a_x0"), ps("a_x1")]
        bank = [ps(f"a_p{i}") for i in range(6)]
        S = norm_sems(sem, "a")
        cs_in = [sem("a_cs_in0"), sem("a_cs_in1")]
        stored = [sem("a_stored0"), sem("a_stored1")]
        w_in, const_in = sem("a_w_in"), sem("a_const_in")
        proj, act_out, kv_out = sem("a_proj"), sem("a_act_out"), sem("a_kv_out")
        conv, silu_q, hist = sem("a_conv"), sem("a_silu_q"), sem("a_hist")
        lat_ms, lat_rs, lat = sem("a_lat_ms"), sem("a_lat_rs"), sem("a_lat")
        link, hist_in, hist_out = sem("a_link"), sem("a_hist_in"), sem("a_hist_out")
        dve_norm, pool_norm, pe_tr, act_hT, dve_hT = norm_transpose(0, keep, xt, xn, ms, rs, hT, xps, S)
        block = ctx.enter_context(nc.Block())
        STORES = 6
        OUTS = 6

        @block.sync
        def _(sp):
            def load(t, p):
                if last(t):
                    sp.dma_start(xt[0:DEC, p, :], io["x_sample"][0]).then_inc(S["x_in"][p], 16)
                else:
                    sp.dma_start(xt[:, p, :], io["x_prompt"][0].rearrange("(t p) d -> t p d", p=P)[t]).then_inc(S["x_in"][p], 16)
                sp.dma_start(cs[:, p, :], io["c_rope"][t]).then_inc(cs_in[p], 16)

            load(0, 0)
            sp.dma_start(gq[:, :], io["g_q"][0:1, :].to_broadcast([P, QL])).then_inc(const_in, 16)
            sp.dma_start(gkv[:, :], io["g_kv"][0:1, :].to_broadcast([P, KL])).then_inc(const_in, 16)
            for j in range(4):
                sp.dma_start(cw[:, j, :], io["conv_w"][0, j].rearrange("(c p) -> p c", p=P), allow_slow_non_contiguous=True).then_inc(const_in, 16)
            for k in range(KD):
                sp.dma_start(w[:, k, :], io["w_in_e"][0, k * P:(k + 1) * P, :]).then_inc(w_in, 16)

            def step(t, p, i):
                if not last(t):
                    sp.wait_ge(S["xn"], t)
                    sp.wait_ge(lat, t)
                    load(t + 1, 1 - p)
                sp.wait_ge(silu_q, t + 1)
                sp.dma_start(scr["qkv"][t], cv[:, p, :, :]).then_inc(stored[p], 16)
                sp.wait_ge(act_out, (t + 1) * OUTS)
                sp.dma_start(scr["z"][t], z[:, p, :]).then_inc(stored[p], 16)
                sp.dma_start(scr["ba"][t], ba[:, p, :]).then_inc(stored[p], 16)
                sp.wait_ge(lat, t + 1)
                sp.dma_start(scr["cq"][t], cqn[:, p, :]).then_inc(stored[p], 16)
                if last(t):
                    ck, kr, n = io["s_ckv"][0, 0], io["s_kr"][0, 0], DEC
                else:
                    ck = io["p_ckv"][0, 0].rearrange("(t p) c -> t p c", p=P)[t]
                    kr, n = io["p_kr"][0, 0].rearrange("(t p) c -> t p c", p=P)[t], P
                sp.dma_start(ck, kvn[0:n, p, 0:KL]).then_inc(stored[p], 16)
                sp.dma_start(kr, kvn[0:n, p, KL:KL + ROPE]).then_inc(stored[p], 16)

            tiles_of(sp, step)
            for p in range(2):
                sp.wait_ge(stored[p], (TILES + 1 - p) // 2 * STORES * 16)

        @block.gpsimd
        def _(pool):
            def conv_rows(dst, at, cols):
                for j in range(3):
                    pool.dma_start(dst[0, 0, j].rearrange("(c p) -> p c", p=P), xp[:, :, at + j], allow_slow_non_contiguous=True).then_inc(cols, 16)

            def step(t, p, i):
                if isinstance(t, int) and t == NT - 1:
                    pool_norm(pool, t + 1)
                    pool.wait_ge(act_out, t * OUTS + 3)
                    conv_rows(io["p_conv"], P, hist_out)
                    pool.wait_ge(hist, NT)
                    for j in range(3):
                        pool.dma_start(xp[:, :, j], io["state_conv"][0, 0, j].rearrange("(c p) -> p c", p=P), allow_slow_non_contiguous=True).then_inc(hist_in, 16)
                elif last(t):
                    pool.wait_ge(act_out, t * OUTS + 3)
                    conv_rows(io["s_conv"], DEC, hist_out)
                else:
                    pool_norm(pool, t + 1)
                pool.wait_ge(lat_ms, t + 1)
                pool.tensor_tensor(rs2[:, :], ms2[:, :], keep["mhalf"][:, 0:2], ALU.pow).then_inc(lat_rs, 1)

            pool_norm(pool, 0)
            tiles_of(pool, step)
            pool.wait_ge(hist_out, 6 * 16)

        @block.scalar
        def _(act):
            def step(t, p, i):
                act.wait_ge(hist, t)
                if last(t):
                    act.wait_ge(hist_out, 3 * 16)
                for g in range(3):
                    act.wait_ge(proj, t * 7 + g + 1)
                    act.copy(xp[:, 4 * g:4 * g + 4, 3:], bank[g][:, :].rearrange("p (c t) -> p c t", c=4)).then_inc(act_out, 1)
                if not last(t):
                    act_hT(act, t + 1, 1 - p)
                act.wait_ge(proj, t * 7 + 4)
                act.wait_ge(stored[p], i * (STORES * 16))
                act.copy(ba[:, p, :], bank[3][:, 0:8])
                act.activation(z[:, p, 0:504], bank[3][:, 8:512], ACT.Silu).then_inc(act_out, 1)
                act.wait_ge(proj, t * 7 + 5)
                act.wait_ge(lat, t)
                act.activation(z[:, p, 504:512], bank[4][:, 0:8], ACT.Silu)
                act.copy(cq[:, :], bank[4][:, 8:392]).then_inc(act_out, 1)
                act.wait_ge(conv, t + 1)
                act.activation(cv[:, p, :, :], cv[:, p, :, :], ACT.Silu).then_inc(silu_q, 1)
                act.wait_ge(proj, t * 7 + 7)
                act.activation(z[:, p, 512:1024], bank[0][:, :], ACT.Silu).then_inc(act_out, 1)

            act.wait_ge(S["xT"], 1)
            act_hT(act, 0, 0)
            tiles_of(act, step)

        @block.tensor
        def _(pe):
            def step(t, p, i):
                pe.wait_ge(S["hT_a"], t + 1)
                pe.wait_ge(S["hT_v"], t + 1)
                pe.wait_ge(act_out, t * OUTS)
                for g in range(3):
                    for c in range(4 * g, 4 * g + 4):
                        for k in range(KD):
                            mm = pe.matmul(bank[g][:, (c % 4) * P:(c % 4 + 1) * P], w[:, k, c * P:(c + 1) * P],
                                           hT[:, p, k, :], start=k == 0, stop=k == KD - 1)
                    mm.then_inc(proj, 1)
                if not last(t):
                    pe_tr(pe, t + 1)
                for g, (a, b) in enumerate(EVEN_GROUPS):
                    dst = bank[0] if g == 3 else bank[3 + g]
                    if g == 2:
                        pe.wait_ge(kv_out, t)
                    if g == 3:
                        pe.wait_ge(act_out, t * OUTS + 1)
                    for k in range(KD):
                        mm = pe.matmul(dst[:, 0:b - a], hT[:, p, k, :], w[:, k, a:b], start=k == 0, stop=k == KD - 1)
                    mm.then_inc(proj, 1)

            pe_tr(pe, 0)
            pe.wait_ge(w_in, 16 * KD)
            tiles_of(pe, step)

        @block.vector
        def _(dve):
            def step(t, p, i):
                ln = Links(dve, link, 6, t)
                if not last(t):
                    dve_norm(dve, t + 1, 1 - p, i + p)
                dve.wait_ge(act_out, t * OUTS + 3)
                if last(t):
                    dve.wait_ge(hist_in, 3 * 16)
                dve.wait_ge(stored[p], i * (STORES * 16))
                for c in range(NCT):
                    u = dve.tensor_scalar(cv[:, p, c, :], xp[:, c, 0:P], cw[:, 0, c:c + 1], None, ALU.mult)
                for j in range(1, 4):
                    ln.link(u)
                    for c in range(NCT):
                        u = dve.scalar_tensor_tensor(out=cv[:, p, c, :], in0=xp[:, c, j:j + P], scalar=cw[:, j, c:c + 1],
                                                     in1=cv[:, p, c, :], op0=ALU.mult, op1=ALU.add)
                u.then_inc(conv, 1)
                dve.wait_ge(conv, t + 1)
                dve.tensor_copy(xp[:, :, 0:3], xp[:, :, P:P + 3]).then_inc(hist, 1)
                if not last(t):
                    dve_hT(dve, t + 1, 1 - p)
                dve.wait_ge(proj, t * 7 + 6)
                dve.tensor_copy(kv[:, :], bank[5][:, 0:KL + ROPE]).then_inc(kv_out, 1)
                dve.wait_ge(kv_out, t + 1)
                dve.wait_ge(act_out, t * OUTS + 5)
                dve.tensor_tensor_reduce(junk[:, 0:QL], cq[:, :], cq[:, :], 1.0 / QL, EPS, ALU.mult, ALU.add, ms2[:, 0:1])
                dve.tensor_tensor_reduce(junk[:, QL:QL + KL], kv[:, 0:KL], kv[:, 0:KL], 1.0 / KL, EPS, ALU.mult, ALU.add,
                                         ms2[:, 1:2]).then_inc(lat_ms, 1)
                dve.wait_ge(cs_in[p], (i + 1) * 16)
                dve.tensor_tensor(rt[:, 0, :], kv[:, KL:KL + ROPE], cs[:, p, 0:32], ALU.mult)
                dve.tensor_tensor(rt[:, 1, 0:16], kv[:, KL + 16:KL + 32], cs[:, p, 32:48], ALU.mult)
                ln.link(dve.tensor_tensor(rt[:, 1, 16:32], kv[:, KL:KL + 16], cs[:, p, 48:64], ALU.mult))
                ln.link(dve.tensor_tensor(kvn[:, p, KL:KL + ROPE], rt[:, 0, :], rt[:, 1, :], ALU.add))
                dve.wait_ge(lat_rs, t + 1)
                ln.link(dve.scalar_tensor_tensor(out=kvn[:, p, 0:KL], in0=kv[:, 0:KL], scalar=rs2[:, 1:2], in1=gkv[:, :],
                                                 op0=ALU.mult, op1=ALU.mult))
                dve.scalar_tensor_tensor(out=cqn[:, p, :], in0=cq[:, :], scalar=rs2[:, 0:1], in1=gq[:, :],
                                         op0=ALU.mult, op1=ALU.mult).then_inc(lat, 1)
                ln.end()

            dve.memset(xp[:, :, 0:3], 0.0)
            dve.wait_ge(const_in, 6 * 16)
            dve_norm(dve, 0, 0, 0)
            dve_hT(dve, 0, 0)
            tiles_of(dve, step)


def bc(ap, n):
    return ap.unsqueeze(2).to_broadcast([ap.shape[0], ap.shape[1], n])


def over_heads(ap, h):
    return ap.unsqueeze(1).to_broadcast([ap.shape[0], h, ap.shape[1]])


def delta(nc, io, keep, scr):
    H = HA
    with ExitStack() as ctx:
        sb, ps, sem = stage(nc, ctx)
        sc = sb("d_sc", [P, 2, 3 * H, P])
        ba = sb("d_ba", [P, 2, 8])
        za = sb("d_za", [P, 2, H * P])
        dtb, nea, gna = sb("d_dtb", [P, H]), sb("d_nea", [P, H]), sb("d_gna", [P, P])
        x8, e8, u8, l4, w4 = (sb(f"d_{n}", [P, 8]) for n in ("x8", "e8", "u8", "l4", "w4"))
        xa, beta, g = sb("d_xa", [P, H]), sb("d_beta", [P, H]), sb("d_g", [P, H])
        gB = sb("d_gB", [P, H, P])
        g8, ge8, bg = sb("d_g8", [P, 8]), sb("d_ge8", [P, 8]), sb("d_bg", [P, H])
        EB, Dm, Em = sb("d_EB", [P, H, P]), sb("d_Dm", [P, H, P]), sb("d_Em", [P, H, P])
        qk, sq = sb("d_qk", [P, 2 * H, P]), sb("d_sq", [P, 2 * H, P])
        ss8, r8, qs8 = sb("d_ss8", [P, 8]), sb("d_r8", [P, 8]), sb("d_qs8", [P, 8])
        vb, kb, kd = sb("d_vb", [P, H, P]), sb("d_kb", [P, H, P]), sb("d_kd", [P, H, P])
        qkT, qe = sb("d_qkT", [P, 2 * H, P]), sb("d_qe", [P, H, P])
        M, MT, A = sb("d_M", [P, H, P]), sb("d_MT", [P, H, P]), sb("d_A", [P, H, P])
        CT = sb("d_CT", [P, 6, H, P])
        T, U, X = sb("d_T", [P, H, P]), sb("d_U", [P, H, P]), sb("d_X", [P, H, P])
        wT, u, vn = sb("d_wT", [P, H, P]), sb("d_u", [P, H, P]), sb("d_vn", [P, H, P])
        St = sb("d_S", [P, H, P])
        o, osq, gz = sb("d_o", [P, H, P]), sb("d_osq", [P, H, P]), sb("d_gz", [P, H, P])
        os4, or4 = sb("d_os4", [P, H]), sb("d_or4", [P, H])
        oT = sb("d_oT", [P, 2, H, P])
        B = [ps(f"d_b{i}") for i in range(5)]
        names = ("x8 e8 u8 ln g gB gc gcB g8 t8 ge8 EB DE E12 mask qkvT qk_out v_out ss r8 qkn qkT qkT_out kbkd kk M A MT "
                 "MT_out T1 U1 wu wT_out u_out o_ps o_out os or4 gz og normed ogT oT_out beta qe bg vb_out").split()
        R = {n: sem("d_" + n) for n in names}
        CTs, Xs, Xo, YYs, TUs = sem("d_CTs"), sem("d_Xs"), sem("d_Xo"), sem("d_YYs"), sem("d_TUs")
        wSs, vns, kvs, Ss = sem("d_wSs"), sem("d_vns"), sem("d_kvs"), sem("d_Ss")
        in_, stored = [sem("d_in0"), sem("d_in1")], [sem("d_st0"), sem("d_st1")]
        const_in, state_out, state_in, s0 = sem("d_const"), sem("d_s_out"), sem("d_s_in"), sem("d_s0")
        link, plink, ea, qs_in = sem("d_link"), sem("d_plink"), sem("d_ea"), sem("d_qs_in")
        block = ctx.enter_context(nc.Block())
        flat = lambda b: b.rearrange("p h t -> p (h t)")
        heads = lambda b: b[:, :].rearrange("p (h t) -> p h t", h=H)

        def state(ap):
            return ap.rearrange("h d e -> d h e")

        @block.sync
        def _(sp):
            sp.dma_start(dtb[:, :], io["dt_bias"][0:1, :].to_broadcast([P, H])).then_inc(const_in, 16)
            sp.dma_start(nea[:, :], io["a_log"][0:1, :].to_broadcast([P, H])).then_inc(const_in, 16)
            sp.dma_start(gna[:, :], io["g_norm_a"][0:1, :].to_broadcast([P, P])).then_inc(const_in, 16)

            def load(t, p):
                sp.dma_start(sc[:, p, :, :], scr["qkv"][t]).then_inc(in_[p], 16)
                sp.dma_start(ba[:, p, :], scr["ba"][t]).then_inc(in_[p], 16)
                sp.dma_start(za[:, p, :], scr["z"][t, :, 0:H * P]).then_inc(in_[p], 16)

            load(0, 0)

            def step(t, p, i):
                if not last(t):
                    sp.wait_ge(R["og"], t)
                    load(t + 1, 1 - p)
                sp.wait_ge(R["oT_out"], t + 1)
                sp.dma_start(scr["oa"][t], flat(oT[:, p, :, :])).then_inc(stored[p], 16)
                if isinstance(t, int) and t == NT - 1:
                    sp.wait_ge(Ss, 2 * NT)
                    sp.dma_start(state(io["p_delta"][0, 0]), St[:, :, :]).then_inc(state_out, 16)
                    sp.wait_ge(state_out, 16)
                    sp.dma_start(St[:, :, :], state(io["state_delta"][0, 0])).then_inc(state_in, 16)
                if last(t):
                    sp.wait_ge(Ss, 2 * NT + 1)
                    sp.dma_start(state(io["s_delta"][0, 0]), St[:, :, :]).then_inc(state_out, 16)

            tiles_of(sp, step)
            sp.wait_ge(state_out, 32)
            sp.wait_ge(stored[0], (TILES + 1) // 2 * 16)
            sp.wait_ge(stored[1], TILES // 2 * 16)

        @block.gpsimd
        def _(pool):
            def step(t, p, i):
                ln = Links(pool, plink, 4, t)
                pool.wait_ge(in_[p], (i + 1) * 48)
                pool.wait_ge(R["og"], t)
                pool.tensor_tensor(gz[:, :, :], za[:, p, :].rearrange("p (h t) -> p h t", h=H), over_heads(gna[:, :], H), ALU.mult).then_inc(R["gz"], 1)
                pool.wait_ge(R["ss"], t + 1)
                ln.link(pool.tensor_tensor(r8[:, :], ss8[:, :], keep["mhalf"][:, :], ALU.pow))
                pool.tensor_tensor(r8[:, :], r8[:, :], qs8[:, :], ALU.mult).then_inc(R["r8"], 1)
                pool.wait_ge(R["E12"], t + 1)
                ln.link(pool.tensor_tensor(Dm[:, :, :], Dm[:, :, :], over_heads(keep["strict"][:, :], H), ALU.mult))
                pool.tensor_tensor(Dm[:, :, :], Dm[:, :, :], bc(beta[:, :], P), ALU.mult)
                pool.tensor_tensor(Em[:, :, :], Em[:, :, :], over_heads(keep["cums"][:, :], H), ALU.mult).then_inc(R["mask"], 1)
                pool.wait_ge(R["qkn"], t + 1)
                pool.wait_ge(R["bg"], t + 1)
                pool.tensor_tensor(kb[:, :, :], qk[:, H:2 * H, :], bc(bg[:, :], P), ALU.mult)
                pool.tensor_tensor(kd[:, :, :], qk[:, H:2 * H, :], bc(ge8[:, H:8], P), ALU.mult).then_inc(R["kbkd"], 1)
                pool.wait_ge(R["M"], t + 1)
                ln.link(pool.tensor_tensor(T[:, :, :], M[:, :, :], over_heads(keep["low1"][:, :], H), ALU.mult))
                pool.tensor_tensor(T[:, :, :], over_heads(keep["ident"][:, :], H), T[:, :, :], ALU.subtract).then_inc(R["T1"], 1)
                pool.wait_ge(R["MT_out"], t + 1)
                for n in range(6):
                    c = pool.tensor_tensor(CT[:, n, :, :], MT[:, :, :], over_heads(keep["levels"][:, n, :], H), ALU.mult)
                    if n == 0:
                        ln.link(c)
                        pool.tensor_tensor(U[:, :, :], over_heads(keep["ident"][:, :], H), CT[:, 0, :, :], ALU.subtract).then_inc(R["U1"], 1)
                    else:
                        c.then_inc(CTs, 1)
                pool.wait_ge(R["os"], t + 1)
                pool.tensor_tensor(or4[:, :], os4[:, :], keep["mhalf"][:, 0:H], ALU.pow).then_inc(R["or4"], 1)
                ln.end()

            pool.memset(qs8[:, 0:H], float(DK) ** -0.5)
            pool.memset(qs8[:, H:8], 1.0).then_inc(qs_in, 1)
            pool.wait_ge(qs_in, 1)
            pool.wait_ge(const_in, 48)
            tiles_of(pool, step)

        @block.scalar
        def _(act):
            def step(t, p, i):
                act.wait_ge(R["qkvT"], t * 3 + 2)
                act.copy(flat(qk[:, 0:H, :]), B[2][:, :])
                act.copy(flat(qk[:, H:2 * H, :]), B[3][:, :]).then_inc(R["qk_out"], 1)
                act.wait_ge(R["x8"], t + 1)
                act.activation(e8[:, :], x8[:, :], ACT.Exp, scale=-1.0).then_inc(R["e8"], 1)
                act.wait_ge(R["u8"], t + 1)
                act.activation(l4[:, 0:H], u8[:, H:8], ACT.Ln).then_inc(R["ln"], 1)
                act.wait_ge(R["gcB"], t + 1)
                act.activation(flat(EB[:, :, :]), B[1][:, :], ACT.Exp).then_inc(R["EB"], 1)
                act.wait_ge(R["t8"], t + 1)
                act.activation(ge8[:, :], g8[:, :], ACT.Exp).then_inc(R["ge8"], 1)
                act.wait_ge(R["DE"], t + 1)
                act.activation(Dm[:, :, :], Dm[:, :, :], ACT.Exp, scale=-1.0)
                act.activation(Em[:, :, :], Em[:, :, :], ACT.Exp).then_inc(R["E12"], 1)
                act.wait_ge(R["qkT"], t + 1)
                act.copy(flat(qkT[:, 0:H, :]), B[2][:, :])
                act.copy(flat(qkT[:, H:2 * H, :]), B[3][:, :]).then_inc(R["qkT_out"], 1)
                act.wait_ge(R["MT"], t + 1)
                act.copy(flat(MT[:, :, :]), B[1][:, :]).then_inc(R["MT_out"], 1)
                for n in range(5):
                    act.wait_ge(Xs, t * 5 + n + 1)
                    act.copy(flat(X[:, :, :]), B[0][:, :]).then_inc(Xo, 1)
                act.wait_ge(R["wu"], t + 1)
                act.copy(flat(wT[:, :, :]), B[0][:, :]).then_inc(R["wT_out"], 1)
                act.copy(flat(u[:, :, :]), B[1][:, :]).then_inc(R["u_out"], 1)
                act.wait_ge(R["o_ps"], t + 1)
                act.copy(flat(o[:, :, :]), B[4][:, :]).then_inc(R["o_out"], 1)
                act.wait_ge(R["ogT"], t + 1)
                act.wait_ge(stored[p], i * 16)
                act.copy(flat(oT[:, p, :, :]), B[0][:, :]).then_inc(R["oT_out"], 1)

            act.wait_ge(const_in, 48)
            act.activation(nea[:, :], nea[:, :], ACT.Exp).then_inc(ea, 1)
            tiles_of(act, step)

        @block.tensor
        def _(pe):
            ident, cums = keep["ident"], keep["cums"]

            def step(t, p, i):
                pe.wait_ge(in_[p], (i + 1) * 48)
                pe.wait_ge(R["oT_out"], t)
                for n in range(3):
                    for h in range(H):
                        mm = pe.transpose(B[2 + n][:, h * P:(h + 1) * P], sc[:, p, n * H + h, :], ident[:, :])
                    mm.then_inc(R["qkvT"], 1)
                pe.wait_ge(R["g"], t + 1)
                pe.matmul(B[0][:, 0:H], cums[:, :], g[:, :], start=True, stop=True)
                pe.matmul(B[0][:, H:8], keep["blk"][:, :], g[:, :], start=True, stop=True).then_inc(R["gc"], 1)
                pe.wait_ge(R["gB"], t + 1)
                for h in range(H):
                    mm = pe.matmul(B[1][:, h * P:(h + 1) * P], gB[:, h, :], cums[:, :], start=True, stop=True)
                mm.then_inc(R["gcB"], 1)
                pe.wait_ge(R["qkn"], t + 1)
                for h in range(2 * H):
                    mm = pe.transpose(B[2 + h // H][:, h % H * P:(h % H + 1) * P], qk[:, h, :], ident[:, :])
                mm.then_inc(R["qkT"], 1)
                pe.wait_ge(R["qkT_out"], t + 1)
                pe.wait_ge(R["g8"], t + 1)
                pe.wait_ge(R["v_out"], t + 1)
                for h in range(H):
                    pe.matmul(B[0][:, h * P:(h + 1) * P], qkT[:, H + h, :], qkT[:, H + h, :], start=True, stop=True)
                    mm = pe.matmul(B[4][:, h * P:(h + 1) * P], qkT[:, H + h, :], qkT[:, h, :], start=True, stop=True)
                mm.then_inc(R["kk"], 1)
                pe.wait_ge(R["M"], t + 1)
                pe.wait_ge(R["DE"], t + 1)
                for h in range(H):
                    mm = pe.transpose(B[1][:, h * P:(h + 1) * P], M[:, h, :], ident[:, :])
                mm.then_inc(R["MT"], 1)
                pe.wait_ge(R["T1"], t + 1)
                pe.wait_ge(R["U1"], t + 1)
                for n in range(5):
                    pe.wait_ge(CTs, t * 5 + n + 1)
                    if n:
                        pe.wait_ge(TUs, t * 5 + n)
                    for h in range(H):
                        mm = pe.matmul(B[0][:, h * P:(h + 1) * P], CT[:, n + 1, h, :], T[:, h, :], start=True, stop=True)
                    mm.then_inc(Xs, 1)
                    pe.wait_ge(Xo, t * 5 + n + 1)
                    for h in range(H):
                        if n < 4:
                            pe.matmul(B[2][:, h * P:(h + 1) * P], U[:, h, :], X[:, h, :], start=True, stop=True)
                        mm = pe.matmul(B[3][:, h * P:(h + 1) * P], X[:, h, :], U[:, h, :], start=True, stop=True)
                    mm.then_inc(YYs, 1)
                pe.wait_ge(TUs, t * 5 + 5)
                pe.wait_ge(R["kbkd"], t + 1)
                pe.wait_ge(R["v_out"], t + 1)
                for h in range(H):
                    pe.matmul(B[0][:, h * P:(h + 1) * P], kb[:, h, :], U[:, h, :], start=True, stop=True)
                    mm = pe.matmul(B[1][:, h * P:(h + 1) * P], U[:, h, :], vb[:, h, :], start=True, stop=True)
                mm.then_inc(R["wu"], 1)
                pe.wait_ge(R["wT_out"], t + 1)
                pe.wait_ge(R["qe"], t + 1)
                pe.wait_ge(R["A"], t + 1)
                if last(t):
                    pe.wait_ge(state_in, 16)
                else:
                    pe.wait_ge(s0, 1)
                for c in range(2):
                    lo, hi = c * CH, (c + 1) * CH
                    if c:
                        pe.wait_ge(Ss, t * 2 + 1)
                    elif not last(t):
                        pe.wait_ge(Ss, t * 2)
                    for h in range(H):
                        mm = pe.matmul(B[2][lo:hi, h * P:(h + 1) * P], wT[:, h, lo:hi], St[:, h, :], start=True, stop=True)
                    mm.then_inc(wSs, 1)
                    for h in range(H):
                        mm = pe.matmul(B[4][lo:hi, h * P:(h + 1) * P], qe[:, h, lo:hi], St[:, h, :],
                                       start=h == 0, stop=False, skip_group_check=True)
                    pe.wait_ge(vns, t * 2 + c + 1)
                    if not (last(t) and c):
                        for h in range(H):
                            mm = pe.matmul(B[3][:, h * P:(h + 1) * P], kd[lo:hi, h, :], vn[lo:hi, h, :], start=True, stop=True)
                        mm.then_inc(kvs, 1)
                for h in range(H):
                    mm = pe.matmul(B[4][:, h * P:(h + 1) * P], A[:, h, :], vn[:, h, :],
                                   start=False, stop=h == H - 1, skip_group_check=True)
                mm.then_inc(R["o_ps"], 1)
                pe.wait_ge(R["og"], t + 1)
                for h in range(H):
                    mm = pe.transpose(B[0][:, h * P:(h + 1) * P], o[:, h, :], ident[:, :])
                mm.then_inc(R["ogT"], 1)

            tiles_of(pe, step)

        @block.vector
        def _(dve):
            def step(t, p, i):
                ln = Links(dve, link, 9, t)
                dve.wait_ge(in_[p], (i + 1) * 48)
                dve.wait_ge(R["e8"], t)
                dve.tensor_copy(x8[:, 0:H], ba[:, p, 0:H])
                ln.link(dve.tensor_tensor(xa[:, :], ba[:, p, H:8], dtb[:, :], ALU.add))
                dve.scalar_tensor_tensor(out=x8[:, H:8], in0=xa[:, :], scalar=-1.0, in1=xa[:, :], op0=ALU.mult, op1=ALU.max).then_inc(R["x8"], 1)
                dve.wait_ge(R["e8"], t + 1)
                dve.tensor_scalar(u8[:, :], e8[:, :], 1.0, None, ALU.add).then_inc(R["u8"], 1)
                dve.wait_ge(R["u8"], t + 1)
                dve.reciprocal(beta[:, :], u8[:, 0:H]).then_inc(R["beta"], 1)
                ln.link(dve.tensor_scalar(w4[:, 0:H], u8[:, H:8], -1.0, None, ALU.add))
                ln.link(dve.tensor_tensor(w4[:, 0:H], e8[:, H:8], w4[:, 0:H], ALU.subtract))
                dve.wait_ge(R["ln"], t + 1)
                ln.link(dve.tensor_tensor(w4[:, 0:H], w4[:, 0:H], l4[:, 0:H], ALU.add))
                ln.link(dve.scalar_tensor_tensor(out=w4[:, 0:H], in0=xa[:, :], scalar=0.0, in1=w4[:, 0:H], op0=ALU.max, op1=ALU.add))
                dve.scalar_tensor_tensor(out=g[:, :], in0=w4[:, 0:H], scalar=-1.0, in1=nea[:, :], op0=ALU.mult, op1=ALU.mult).then_inc(R["g"], 1)
                dve.wait_ge(R["g"], t + 1)
                dve.tensor_copy(gB[:, :, :], bc(g[:, :], P)).then_inc(R["gB"], 1)
                dve.wait_ge(R["qk_out"], t + 1)
                ln.link(dve.tensor_tensor(sq[:, :, :], qk[:, :, :], qk[:, :, :], ALU.mult))
                ln.link(dve.tensor_reduce(ss8[:, :], sq[:, :, :], AX, ALU.add))
                dve.tensor_scalar(ss8[:, :], ss8[:, :], EPS, None, ALU.add).then_inc(R["ss"], 1)
                dve.wait_ge(R["qkvT"], t * 3 + 3)
                dve.wait_ge(R["beta"], t + 1)
                dve.tensor_tensor(vb[:, :, :], heads(B[4]), bc(beta[:, :], P), ALU.mult).then_inc(R["v_out"], 1)
                dve.wait_ge(R["gc"], t + 1)
                dve.tensor_copy(g8[:, :], B[0][:, 0:8]).then_inc(R["g8"], 1)
                dve.wait_ge(R["g8"], t + 1)
                dve.wait_ge(R["EB"], t + 1)
                for h in range(H):
                    dve.tensor_scalar(Dm[:, h, :], B[1][:, h * P:(h + 1) * P], g8[:, h:h + 1], 0.0, ALU.subtract, ALU.max)
                    d = dve.tensor_scalar(Em[:, h, :], B[1][:, h * P:(h + 1) * P], g8[:, h:h + 1], 0.0, ALU.subtract, ALU.min)
                d.then_inc(R["DE"], 1)
                dve.tensor_tensor(g8[:, H:8], g8[:, H:8], g8[:, 0:H], ALU.subtract).then_inc(R["t8"], 1)
                dve.wait_ge(R["ge8"], t + 1)
                dve.tensor_tensor(bg[:, :], beta[:, :], ge8[:, 0:H], ALU.mult).then_inc(R["bg"], 1)
                dve.wait_ge(R["r8"], t + 1)
                dve.tensor_tensor(qk[:, :, :], qk[:, :, :], bc(r8[:, :], P), ALU.mult).then_inc(R["qkn"], 1)
                dve.wait_ge(R["qkT_out"], t + 1)
                dve.tensor_tensor(qe[:, :, :], qkT[:, 0:H, :], EB[:, :, :], ALU.mult).then_inc(R["qe"], 1)
                dve.wait_ge(R["kk"], t + 1)
                dve.wait_ge(R["mask"], t + 1)
                dve.tensor_tensor(M[:, :, :], heads(B[0]), Dm[:, :, :], ALU.mult).then_inc(R["M"], 1)
                dve.tensor_tensor(A[:, :, :], heads(B[4]), Em[:, :, :], ALU.mult).then_inc(R["A"], 1)
                for n in range(5):
                    dve.wait_ge(YYs, t * 5 + n + 1)
                    if n < 4:
                        dve.tensor_tensor(T[:, :, :], T[:, :, :], heads(B[2]), ALU.subtract)
                    dve.tensor_tensor(U[:, :, :], U[:, :, :], heads(B[3]), ALU.subtract).then_inc(TUs, 1)
                dve.wait_ge(R["u_out"], t + 1)
                for c in range(2):
                    lo, hi = c * CH, (c + 1) * CH
                    dve.wait_ge(wSs, t * 2 + c + 1)
                    dve.tensor_tensor(flat(vn[lo:hi, :, :]), flat(u[lo:hi, :, :]), B[2][lo:hi, :], ALU.subtract).then_inc(vns, 1)
                    if not (last(t) and c):
                        dve.wait_ge(kvs, t * 2 + c + 1)
                        for h in range(H):
                            d = dve.scalar_tensor_tensor(out=St[:, h, :], in0=St[:, h, :], scalar=EB[:, h, hi - 1:hi],
                                                         in1=B[3][:, h * P:(h + 1) * P], op0=ALU.mult, op1=ALU.add)
                        d.then_inc(Ss, 1)
                dve.wait_ge(R["o_out"], t + 1)
                ln.link(dve.tensor_tensor(osq[:, :, :], o[:, :, :], o[:, :, :], ALU.mult))
                ln.link(dve.tensor_reduce(os4[:, :], osq[:, :, :], AX, ALU.add))
                dve.tensor_scalar(os4[:, :], os4[:, :], 1.0 / P, EPS, ALU.mult, ALU.add).then_inc(R["os"], 1)
                dve.wait_ge(R["or4"], t + 1)
                dve.wait_ge(R["gz"], t + 1)
                dve.tensor_tensor(o[:, :, :], o[:, :, :], bc(or4[:, :], P), ALU.mult).then_inc(R["normed"], 1)
                dve.wait_ge(R["normed"], t + 1)
                dve.tensor_tensor(o[:, :, :], o[:, :, :], gz[:, :, :], ALU.mult).then_inc(R["og"], 1)
                ln.end()

            dve.memset(St[:, :, :], 0.0).then_inc(s0, 1)
            dve.wait_ge(ea, 1)
            tiles_of(dve, step)


def keys(nc, io, keep, scr, kT, V, sample):
    G = 4
    tag = "ks" if sample else "kp"
    with ExitStack() as ctx:
        sb, ps, sem = stage(nc, ctx)
        wk = sb(f"{tag}_w", [P, 2, HB * P])
        ck = sb(f"{tag}_ck", [P, 2, G, KL])
        kr = sb(f"{tag}_kr", [P, 2, G, HQ])
        cT = sb(f"{tag}_cT", [P, 2, 4 * P])
        bT = [ps(f"{tag}_t{i}") for i in range(3)]
        bK = [ps(f"{tag}_k{i}") for i in range(4)]
        w_in = sem(f"{tag}_w_in")
        in_ = [sem(f"{tag}_in0"), sem(f"{tag}_in1")]
        tr, tr_out, kr_out = sem(f"{tag}_tr"), sem(f"{tag}_tr_out"), sem(f"{tag}_kr_out")
        mmk, k_a, k_v, zeroed = sem(f"{tag}_mm"), sem(f"{tag}_k_a"), sem(f"{tag}_k_v"), sem(f"{tag}_zero")
        block = ctx.enter_context(nc.Block())
        if sample:
            ckd = io["cache_ckv"][0, 0].rearrange("(g j p) c -> g p j c", p=P, j=G)
            krd = io["cache_kr"][0, 0].rearrange("(g j p) c -> g p j c", p=P, j=G)
        else:
            ckd = io["p_ckv"][0, 0].rearrange("(g j p) c -> g p j c", p=P, j=G)
            krd = io["p_kr"][0, 0].rearrange("(g j p) c -> g p j c", p=P, j=G)

        @block.sync
        def _(sp):
            sp.dma_start(wk[:, :, :], io["w_ukv"][0].rearrange("(k p) n -> p k n", p=P)).then_inc(w_in, 16)
            sp.wait_ge(zeroed, 1)
            for g in range(4):
                p = g % 2
                if g >= 2:
                    sp.wait_ge(tr, g - 1)
                sp.dma_start(ck[:, p, :, :], ckd[g]).then_inc(in_[p], 16)
                sp.dma_start(kr[:, p, :, NOPE:HQ], krd[g]).then_inc(in_[p], 16)
            if sample:
                sp.wait_ge(tr, 3)
                sp.dma_start(ck[0:DEC, 0, 0, :], io["s_ckv"][0, 0]).then_inc(in_[0], 16)
                sp.dma_start(kr[0:DEC, 0, 0, NOPE:HQ], io["s_kr"][0, 0]).then_inc(in_[0], 16)

        N = 5 if sample else 4

        def parts(g):
            return (1, DEC) if g == 4 else (G, P)

        @block.tensor
        def _(pe):
            pe.wait_ge(w_in, 16)
            n = 0
            for g in range(N):
                p = g % 2
                tiles, rows = parts(g)
                width = (tiles - 1) * P + rows
                pe.wait_ge(in_[p], (g // 2 + 1) * 32)
                if g:
                    pe.wait_ge(tr_out, g)
                    pe.wait_ge(kr_out, g)
                for j in range(tiles):
                    for k in range(2):
                        pe.transpose(bT[k][:, j * P:j * P + rows], ck[0:rows, p, j, k * P:(k + 1) * P], keep["ident"][0:rows, 0:rows])
                    mm = pe.transpose(bT[2][0:HQ, j * P:j * P + rows], kr[0:rows, p, j, :], keep["ident"][0:rows, 0:rows])
                mm.then_inc(tr, 1)
                pe.wait_ge(tr_out, g + 1)
                for m in range(HB + tiles):
                    b = bK[n % 4]
                    if n >= 4:
                        if n % 2:
                            pe.wait_ge(k_v, (n - 4) // 2 + 1)
                        else:
                            pe.wait_ge(k_a, (n - 4) // 2 + 1)
                    for k in range(2):
                        if m < HB:
                            mm = pe.matmul(b[0:NOPE, 0:width], wk[:, k, m * P:m * P + NOPE], cT[:, k, 0:width], start=k == 0, stop=k == 1)
                        else:
                            j = m - HB
                            mm = pe.matmul(b[0:rows, :].rearrange("p (h e) -> p h e", h=HB), cT[:, k, j * P:j * P + rows],
                                           wk[:, k, :].rearrange("p (h e) -> p h e", h=HB)[:, :, NOPE:P], start=k == 0, stop=k == 1)
                    mm.then_inc(mmk, 1)
                    n += 1

        def drain(eng, copy, odd, done):
            def f(g, n):
                tiles, rows = parts(g)
                width = (tiles - 1) * P + rows
                for m in range(HB + tiles):
                    if n % 2 == odd:
                        eng.wait_ge(mmk, n + 1)
                        b = bK[n % 4]
                        if m < HB:
                            copy(kT[0:NOPE, m, g * G * P:g * G * P + width], b[0:NOPE, 0:width]).then_inc(done, 1)
                        else:
                            copy(V[0:rows, g * G + m - HB, :, 0:DV],
                                 b[0:rows, :].rearrange("p (h e) -> p h e", h=HB)).then_inc(done, 1)
                    n += 1
                return n
            return f

        @block.scalar
        def _(act):
            f, n = drain(act, act.copy, 0, k_a), 0
            for g in range(N):
                tiles, rows = parts(g)
                width = (tiles - 1) * P + rows
                act.wait_ge(tr, g + 1)
                if g:
                    act.wait_ge(mmk, n)
                act.copy(cT[:, 0, 0:width], bT[0][:, 0:width])
                act.copy(cT[:, 1, 0:width], bT[1][:, 0:width]).then_inc(tr_out, 1)
                n = f(g, n)

        @block.vector
        def _(dve):
            dve.memset(kr[:, :, :, 0:NOPE], 0.0).then_inc(zeroed, 1)
            dve.memset(V[:, :, :, DV:DV + 1], 1.0)
            f, n = drain(dve, dve.tensor_copy, 1, k_v), 0
            for g in range(N):
                tiles, rows = parts(g)
                width = (tiles - 1) * P + rows
                dve.wait_ge(tr, g + 1)
                dve.tensor_copy(kT[NOPE:HQ, :, g * G * P:g * G * P + width],
                                bT[2][NOPE:HQ, 0:width].unsqueeze(1).to_broadcast([ROPE, HB, width])).then_inc(kr_out, 1)
                n = f(g, n)


def attention(nc, io, keep, scr, kT, V, sample):
    tag = "s" if sample else "q"
    tiles = [SAMPLE] if sample else list(range(NT))
    with ExitStack() as ctx:
        sb, ps, sem0 = stage(nc, ctx)
        sem = lambda n: sem0(f"{tag}_{n}")
        wu = sb(f"{tag}_wu", [P, 3, HB * HQ])
        cq = sb(f"{tag}_cq", [P, 2, QL])
        cs = sb(f"{tag}_cs", [P, 2, 64])
        zb = sb(f"{tag}_zb", [P, 2, HB * DV])
        cqT = sb(f"{tag}_cqT", [P, 3, P])
        qb = sb(f"{tag}_qb", [P, HB, HQ])
        rt = sb(f"{tag}_rt", [P, 2, HB, ROPE])
        qT = sb(f"{tag}_qT", [P, HB, P])
        qc = sb(f"{tag}_qc", [P, 2, P])
        Pr = sb(f"{tag}_P", [P, 2, 17 * P])
        mx = sb(f"{tag}_mx", [P, 2, 8])
        PT = sb(f"{tag}_PT", [P, 2, 512])
        rc = sb(f"{tag}_rc", [P, 1])
        ob = sb(f"{tag}_ob", [P, HB * DV])
        obT = sb(f"{tag}_obT", [P, 2, 512])
        sps = ps(f"{tag}_sps", [P, 5, 512])
        tps = [ps(f"{tag}_t0"), ps(f"{tag}_t1")]
        ops = ps(f"{tag}_o")
        w_in = sem("w_in")
        in_, stored = [sem("in0"), sem("in1")], [sem("st0"), sem("st1")]
        cqt, cqt_out, qps, qb_out, roped, qbt, qT_out, zero = (sem(n) for n in ("cqt", "cqt_out", "qps", "qb_out", "roped", "qbt", "qT_out", "zero"))
        qc_r, sc_r, mx_r, exp_r, tr_r, pt_a, pt_v, pv_r, o_r, obt, obt_out, parts, inv, init = (
            sem(n) for n in ("qc", "scores", "max", "exp", "tr", "pt_a", "pt_v", "pv", "o", "obt", "obt_out", "parts", "inv", "init"))
        block = ctx.enter_context(nc.Block())
        scale = float(HQ) ** -0.5
        flat = sps[:, :, :].rearrange("p a b -> p (a b)")

        class Size:

            def __init__(self, t, m, prev):
                self.n = PAST + DEC if sample else (t + 1) * P
                self.own = 0 if sample else CH
                self.kt = -(-self.n // P)
                self.nb = -(-self.n // 512)
                self.ng = -(-self.kt // 4)
                self.na, self.nv = (self.ng + 1) // 2, self.ng // 2
                self.q0 = m * HB
                self.sc0 = prev.sc0 + HB * prev.nb if prev else 0
                self.tr0 = prev.tr0 + HB * prev.ng if prev else 0
                self.a0 = prev.a0 + HB * prev.na if prev else 0
                self.v0 = prev.v0 + HB * prev.nv if prev else 0

            def bank(self, b):
                return 512 * b, min(self.n, 512 * (b + 1))

        sizes = []
        for m, t in enumerate(tiles):
            sizes.append(Size(t, m, sizes[-1] if sizes else None))

        def heads(eng, body):
            with eng.Fori(0, HB // 2 - 1) as i:
                body(i * 2, 0, True)
                body(i * 2 + 1, 1, True)
            body(HB - 2, 0, True)
            body(HB - 1, 1, False)

        @block.sync
        def _(sp):
            sp.dma_start(wu[:, :, :], io["w_uq"][0].rearrange("(k p) n -> p k n", p=P)).then_inc(w_in, 16)

            def load(m):
                if m >= 2:
                    sp.wait_ge(obt, m - 1)
                sp.dma_start(cq[:, m % 2, :], scr["cq"][tiles[m]]).then_inc(in_[m % 2], 16)
                sp.dma_start(cs[:, m % 2, :], io["c_rope"][tiles[m]]).then_inc(in_[m % 2], 16)
                sp.dma_start(zb[:, m % 2, :], scr["z"][tiles[m], :, 512:1024]).then_inc(in_[m % 2], 16)

            load(0)
            for m, t in enumerate(tiles):
                if m + 1 < len(tiles):
                    load(m + 1)
                sp.wait_ge(obt_out, m + 1)
                sp.dma_start(scr["ob"][t], obT[:, m % 2, :]).then_inc(stored[m % 2], 16)
            for p in range(min(2, len(tiles))):
                sp.wait_ge(stored[p], (len(tiles) + 1 - p) // 2 * 16)

        @block.gpsimd
        def _(pool):
            for m, z in enumerate(sizes):
                if z.own:
                    if m:
                        pool.wait_ge(pv_r, z.q0)
                    for p in range(2):
                        u = pool.memset(Pr[0:CH, p, z.n - z.own:z.n], 0.0)
                    u.then_inc(zero, 1)
                elif z.n < z.kt * P:
                    for p in range(2):
                        u = pool.memset(Pr[:, p, z.n:z.kt * P], 0.0)
                    u.then_inc(zero, 1)
                pool.wait_ge(qT_out, m + 1)
                with pool.Fori(0, HB // 2) as i:
                    for p in range(2):
                        pool.wait_ge(sc_r, i * (2 * z.nb) + z.sc0)
                        pool.tensor_copy(qc[0:HQ, p, :], qT[0:HQ, i * 2 + p, :]).then_inc(qc_r, 1)

        @block.tensor
        def _(pe):
            pe.wait_ge(w_in, 16)
            ident = keep["ident"]
            for m, z in enumerate(sizes):
                pe.wait_ge(in_[m % 2], (m // 2 + 1) * 48)
                if m:
                    pe.wait_ge(obt_out, m)
                for k in range(3):
                    mm = pe.transpose(tps[0][:, k * P:(k + 1) * P], cq[:, m % 2, k * P:(k + 1) * P], ident[:, :])
                mm.then_inc(cqt, 1)
                pe.wait_ge(cqt_out, m + 1)
                for b in range(2):
                    for k in range(3):
                        mm = pe.matmul(tps[b][:, 0:384], cqT[:, k, :], wu[:, k, b * 384:(b + 1) * 384], start=k == 0, stop=k == 2)
                mm.then_inc(qps, 1)
                pe.wait_ge(roped, m + 1)
                for h in range(HB):
                    mm = pe.transpose(tps[h // 4][0:HQ, h % 4 * P:(h % 4 + 1) * P], qb[:, h, :], ident[:, :])
                mm.then_inc(qbt, 1)
                pe.wait_ge(qT_out, m + 1)

                def scores(h, p):
                    pe.wait_ge(qc_r, h + (z.q0 + 1))
                    for b in range(z.nb):
                        lo, hi = z.bank(b)
                        if isinstance(h, int) and h == 0:
                            pe.wait_ge(exp_r, z.sc0)
                        else:
                            pe.wait_ge(exp_r, h * z.nb + (z.sc0 + b + 1 - z.nb))
                        pe.matmul(sps[:, b, 0:hi - lo], qc[0:HQ, p, :], kT[0:HQ, h, lo:hi],
                                  start=True, stop=True).then_inc(sc_r, 1)

                def transposes(h, p, b):
                    n = (h * z.na if b % 2 == 0 else h * z.nv) + ((z.a0 if b % 2 == 0 else z.v0) + b // 2)
                    pe.wait_ge(pt_a if b % 2 == 0 else pt_v, n)
                    for j in range(4 * b, min(4 * b + 4, z.kt)):
                        mm = pe.transpose(tps[b % 2][:, (j % 4) * P:(j % 4 + 1) * P], Pr[:, p, j * P:(j + 1) * P], ident[:, :])
                    mm.then_inc(tr_r, 1)

                def product(h, b):
                    n = (h * z.na if b % 2 == 0 else h * z.nv) + ((z.a0 if b % 2 == 0 else z.v0) + b // 2 + 1)
                    pe.wait_ge(pt_a if b % 2 == 0 else pt_v, n)
                    if b == 0:
                        pe.wait_ge(o_r, h + z.q0)
                    for j in range(4 * b, min(4 * b + 4, z.kt)):
                        rows = min(P, z.n - j * P)
                        mm = pe.matmul(ops[:, 0:DV + 1], PT[0:rows, b % 2, (j % 4) * P:(j % 4 + 1) * P], V[0:rows, j, h, :],
                                       start=j == 0, stop=j == z.kt - 1)
                    if b == z.ng - 1:
                        mm.then_inc(pv_r, 1)

                def body(h, p, more):
                    if more:
                        scores(h + 1, 1 - p)
                    pe.wait_ge(exp_r, (h + 1) * z.nb + z.sc0)
                    transposes(h, p, 0)
                    for b in range(1, z.ng):
                        transposes(h, p, b)
                        product(h, b - 1)
                    product(h, z.ng - 1)

                scores(0, 0)
                heads(pe, body)
                pe.wait_ge(o_r, z.q0 + HB)
                for k in range(4):
                    mm = pe.transpose(tps[0][:, k * P:(k + 1) * P], ob[:, k * P:(k + 1) * P], ident[:, :])
                mm.then_inc(obt, 1)

        @block.scalar
        def _(act):
            for m, z in enumerate(sizes):
                act.wait_ge(cqt, m + 1)
                act.copy(cqT[:, :, :], tps[0][:, 0:384].rearrange("p (k t) -> p k t", k=3)).then_inc(cqt_out, 1)
                act.wait_ge(qps, m + 1)
                for b in range(2):
                    a = act.mul(qb[:, 4 * b:4 * b + 4, :], tps[b][:, 0:384].rearrange("p (h c) -> p h c", h=4), scale)
                a.then_inc(qb_out, 1)
                act.wait_ge(qbt, m + 1)
                for b in range(2):
                    a = act.copy(qT[0:HQ, 4 * b:4 * b + 4, :], tps[b][0:HQ, :].rearrange("p (h t) -> p h t", h=4))
                a.then_inc(qT_out, 1)

                def exps(h, p):
                    act.wait_ge(mx_r, h + (z.q0 + 1))
                    for b in range(z.nb):
                        lo, hi = z.bank(b)
                        own = z.own if b == z.nb - 1 else 0
                        a = act.activation(Pr[:, p, lo:hi - own], flat[:, lo:hi - own], ACT.Exp, bias=mx[:, p, 7:8])
                        if own:
                            a = act.activation(Pr[CH:P, p, hi - own:hi], flat[CH:P, hi - own:hi], ACT.Exp, bias=mx[CH:P, p, 7:8])
                        a.then_inc(exp_r, 1)

                def body(h, p, more):
                    for b in range(0, z.ng, 2):
                        act.wait_ge(tr_r, h * z.ng + (z.tr0 + b + 1))
                        w = min(4, z.kt - 4 * b) * P
                        act.copy(PT[:, 0, 0:w], tps[0][:, 0:w]).then_inc(pt_a, 1)
                    if more:
                        exps(h + 1, 1 - p)

                act.wait_ge(zero, m + 1)
                exps(0, 0)
                heads(act, body)
                act.wait_ge(obt, m + 1)
                if m >= 2:
                    act.wait_ge(stored[m % 2], m // 2 * 16)
                act.copy(obT[:, m % 2, :], tps[0][:, :]).then_inc(obt_out, 1)

        @block.vector
        def _(dve):
            dve.memset(mx[:, :, 0:1], -3.0e38).then_inc(init, 1)
            dve.wait_ge(init, 1)
            for m, z in enumerate(sizes):
                dve.wait_ge(qb_out, m + 1)
                dve.wait_ge(in_[m % 2], (m // 2 + 1) * 48)
                ck = over_heads(cs[:, m % 2, 0:32], HB)
                dve.tensor_tensor(rt[:, 0, :, :], qb[:, :, NOPE:HQ], ck, ALU.mult)
                dve.tensor_tensor(rt[:, 1, :, 0:16], qb[:, :, NOPE + 16:HQ], over_heads(cs[:, m % 2, 32:48], HB), ALU.mult)
                dve.tensor_tensor(rt[:, 1, :, 16:32], qb[:, :, NOPE:NOPE + 16], over_heads(cs[:, m % 2, 48:64], HB), ALU.mult).then_inc(init, 1)
                dve.wait_ge(init, m + 2)
                dve.tensor_tensor(qb[:, :, NOPE:HQ], rt[:, 0, :, :], rt[:, 1, :, :], ALU.add).then_inc(roped, 1)

                def maxima(h, p):
                    for b in range(z.nb):
                        lo, hi = z.bank(b)
                        own = z.own if b == z.nb - 1 else 0
                        dve.wait_ge(sc_r, h * z.nb + (z.sc0 + b + 1))
                        u = dve.tensor_reduce(mx[:, p, 1 + b:2 + b], flat[:, lo:hi - own], AX, ALU.max)
                        if own:
                            u = dve.tensor_reduce(mx[CH:P, p, 0:1], flat[CH:P, hi - own:hi], AX, ALU.max)
                    u.then_inc(parts, 1)
                    dve.wait_ge(parts, h + (z.q0 + 1))
                    dve.tensor_reduce(mx[:, p, 7:8], mx[:, p, 0:1 + z.nb], AX, ALU.max, negate=True).then_inc(mx_r, 1)

                def body(h, p, more):
                    if more:
                        maxima(h + 1, 1 - p)
                    for b in range(1, z.ng, 2):
                        dve.wait_ge(tr_r, h * z.ng + (z.tr0 + b + 1))
                        w = min(4, z.kt - 4 * b) * P
                        dve.tensor_copy(PT[:, 1, 0:w], tps[1][:, 0:w]).then_inc(pt_v, 1)
                    dve.wait_ge(pv_r, h + (z.q0 + 1))
                    dve.reciprocal(rc[:, :], ops[:, DV:DV + 1]).then_inc(inv, 1)
                    dve.wait_ge(inv, h + (z.q0 + 1))
                    dve.scalar_tensor_tensor(out=ob[:, :].rearrange("p (h e) -> p h e", h=HB)[:, h, :], in0=ops[:, 0:DV], scalar=rc[:, 0:1],
                                             in1=zb[:, m % 2, :].rearrange("p (h e) -> p h e", h=HB)[:, h, :],
                                             op0=ALU.mult, op1=ALU.mult).then_inc(o_r, 1)

                if m:
                    dve.wait_ge(obt, m)
                maxima(0, 0)
                heads(dve, body)


def gate_rows(nc, keep, layer, sb, sem, banks, gB, tag):
    dg = sb(f"{tag}_dg", [P, 2 * KD, P])
    diag, rows, got = sem(f"{tag}_diag"), sem(f"{tag}_rows"), sem(f"{tag}_got")

    def dve_part(dve):
        for n in range(2 * KD):
            c, k = n // KD, n % KD
            u = dve.tensor_scalar(dg[:, n, :], keep["ident"][:, :], keep["gg"][:, layer, c, k:k + 1], None, ALU.mult)
        u.then_inc(diag, 1)
        dve.wait_ge(rows, 1)
        for c in range(2):
            for j in range(2):
                u = dve.tensor_copy(gB[:, c, j * 512:(j + 1) * 512], banks[2 * c + j][:, :])
        u.then_inc(got, 1)
        dve.wait_ge(got, 1)

    def pe_part(pe):
        pe.wait_ge(diag, 1)
        for c in range(2):
            for j in range(2):
                mm = pe.matmul(banks[2 * c + j][:, :], keep["ones"][:, :], dg[:, c * KD + 4 * j:c * KD + 4 * j + 4, :],
                               start=True, stop=True)
        mm.then_inc(rows, 1)
        pe.wait_ge(got, 1)

    return dve_part, pe_part


def close_even(nc, io, keep, scr):
    with ExitStack() as ctx:
        sb, ps, sem = stage(nc, ctx)
        w = sb("c_w", [P, KD, D])
        oc = sb("c_oc", [P, 2, KD, P])
        xt = sb("c_xt", [P, 2, D])
        y = sb("c_y", [P, 2, D])
        junk = sb("c_junk", [P, D])
        gB = sb("c_gB", [P, 2, D])
        ms, rs = sb("c_ms", [P, 1]), sb("c_rs", [P, 1])
        bank = [ps(f"c_b{i}") for i in range(4)]
        w_in, mm_r, y_r, ms_r, rs_r, yn, out = (sem("c_" + n) for n in ("w_in", "mm", "y", "ms", "rs", "yn", "out"))
        in_, stored = [sem("c_in0"), sem("c_in1")], [sem("c_st0"), sem("c_st1")]
        dve_rows, pe_rows = gate_rows(nc, keep, 0, sb, sem, bank, gB, "c")
        block = ctx.enter_context(nc.Block())

        @block.sync
        def _(sp):
            def load(t, p):
                sp.dma_start(oc[:, p, 0:4, :], scr["oa"][t].rearrange("p (k t) -> p k t", k=4)).then_inc(in_[p], 16)
                sp.dma_start(oc[:, p, 4:8, :], scr["ob"][t].rearrange("p (k t) -> p k t", k=4)).then_inc(in_[p], 16)
                if last(t):
                    sp.dma_start(xt[0:DEC, p, :], io["x_sample"][0]).then_inc(in_[p], 16)
                else:
                    sp.dma_start(xt[:, p, :], io["x_prompt"][0].rearrange("(t p) d -> t p d", p=P)[t]).then_inc(in_[p], 16)

            load(0, 0)
            sp.dma_start(w[:, :, :], io["w_out_e"][0].rearrange("(k p) n -> p k n", p=P)).then_inc(w_in, 16)

            def step(t, p, i):
                if not last(t):
                    sp.wait_ge(out, t)
                    load(t + 1, 1 - p)
                sp.wait_ge(out, t + 1)
                sp.dma_start(scr["x1"][t], y[:, p, :]).then_inc(stored[p], 16)

            tiles_of(sp, step)
            sp.wait_ge(stored[0], (TILES + 1) // 2 * 16)
            sp.wait_ge(stored[1], TILES // 2 * 16)

        @block.gpsimd
        def _(pool):
            def step(t, p, i):
                pool.wait_ge(ms_r, t + 1)
                pool.tensor_tensor(rs[:, :], ms[:, :], keep["mhalf"][:, 0:1], ALU.pow).then_inc(rs_r, 1)
            tiles_of(pool, step)

        @block.scalar
        def _(act):
            def step(t, p, i):
                act.wait_ge(mm_r, t + 1)
                act.wait_ge(stored[p], i * 16)
                act.copy(y[:, p, 0:512], bank[2 * p][:, :])
                act.copy(y[:, p, 512:D], bank[2 * p + 1][:, :]).then_inc(y_r, 1)
            tiles_of(act, step)

        @block.tensor
        def _(pe):
            pe_rows(pe)
            pe.wait_ge(w_in, 16)

            def step(t, p, i):
                pe.wait_ge(in_[p], (i + 1) * 48)
                if p or isinstance(t, int):
                    pe.wait_ge(y_r, t - 1)
                else:
                    pe.wait_ge(y_r, t)
                for j in range(2):
                    for k in range(KD):
                        mm = pe.matmul(bank[2 * p + j][:, :], oc[:, p, k, :], w[:, k, j * 512:(j + 1) * 512], start=k == 0, stop=k == KD - 1)
                mm.then_inc(mm_r, 1)
            tiles_of(pe, step)

        @block.vector
        def _(dve):
            dve_rows(dve)

            def step(t, p, i):
                dve.wait_ge(y_r, t + 1)
                dve.tensor_tensor_reduce(junk[:, :], y[:, p, :], y[:, p, :], 1.0 / D, EPS, ALU.mult, ALU.add, ms[:, :]).then_inc(ms_r, 1)
                dve.wait_ge(rs_r, t + 1)
                dve.wait_ge(in_[p], (i + 1) * 48)
                dve.scalar_tensor_tensor(out=y[:, p, :], in0=y[:, p, :], scalar=rs[:, 0:1], in1=gB[:, cond(t), :],
                                         op0=ALU.mult, op1=ALU.mult).then_inc(yn, 1)
                dve.wait_ge(yn, t + 1)
                dve.tensor_tensor(y[:, p, :], y[:, p, :], xt[:, p, :], ALU.add).then_inc(out, 1)
            tiles_of(dve, step)


def in_odd(nc, io, keep, scr):
    with ExitStack() as ctx:
        sb, ps, sem = stage(nc, ctx)
        w = sb("e_w", [P, KD, IN_O])
        xt = sb("e_xt", [P, 2, D])
        xn = sb("e_xn", [P, D])
        hT = sb("e_hT", [P, 2, KD, P])
        r = sb("e_r", [P, IN_O])
        ms, rs = sb("e_ms", [P, 1]), sb("e_rs", [P, 1])
        xps = [ps("e_x0"), ps("e_x1")]
        bank = [ps(f"e_p{i}") for i in range(4)]
        S = norm_sems(sem, "e")
        w_in, proj, a_out, v_out = (sem("e_" + n) for n in ("w_in", "proj", "a_out", "v_out"))
        st = [sem(f"e_st{j}") for j in range(4)]
        dve_norm, pool_norm, pe_tr, act_hT, dve_hT = norm_transpose(1, keep, xt, xn, ms, rs, hT, xps, S)
        block = ctx.enter_context(nc.Block())

        @block.sync
        def _(sp):
            def load(t, p):
                sp.dma_start(xt[:, p, :], scr["x1"][t]).then_inc(S["x_in"][p], 16)

            load(0, 0)
            for k in range(KD):
                sp.dma_start(w[:, k, :], io["w_in_o"][0, k * P:(k + 1) * P, :]).then_inc(w_in, 16)

            def step(t, p, i):
                if not last(t):
                    sp.wait_ge(S["xn"], t)
                    load(t + 1, 1 - p)
                for j in range(4):
                    if j in (0, 3):
                        sp.wait_ge(a_out, t * 4 + (2 if j == 0 else 4))
                    else:
                        sp.wait_ge(v_out, t * 4 + 2 * j)
                    sp.dma_start(scr["odd"][t, :, j * D:(j + 1) * D], r[:, j * D:(j + 1) * D]).then_inc(st[j], 16)

            tiles_of(sp, step)
            for j in range(4):
                sp.wait_ge(st[j], TILES * 16)

        @block.gpsimd
        def _(pool):
            def step(t, p, i):
                if not last(t):
                    pool_norm(pool, t + 1)
            pool_norm(pool, 0)
            tiles_of(pool, step)

        @block.scalar
        def _(act):
            def step(t, p, i):
                for n in (0, 1, 6, 7):
                    if n == 6 and not last(t):
                        act_hT(act, t + 1, 1 - p)
                    act.wait_ge(st[n // 2], t * 16)
                    act.wait_ge(proj, t * 8 + n + 1)
                    act.activation(r[:, n * 512:(n + 1) * 512], bank[n % 4][:, :], ACT.Silu).then_inc(a_out, 1)

            act_hT(act, 0, 0)
            tiles_of(act, step)

        @block.tensor
        def _(pe):
            def step(t, p, i):
                pe.wait_ge(S["hT_a"], t + 1)
                pe.wait_ge(S["hT_v"], t + 1)
                for n in range(8):
                    if n in (0, 1):
                        pe.wait_ge(v_out, t * 4)
                    elif n in (2, 3):
                        pe.wait_ge(a_out, t * 4)
                    elif n in (4, 5):
                        pe.wait_ge(a_out, t * 4 + (n - 3))
                    else:
                        pe.wait_ge(v_out, t * 4 + (n - 5))
                    for c in range(4):
                        for k in range(KD):
                            if n < 4:
                                a = n * 512 + c * P
                                mm = pe.matmul(bank[n % 4][:, c * P:(c + 1) * P], w[:, k, a:a + P], hT[:, p, k, :], start=k == 0, stop=k == KD - 1)
                            elif c == 0:
                                mm = pe.matmul(bank[n % 4][:, :], hT[:, p, k, :], w[:, k, n * 512:(n + 1) * 512], start=k == 0, stop=k == KD - 1)
                    mm.then_inc(proj, 1)
                    if n == 3 and not last(t):
                        pe_tr(pe, t + 1)

            pe_tr(pe, 0)
            pe.wait_ge(w_in, 16 * KD)
            tiles_of(pe, step)

        @block.vector
        def _(dve):
            def step(t, p, i):
                if not last(t):
                    dve_norm(dve, t + 1, 1 - p, i + p)
                for n in (2, 3, 4, 5):
                    if n == 4 and not last(t):
                        dve_hT(dve, t + 1, 1 - p)
                    dve.wait_ge(st[n // 2], t * 16)
                    dve.wait_ge(proj, t * 8 + n + 1)
                    dve.tensor_copy(r[:, n * 512:(n + 1) * 512], bank[n % 4][:, :]).then_inc(v_out, 1)

            dve_norm(dve, 0, 0, 0)
            dve_hT(dve, 0, 0)
            tiles_of(dve, step)


def hgrn(nc, io, keep, scr):
    H = HC
    with ExitStack() as ctx:
        sb, ps, sem = stage(nc, ctx)
        w = sb("h_w", [P, KD, D])
        r = sb("h_r", [P, 2, 4, H, P])
        gB = sb("h_gB", [P, 2, D])
        gnc = sb("h_gnc", [P, P])
        reset = sb("h_reset", [P, H, P])
        kT, G = sb("h_kT", [P, H, P]), sb("h_G", [P, H, P])
        fg = sb("h_fg", [P, H, P])
        EG = sb("h_EG", [P, H, P])
        DL, EL = sb("h_DL", [P, 2, 512]), sb("h_EL", [P, 2, 2, 512])
        KLv, QLv = sb("h_KL", [P, 2, H, P]), sb("h_QL", [P, 2, 512])
        A = sb("h_A", [P, H, P])
        kdT, kd, qe = sb("h_kdT", [P, H, P]), sb("h_kd", [P, H, P]), sb("h_qe", [P, H, P])
        St = sb("h_S", [P, H, P])
        o = sb("h_o", [P, H, P])
        os8, or8 = sb("h_os8", [P, 8]), sb("h_or8", [P, 8])
        oT = sb("h_oT", [P, H, P])
        xt, y = sb("h_xt", [P, D]), sb("h_y", [P, D])
        ms, rs, hold = sb("h_ms", [P, 1]), sb("h_rs", [P, 1]), sb("h_hold", [P, 6])
        bank = [ps(f"h_b{i}") for i in range(8)]
        names = ("sg1 sg2 fg lf G EG fin tail kd kdt kd_out dq dg osum A kS qe o_ps o_out on0 on os or og ogt oT_out mm y ms rs yn out scanned").split()
        R = {n: sem("h_" + n) for n in names}
        dls, els, kqs, scs, Ac = (sem("h_" + n) for n in ("dl", "el", "kq", "sc", "Ac"))
        Ss, kSs, qSs = sem("h_S"), sem("h_kSs"), sem("h_qSs")
        in_, x_in, stored = [sem("h_in0"), sem("h_in1")], sem("h_x_in"), sem("h_stored")
        const_in, state_out, state_in, init = sem("h_const"), sem("h_so"), sem("h_si"), sem("h_init")
        link, pl = sem("h_link"), sem("h_pl")
        dve_rows, pe_rows = gate_rows(nc, keep, 1, sb, sem, bank, gB, "h")
        block = ctx.enter_context(nc.Block())
        flat = lambda b: b.rearrange("p h t -> p (h t)")
        heads4 = lambda b: b[:, :].rearrange("p (h t) -> p h t", h=4)
        state = lambda ap: ap.rearrange("h d e -> d h e")

        def halves(ap, b):
            return ap.rearrange("p h (n a b) -> p (h n) a b", a=2, b=b)

        @block.sync
        def _(sp):
            sp.dma_start(gnc[:, :], io["g_norm_c"][0:1, :].to_broadcast([P, P])).then_inc(const_in, 16)

            def load(t, p):
                sp.dma_start(r[:, p, :, :, :], scr["odd"][t].rearrange("p (j h t) -> p j h t", j=4, h=H)).then_inc(in_[p], 16)

            load(0, 0)
            sp.dma_start(w[:, :, :], io["w_out_o"][0].rearrange("(k p) n -> p k n", p=P)).then_inc(const_in, 16)

            def step(t, p, i):
                if not last(t):
                    sp.wait_ge(R["og"], t)
                    load(t + 1, 1 - p)
                sp.wait_ge(R["out"], t)
                sp.dma_start(xt[:, :], scr["x1"][t]).then_inc(x_in, 16)
                if isinstance(t, int) and t == NT - 1:
                    sp.wait_ge(Ss, 2 * NT)
                    sp.dma_start(state(io["p_hgrn"][0, 0]), St[:, :, :]).then_inc(state_out, 16)
                    sp.wait_ge(state_out, 16)
                    sp.wait_ge(R["o_ps"], NT)
                    sp.dma_start(St[:, :, :], state(io["state_hgrn"][0, 0])).then_inc(state_in, 16)
                if last(t):
                    sp.wait_ge(Ss, 2 * NT + 1)
                    sp.dma_start(state(io["s_hgrn"][0, 0]), St[:, :, :]).then_inc(state_out, 16)
                sp.wait_ge(R["out"], t + 1)
                if last(t):
                    sp.dma_start(io["y_sample"][0], y[0:DEC, :]).then_inc(stored, 16)
                else:
                    sp.dma_start(io["y_prompt"][0].rearrange("(t p) d -> t p d", p=P)[t], y[:, :]).then_inc(stored, 16)

            tiles_of(sp, step)
            sp.wait_ge(state_out, 32)
            sp.wait_ge(stored, TILES * 16)

        @block.gpsimd
        def _(pool):
            def step(t, p, i):
                pool.wait_ge(in_[p], (i + 1) * 16)
                pool.tensor_tensor(r[:, p, 3, :, :], r[:, p, 3, :, :], over_heads(gnc[:, :], H), ALU.mult).then_inc(R["on0"], 1)
                pool.wait_ge(R["EG"], t + 1)
                pool.wait_ge(R["o_ps"], t)
                pool.tensor_tensor(qe[:, :, :], r[:, p, 0, :, :], EG[:, :, :], ALU.mult).then_inc(R["qe"], 1)
                pool.wait_ge(R["os"], t + 1)
                pool.tensor_tensor(or8[:, :], os8[:, :], keep["mhalf"][:, :], ALU.pow).then_inc(R["or"], 1)
                pool.wait_ge(R["ms"], t + 1)
                pool.tensor_tensor(rs[:, :], ms[:, :], keep["mhalf"][:, 0:1], ALU.pow).then_inc(R["rs"], 1)

            pool.wait_ge(const_in, 32)
            tiles_of(pool, step)

        @block.scalar
        def _(act):
            def step(t, p, i):
                act.wait_ge(in_[p], (i + 1) * 16)
                act.wait_ge(R["kd"], t)
                act.activation(flat(fg[:, :, :]), flat(r[:, p, 1, :, :]), ACT.Exp, scale=-1.0).then_inc(R["sg1"], 1)
                act.wait_ge(R["fg"], t + 1)
                act.activation(flat(fg[:, :, :]), flat(fg[:, :, :]), ACT.Ln).then_inc(R["lf"], 1)
                act.wait_ge(R["G"], t + 1)
                act.wait_ge(Ss, t * 2) if not last(t) else act.wait_ge(Ss, 2 * NT)
                act.activation(flat(EG[:, :, :]), flat(G[:, :, :]), ACT.Exp).then_inc(R["EG"], 1)
                act.wait_ge(R["tail"], t + 1)
                act.activation(flat(kdT[:, :, :]), flat(kdT[:, :, :]), ACT.Exp).then_inc(R["fin"], 1)
                for n in range(6):
                    act.wait_ge(dls, t * 6 + n + 1)
                    act.activation(EL[:, n % 2, :, :], DL[:, :, :], ACT.Exp).then_inc(els, 1)
                    if n == 0:
                        act.wait_ge(R["kdt"], t + 1)
                        act.copy(flat(kd[:, 0:4, :]), bank[4][:, :])
                        act.copy(flat(kd[:, 4:8, :]), bank[5][:, :]).then_inc(R["kd_out"], 1)
                act.wait_ge(R["o_ps"], t + 1)
                act.copy(flat(o[:, 0:4, :]), bank[6][:, :])
                act.copy(flat(o[:, 4:8, :]), bank[7][:, :]).then_inc(R["o_out"], 1)
                act.wait_ge(R["ogt"], t + 1)
                act.copy(flat(oT[:, 0:4, :]), bank[4][:, :])
                act.copy(flat(oT[:, 4:8, :]), bank[5][:, :]).then_inc(R["oT_out"], 1)
                act.wait_ge(R["mm"], t + 1)
                act.wait_ge(stored, t * 16)
                act.copy(y[:, 0:512], bank[2][:, :])
                act.copy(y[:, 512:D], bank[3][:, :]).then_inc(R["y"], 1)

            tiles_of(act, step)

        @block.tensor
        def _(pe):
            pe_rows(pe)
            pe.wait_ge(const_in, 32)
            pe.wait_ge(init, 1)
            ident = keep["ident"]

            def step(t, p, i):
                pe.wait_ge(in_[p], (i + 1) * 16)
                pe.wait_ge(R["y"], t)
                pe.wait_ge(R["sg2"], t + 1)
                for h in range(H):
                    mm = pe.matmul(bank[2 + h // 4][:, h % 4 * P:(h % 4 + 1) * P], kT[:, h, :], r[:, p, 0, h, :], start=True, stop=True)
                mm.then_inc(R["dq"], 1)
                pe.wait_ge(R["kd"], t + 1)
                for h in range(H):
                    mm = pe.transpose(bank[4 + h // 4][:, h % 4 * P:(h % 4 + 1) * P], kdT[:, h, :], ident[:, :])
                mm.then_inc(R["kdt"], 1)
                for n in range(6):
                    pe.wait_ge(kqs, t * 6 + n + 1)
                    if n >= 2:
                        pe.wait_ge(Ac, t * 6 + n - 1)
                    for h in range(H):
                        mm = pe.matmul(bank[n % 2][:, h * CH:(h + 1) * CH], KLv[:, n % 2, h, :], QLv[:, n % 2, h * CH:(h + 1) * CH],
                                       start=True, stop=True)
                    mm.then_inc(scs, 1)
                if last(t):
                    pe.wait_ge(state_in, 16)
                pe.wait_ge(R["kd_out"], t + 1)
                pe.wait_ge(R["qe"], t + 1)
                pe.wait_ge(R["dg"], t + 1)
                for c in range(2):
                    lo, hi = c * CH, (c + 1) * CH
                    if c:
                        pe.wait_ge(Ss, t * 2 + 1)
                    elif not last(t):
                        pe.wait_ge(Ss, t * 2)
                    for h in range(H):
                        mm = pe.matmul(bank[6 + h // 4][lo:hi, h % 4 * P:(h % 4 + 1) * P], qe[:, h, lo:hi], St[:, h, :],
                                       start=h % 4 == 0, stop=False, skip_group_check=True)
                    mm.then_inc(qSs, 1)
                    if not (last(t) and c):
                        for h in range(H):
                            mm = pe.matmul(bank[2 + h // 4][:, h % 4 * P:(h % 4 + 1) * P], kd[lo:hi, h, :], r[lo:hi, p, 2, h, :],
                                           start=True, stop=True)
                        mm.then_inc(kSs, 1)
                pe.wait_ge(Ac, t * 6 + 6)
                for h in range(H):
                    mm = pe.matmul(bank[6 + h // 4][:, h % 4 * P:(h % 4 + 1) * P], A[:, h, :], r[:, p, 2, h, :],
                                   start=False, stop=h % 4 == 3, skip_group_check=True)
                mm.then_inc(R["o_ps"], 1)
                pe.wait_ge(R["og"], t + 1)
                for h in range(H):
                    mm = pe.transpose(bank[4 + h // 4][:, h % 4 * P:(h % 4 + 1) * P], o[:, h, :], ident[:, :])
                mm.then_inc(R["ogt"], 1)
                pe.wait_ge(R["oT_out"], t + 1)
                if not last(t):
                    pe.wait_ge(Ss, t * 2 + 2)
                for j in range(2):
                    for k in range(KD):
                        mm = pe.matmul(bank[2 + j][:, :], oT[:, k, :], w[:, k, j * 512:(j + 1) * 512], start=k == 0, stop=k == KD - 1)
                mm.then_inc(R["mm"], 1)

            tiles_of(pe, step)

        @block.vector
        def _(dve):
            dve_rows(dve)
            dve.memset(reset[:, :, :], 1.0)
            dve.memset(KLv[:, :, :, :], 0.0)
            dve.memset(St[:, :, :], 0.0).then_inc(init, 1)
            dve.wait_ge(init, 1)
            dve.memset(reset[:, :, :].rearrange("p h (c t) -> p (h c) t", t=CH)[:, :, 0:1], 0.0).then_inc(init, 1)
            dve.wait_ge(init, 2)

            def step(t, p, i):
                ln = Links(dve, link, 2, t)
                dve.wait_ge(R["sg1"], t + 1)
                ln.link(dve.tensor_scalar(flat(fg[:, :, :]), flat(fg[:, :, :]), 1.0, None, ALU.add))
                ln.link(dve.reciprocal(flat(fg[:, :, :]), flat(fg[:, :, :])))
                for h in range(H):
                    u = dve.tensor_scalar(fg[:, h, :], fg[:, h, :], keep["lb"][:, 1, h:h + 1], keep["lb"][:, 0, h:h + 1], ALU.mult, ALU.add)
                u.then_inc(R["osum"], 1)
                dve.wait_ge(R["osum"], t + 1)
                dve.tensor_scalar(flat(kT[:, :, :]), flat(fg[:, :, :]), -1.0, 1.0, ALU.mult, ALU.add).then_inc(R["sg2"], 1)
                dve.wait_ge(R["sg2"], t + 1)
                dve.tensor_copy(os8[:, 0:1], kT[:, 0, 0:1]).then_inc(R["fg"], 1)
                dve.wait_ge(R["lf"], t + 1)
                dve.tensor_tensor_scan(flat(G[:, :, :]), flat(reset[:, :, :]), flat(fg[:, :, :]), 0.0, ALU.mult, ALU.add).then_inc(R["G"], 1)
                dve.wait_ge(R["G"], t + 1)
                Gc = G[:, :, :].rearrange("p h (c t) -> p (h c) t", t=CH)
                dve.tensor_tensor(kdT[:, :, :].rearrange("p h (c t) -> p (h c) t", t=CH), Gc[:, :, CH - 1:CH].to_broadcast([P, 2 * H, CH]), Gc,
                                  ALU.subtract).then_inc(R["tail"], 1)
                dve.wait_ge(R["dq"], t + 1)
                for j in range(2):
                    u = dve.tensor_tensor(A[:, 4 * j:4 * j + 4, :], heads4(bank[2 + j]), over_heads(keep["ident"][:, :], 4), ALU.mult)
                u.then_inc(R["dg"], 1)
                dve.wait_ge(R["fin"], t + 1)
                dve.tensor_tensor(kdT[:, :, :], kT[:, :, :], kdT[:, :, :], ALU.mult).then_inc(R["kd"], 1)

                def differences(n):
                    b = LEVELS[n]
                    g = halves(G[:, :, :], b)
                    mid = g[:, :, 0, b - 1:b].to_broadcast([P, 512 // b, b])
                    dve.tensor_tensor(DL[:, 0, :].rearrange("p (n b) -> p n b", b=b), mid, g[:, :, 0, :], ALU.subtract)
                    dve.tensor_tensor(DL[:, 1, :].rearrange("p (n b) -> p n b", b=b), g[:, :, 1, :], mid, ALU.subtract).then_inc(dls, 1)

                def operands(n):
                    b = LEVELS[n]
                    dve.wait_ge(els, t * 6 + n + 1)
                    dve.tensor_tensor(halves(KLv[:, n % 2, :, :], b)[:, :, 0, :], halves(kT[:, :, :], b)[:, :, 0, :],
                                      EL[:, n % 2, 0, :].rearrange("p (n b) -> p n b", b=b), ALU.mult)
                    dve.tensor_tensor(QLv[:, n % 2, :].rearrange("p (n b) -> p n b", b=b), halves(r[:, p, 0, :, :], b)[:, :, 1, :],
                                      EL[:, n % 2, 1, :].rearrange("p (n b) -> p n b", b=b), ALU.mult).then_inc(kqs, 1)

                def take(n):
                    b = LEVELS[n]
                    dve.wait_ge(scs, t * 6 + n + 1)
                    dst = A[:, :, :].rearrange("p h (n a b) -> p h n a b", a=2, b=b)[:, :, :, 1, :]
                    src = bank[n % 2][:, :].rearrange("p (h n b) -> p h n b", h=H, b=b)
                    mask = keep["levels"][:, n, :].bitcast(I32).rearrange("p (n a b) -> p n a b", a=2, b=b)[:, :, 1, :]
                    if n:
                        dve.wait_ge(Ac, t * 6 + n)
                    dve.memset(hold[:, n:n + 1], 0.0)
                    dve.copy_predicated(dst, mask.unsqueeze(1).to_broadcast([P, H, CH // b, b]), src).then_inc(Ac, 1)

                dve.wait_ge(R["dg"], t + 1)
                differences(0)
                for n in range(6):
                    operands(n)
                    if n < 5:
                        differences(n + 1)
                    if n:
                        take(n - 1)
                for c in range(2):
                    if not (last(t) and c):
                        dve.wait_ge(qSs, t * 2 + c + 1)
                        dve.wait_ge(kSs, t * 2 + c + 1)
                        for h in range(H):
                            u = dve.scalar_tensor_tensor(out=St[:, h, :], in0=St[:, h, :], scalar=EG[:, h, (c + 1) * CH - 1:(c + 1) * CH],
                                                         in1=bank[2 + h // 4][:, h % 4 * P:(h % 4 + 1) * P], op0=ALU.mult, op1=ALU.add)
                        u.then_inc(Ss, 1)
                    if c == 0:
                        take(5)
                dve.wait_ge(R["o_out"], t + 1)
                dve.tensor_tensor(kdT[:, :, :], o[:, :, :], o[:, :, :], ALU.mult).then_inc(R["on"], 1)
                dve.wait_ge(R["on"], t + 1)
                dve.tensor_reduce(os8[:, :], kdT[:, :, :], AX, ALU.add).then_inc(pl, 1)
                dve.wait_ge(pl, t + 1)
                dve.tensor_scalar(os8[:, :], os8[:, :], 1.0 / P, EPS, ALU.mult, ALU.add).then_inc(R["os"], 1)
                dve.wait_ge(R["or"], t + 1)
                dve.tensor_tensor(o[:, :, :], o[:, :, :], bc(or8[:, :], P), ALU.mult).then_inc(R["scanned"], 1)
                dve.wait_ge(R["scanned"], t + 1)
                dve.wait_ge(R["on0"], t + 1)
                dve.tensor_tensor(o[:, :, :], o[:, :, :], r[:, p, 3, :, :], ALU.mult).then_inc(R["og"], 1)
                dve.wait_ge(R["y"], t + 1)
                dve.tensor_tensor_reduce(flat(kdT[:, :, :]), y[:, :], y[:, :], 1.0 / D, EPS, ALU.mult, ALU.add, ms[:, :]).then_inc(R["ms"], 1)
                dve.wait_ge(R["rs"], t + 1)
                dve.wait_ge(x_in, (t + 1) * 16)
                dve.scalar_tensor_tensor(out=y[:, :], in0=y[:, :], scalar=rs[:, 0:1], in1=gB[:, cond(t), :],
                                         op0=ALU.mult, op1=ALU.mult).then_inc(R["yn"], 1)
                dve.wait_ge(R["yn"], t + 1)
                dve.tensor_tensor(y[:, :], y[:, :], xt[:, :], ALU.add).then_inc(R["out"], 1)
                ln.end()

            tiles_of(dve, step)


def program(nc, io):
    scr = {n: nc.dram_tensor("scr_" + n, list(s), F32, kind="Internal").ap() for n, s in (
        ("qkv", (TILES, P, NCT, P)), ("z", (TILES, P, D)), ("ba", (TILES, P, 8)), ("cq", (TILES, P, QL)),
        ("oa", (TILES, P, 512)), ("ob", (TILES, P, 512)), ("x1", (TILES, P, D)), ("odd", (TILES, P, IN_O)))}
    with ExitStack() as ctx:
        keep = {n: ctx.enter_context(nc.sbuf_tensor("k_" + n, list(s), F32)) for n, s in (
            ("ident", (P, P)), ("cums", (P, P)), ("strict", (P, P)), ("blk", (P, P)), ("low1", (P, P)),
            ("levels", (P, 6, P)), ("ones", (P, P)), ("mhalf", (P, 8)), ("lb", (P, 2, KD)),
            ("mA", (P, 2, 2, KD)), ("mB", (P, 2, 2, KD)), ("gg", (P, 2, 2, KD)))}
        modulation(nc, io, keep)
        in_even(nc, io, keep, scr)
        delta(nc, io, keep, scr)
        with ExitStack() as kv:
            kT = kv.enter_context(nc.sbuf_tensor("kT", [P, HB, PAST + DEC], F32))
            V = kv.enter_context(nc.sbuf_tensor("V", [P, NT + 1, HB, DV + 1], F32))
            for sample in (False, True):
                keys(nc, io, keep, scr, kT, V, sample)
                attention(nc, io, keep, scr, kT, V, sample)
        close_even(nc, io, keep, scr)
        in_odd(nc, io, keep, scr)
        hgrn(nc, io, keep, scr)


INS = ("x_prompt x_sample c_prompt c_sample cache_ckv cache_kr state_delta state_conv state_hgrn w_ada b_ada g_pre g_post "
       "w_in_e conv_w a_log dt_bias g_norm_a g_q w_uq g_kv w_ukv w_out_e w_in_o lb_logits g_norm_c w_out_o").split()
OUTS = (("y_prompt", (1, SEQ, D)), ("y_sample", (1, DEC, D)), ("p_delta", (1, 1, HA, DK, DK)), ("p_conv", (1, 1, 3, QKV)),
        ("p_ckv", (1, 1, SEQ, KL)), ("p_kr", (1, 1, SEQ, ROPE)), ("p_hgrn", (1, 1, HC, P, P)),
        ("s_delta", (1, 1, HA, DK, DK)), ("s_conv", (1, 1, 3, QKV)), ("s_ckv", (1, 1, DEC, KL)), ("s_kr", (1, 1, DEC, ROPE)),
        ("s_hgrn", (1, 1, HC, P, P)))


def constants():
    import numpy as np
    a = np.arange(P)
    same = (a[:, None] // CH) == (a[None, :] // CH)
    levels = np.zeros((P, 6, P), np.float32)
    for n, b in enumerate(LEVELS):
        block = (a[:, None] // (2 * b)) == (a[None, :] // (2 * b))
        levels[:, n, :] = block & (a[:, None] // b % 2 == 0) & (a[None, :] // b % 2 == 1)
    half = ROPE // 2
    inv = (np.float32(10000.0) ** (-np.arange(half, dtype=np.float32) / np.float32(half))).astype(np.float32)
    ang = np.arange(TILES * P, dtype=np.float32)[:, None] * inv[None, :]
    cos, sin = np.cos(ang).astype(np.float32), np.sin(ang).astype(np.float32)
    rope = np.concatenate([cos, cos, -sin, sin], axis=1).reshape(TILES, P, 64)
    return {
        "c_ident": np.eye(P, dtype=np.float32),
        "c_cums": (same & (a[:, None] <= a[None, :])).astype(np.float32),
        "c_blk": same.astype(np.float32),
        "c_strict": (same & (a[:, None] > a[None, :])).astype(np.float32),
        "c_low1": np.ascontiguousarray(levels[:, 0, :].T),
        "c_levels": levels,
        "c_rope": rope,
    }


def kernel(**inputs):
    import numpy as np
    import concourse.bacc as bacc
    from concourse.bass_utils import run_bass_kernel_spmd

    nc = bacc.Bacc("TRN2", target_bir_lowering=False, num_devices=1)
    arrays = {n: np.ascontiguousarray(inputs[n]) for n in INS}
    arrays.update(constants())
    io = {n: nc.dram_tensor(n, a.shape, F32, kind="ExternalInput").ap() for n, a in arrays.items()}
    for n, s in OUTS:
        io[n] = nc.dram_tensor(n, s, F32, kind="ExternalOutput").ap()
    program(nc, io)
    r = run_bass_kernel_spmd(nc, [arrays], core_ids=[0])
    return tuple(r.results[0][n] for n, _ in OUTS)
```

```python
from contextlib import ExitStack

import concourse.bass as bass
from concourse import mybir

F32 = mybir.dt.float32
I32 = mybir.dt.int32
ALU = mybir.AluOpType
ACT = mybir.ActivationFunctionType
AX = mybir.AxisListType.X

P = 128
D = 1024
KD = D // P
SEQ = 2048
NT = SEQ // P
TILES = NT + 1
SAMPLE = NT
DEC = 64
CH = 64
PAST = 2048
EPS = 1e-6
HA, DK = 4, 128
QKV = 3 * HA * DK
NCT = QKV // P
HB, NOPE, ROPE, DV = 8, 64, 32, 64
HQ = NOPE + ROPE
QL, KL = 384, 256
IN_E = 3240
HC = 8
IN_O = 4096
LEVELS = (1, 2, 4, 8, 16, 32)
TOK = QKV
EVEN_GROUPS = ((1536, 2048), (2048, 2440), (2440, 2728), (2728, 3240))


class Links:

    def __init__(self, eng, sem, per, tile):
        self.eng, self.sem, self.per, self.k = eng, sem, per, 0
        self.base = tile * per

    def did(self, ins):
        ins.then_inc(self.sem, 1)
        self.k += 1
        return self.k

    def need(self, k):
        self.eng.wait_ge(self.sem, self.base + k)

    def link(self, ins):
        self.need(self.did(ins))

    def end(self):
        assert self.k == self.per, self.k


def stage(nc, ctx):
    def sb(name, shape, dt=F32):
        return ctx.enter_context(nc.sbuf_tensor(name, shape, dt))

    def ps(name, shape=(P, 512)):
        return ctx.enter_context(nc.psum_tensor(name, list(shape), F32))

    sems = []

    def sem(name):
        sems.append(nc.alloc_semaphore(name))
        return sems[-1]

    def clear():
        nc.clear_and_free_semaphores(sems)
        nc.all_engine_barrier()

    ctx.callback(clear)
    return sb, ps, sem


def tiles_of(eng, body):
    with eng.Fori(0, NT // 2 - 1) as i:
        body(i * 2, 0, i)
        body(i * 2 + 1, 1, i)
    body(NT - 2, 0, NT // 2 - 1)
    body(NT - 1, 1, NT // 2 - 1)
    body(SAMPLE, 0, NT // 2)


def after_first(eng, body):
    body(0, 0, 0, first=True)
    body(1, 1, 0)
    with eng.Fori(1, NT // 2 - 1) as i:
        body(i * 2, 0, i)
        body(i * 2 + 1, 1, i)
    body(NT - 2, 0, NT // 2 - 1)
    body(NT - 1, 1, NT // 2 - 1)
    body(SAMPLE, 0, NT // 2)


def last(t):
    return isinstance(t, int) and t == SAMPLE


def cond(t):
    return 1 if last(t) else 0


def modulation(nc, io, keep):
    with ExitStack() as ctx:
        sb, ps, sem = stage(nc, ctx)
        cT = sb("cT", [P, 2, KD])
        scT = sb("scT", [P, KD, 2])
        wa = sb("wa", [P, 2, 3 * D])
        bT = sb("bT", [P, 2, 24])
        gpre = sb("gpre", [P, 2, KD])
        gpost = sb("gpost", [P, 2, KD])
        lb = sb("lbl", [P, 2, KD])
        lt = sb("lt", [P, 4, KD])
        md = sb("md", [P, 2, 24, 2])
        mps = ps("mps", [P, 2, 512])
        consts = sem("m_consts")
        weights = sem("m_weights")
        w_in = [sem("m_w0"), sem("m_w1")]
        silu = sem("m_silu")
        zeroed = sem("m_zeroed")
        used = sem("m_used")
        link = sem("m_link")
        lexp = sem("m_lexp")
        lmax = sem("m_lmax")
        block = ctx.enter_context(nc.Block())

        @block.sync
        def _(sp):
            for j, c in enumerate((io["c_prompt"], io["c_sample"])):
                sp.dma_start(cT[:, j, :], c.rearrange("a (k p) -> p (a k)", p=P), allow_slow_non_contiguous=True).then_inc(consts, 16)
            sp.dma_start(keep["ident"][:, :], io["c_ident"]).then_inc(consts, 16)
            sp.dma_start(keep["cums"][:, :], io["c_cums"]).then_inc(consts, 16)
            sp.dma_start(keep["blk"][:, :], io["c_blk"]).then_inc(consts, 16)
            sp.dma_start(keep["low1"][:, :], io["c_low1"]).then_inc(consts, 16)
            sp.dma_start(keep["strict"][:, :], io["c_strict"]).then_inc(consts, 16)
            sp.dma_start(keep["levels"][:, :, :], io["c_levels"]).then_inc(consts, 16)
            strips = io["w_ada"].rearrange("l (k p) n -> (l k) p n", p=P)
            for p in range(2):
                sp.dma_start(wa[:, p, :], strips[p]).then_inc(w_in[p], 16)
            with sp.Fori(0, KD - 1) as i:
                for p in range(2):
                    sp.wait_ge(used, i * 2 + (p + 1))
                    sp.dma_start(wa[:, p, :], strips[i * 2 + (p + 2)]).then_inc(w_in[p], 16)

        @block.gpsimd
        def _(pool):
            for l in range(2):
                pool.dma_start(gpre[:, l, :], io["g_pre"][l].rearrange("(k p) -> p k", p=P), allow_slow_non_contiguous=True).then_inc(weights, 16)
                pool.dma_start(gpost[:, l, :], io["g_post"][l].rearrange("(k p) -> p k", p=P), allow_slow_non_contiguous=True).then_inc(weights, 16)
                pool.dma_start(bT[:, l, :], io["b_ada"][l].rearrange("(k p) -> p k", p=P), allow_slow_non_contiguous=True).then_inc(weights, 16)
                pool.dma_start(lb[:, l, :], io["lb_logits"][l].rearrange("(k p) -> p k", p=P), allow_slow_non_contiguous=True).then_inc(weights, 16)
            pool.memset(keep["ones"][:, :], 1.0)
            pool.memset(keep["mhalf"][:, :], -0.5).then_inc(silu, 1)

        @block.scalar
        def _(act):
            act.wait_ge(consts, 8 * 16)
            for j in range(2):
                act.activation(scT[:, :, j], cT[:, j, :], ACT.Silu).then_inc(silu, 1)
            act.wait_ge(lmax, 1)
            act.activation(lt[:, 1:3, :], lt[:, 1:3, :], ACT.Exp).then_inc(lexp, 1)

        @block.tensor
        def _(pe):
            pe.wait_ge(silu, 3)
            pe.wait_ge(zeroed, 1)
            for l in range(2):
                with pe.Fori(0, KD // 2) as i:
                    for p in range(2):
                        pe.wait_ge(w_in[p], (i + (l * KD // 2 + 1)) * 16)
                        for ct in range(24):
                            mm = pe.matmul(mps[:, l, 2 * ct:2 * ct + 2], wa[:, p, ct * P:(ct + 1) * P],
                                           scT[:, i * 2 + p, :], start=False, stop=False, skip_group_check=True)
                        mm.then_inc(used, 1)

        @block.vector
        def _(dve):
            ln = Links(dve, link, 11, 0)
            dve.memset(mps[:, :, :], 0.0).then_inc(zeroed, 1)
            dve.wait_ge(weights, 8 * 16)
            dve.wait_ge(consts, 8 * 16)
            ln.link(dve.tensor_tensor(lt[:, 0, :], lb[:, 0, :], lb[:, 1, :], ALU.max))
            for l in range(2):
                t = dve.tensor_tensor(lt[:, 1 + l, :], lb[:, l, :], lt[:, 0, :], ALU.subtract)
            t.then_inc(lmax, 1)
            dve.wait_ge(lexp, 1)
            ln.link(dve.tensor_tensor(lt[:, 0, :], lt[:, 1, :], lt[:, 2, :], ALU.add))
            ln.link(dve.reciprocal(lt[:, 3, :], lt[:, 0, :]))
            ln.link(dve.tensor_tensor(lt[:, 1, :], lt[:, 1, :], lt[:, 3, :], ALU.mult))
            ln.link(dve.tensor_tensor(lt[:, 2, :], lt[:, 2, :], lt[:, 3, :], ALU.mult))
            ln.link(dve.tensor_tensor(lt[:, 2, :], lt[:, 2, :], lt[:, 1, :], ALU.add))
            ln.link(dve.tensor_tensor(keep["lb"][:, 0, :], lt[:, 2, :], lt[:, 1, :], ALU.subtract))
            ln.link(dve.tensor_scalar(keep["lb"][:, 1, :], keep["lb"][:, 0, :], -1.0, 1.0, ALU.mult, ALU.add))
            dve.wait_ge(used, 2 * KD)
            for l in range(2):
                t = dve.tensor_tensor(md[:, l, :, :], mps[:, l, 0:48].rearrange("p (a b) -> p a b", b=2),
                                      bT[:, l, :].unsqueeze(2).to_broadcast([P, 24, 2]), ALU.add)
            ln.link(t)
            for l in range(2):
                for c in range(2):
                    t = dve.tensor_scalar(keep["mA"][:, l, c, :], md[:, l, 8:16, c], 1.0, None, ALU.add)
                    dve.tensor_copy(keep["mB"][:, l, c, :], md[:, l, 0:8, c])
                    u = dve.tensor_tensor(keep["gg"][:, l, c, :], md[:, l, 16:24, c], gpost[:, l, :], ALU.mult)
            ln.link(u)
            for l in range(2):
                for c in range(2):
                    t = dve.tensor_tensor(keep["mA"][:, l, c, :], keep["mA"][:, l, c, :], gpre[:, l, :], ALU.mult)
            ln.link(t)
            ln.end()


def norm_transpose(layer, keep, xt, xn, ms, rs, hT, xps, S):

    def dve_norm(dve, t, p, i):
        dve.wait_ge(S["x_in"][p], (i + 1) * 16)
        dve.wait_ge(S["xT"], t * 2)
        dve.tensor_tensor_reduce(xn[:, :], xt[:, p, :], xt[:, p, :], 1.0 / D, EPS,
                                 ALU.mult, ALU.add, ms[:, 0:1]).then_inc(S["x_ms"], 1)
        dve.wait_ge(S["x_rs"], t + 1)
        dve.tensor_scalar(xn[:, :], xt[:, p, :], rs[:, 0:1], None, ALU.mult).then_inc(S["xn"], 1)

    def pool_norm(pool, t):
        pool.wait_ge(S["x_ms"], t + 1)
        pool.tensor_tensor(rs[:, 0:1], ms[:, 0:1], keep["mhalf"][:, 0:1], ALU.pow).then_inc(S["x_rs"], 1)

    def pe_transposes(pe, t):
        pe.wait_ge(S["xn"], t + 1)
        pe.wait_ge(S["hT_a"], t)
        pe.wait_ge(S["hT_v"], t)
        for k in range(KD):
            mm = pe.transpose(xps[k // 4][:, (k % 4) * P:(k % 4 + 1) * P], xn[:, k * P:(k + 1) * P], keep["ident"][:, :])
            if k % 4 == 3:
                mm.then_inc(S["xT"], 1)

    def act_hT(act, t, p):
        act.wait_ge(S["xT"], t * 2 + 1)
        for k in range(4):
            u = act.activation(hT[:, p, k, :], xps[0][:, k * P:(k + 1) * P], ACT.Identity,
                               bias=keep["mB"][:, layer, cond(t), k:k + 1], scale=keep["mA"][:, layer, cond(t), k:k + 1])
        u.then_inc(S["hT_a"], 1)

    def dve_hT(dve, t, p):
        dve.wait_ge(S["xT"], t * 2 + 2)
        for k in range(4, 8):
            u = dve.tensor_scalar(hT[:, p, k, :], xps[1][:, (k - 4) * P:(k - 3) * P],
                                  keep["mA"][:, layer, cond(t), k:k + 1], keep["mB"][:, layer, cond(t), k:k + 1],
                                  ALU.mult, ALU.add)
        u.then_inc(S["hT_v"], 1)

    return dve_norm, pool_norm, pe_transposes, act_hT, dve_hT


def norm_sems(sem, tag):
    S = {n: sem(f"{tag}_{n}") for n in ("x_ms", "x_rs", "xn", "xT", "hT_a", "hT_v")}
    S["x_in"] = [sem(f"{tag}_x_in0"), sem(f"{tag}_x_in1")]
    return S


def in_even(nc, io, keep, scr):
    with ExitStack() as ctx:
        sb, ps, sem = stage(nc, ctx)
        w = sb("a_w", [P, KD, IN_E])
        xt = sb("a_xt", [P, 2, D])
        xn = sb("a_xn", [P, D])
        hT = sb("a_hT", [P, 2, KD, P])
        xp = sb("a_xp", [P, NCT, P + 3])
        cv = sb("a_cv", [P, 2, NCT, P])
        z = sb("a_z", [P, 2, D])
        ba = sb("a_ba", [P, 2, 8])
        cq = sb("a_cq", [P, QL])
        kv = sb("a_kv", [P, KL + ROPE])
        cqn = sb("a_cqn", [P, 2, QL])
        kvn = sb("a_kvn", [P, 2, KL + ROPE])
        junk = sb("a_junk", [P, QL + KL])
        cs = sb("a_cs", [P, 2, 64])
        rt = sb("a_rt", [P, 2, ROPE])
        cw = sb("a_cw", [P, 4, NCT])
        gq = sb("a_gq", [P, QL])
        gkv = sb("a_gkv", [P, KL])
        ms = sb("a_ms", [P, 1])
        rs = sb("a_rs", [P, 1])
        ms2 = sb("a_ms2", [P, 2])
        rs2 = sb("a_rs2", [P, 2])
        xps = [ps("a_x0"), ps("a_x1")]
        bank = [ps(f"a_p{i}") for i in range(6)]
        S = norm_sems(sem, "a")
        cs_in = [sem("a_cs_in0"), sem("a_cs_in1")]
        stored = [sem("a_stored0"), sem("a_stored1")]
        w_in, const_in = sem("a_w_in"), sem("a_const_in")
        proj, act_out, kv_out = sem("a_proj"), sem("a_act_out"), sem("a_kv_out")
        conv, silu_q, hist = sem("a_conv"), sem("a_silu_q"), sem("a_hist")
        lat_ms, lat_rs, lat = sem("a_lat_ms"), sem("a_lat_rs"), sem("a_lat")
        link, hist_in, hist_out = sem("a_link"), sem("a_hist_in"), sem("a_hist_out")
        dve_norm, pool_norm, pe_tr, act_hT, dve_hT = norm_transpose(0, keep, xt, xn, ms, rs, hT, xps, S)
        block = ctx.enter_context(nc.Block())
        STORES = 6
        OUTS = 6

        @block.sync
        def _(sp):
            def load(t, p):
                if last(t):
                    sp.dma_start(xt[0:DEC, p, :], io["x_sample"][0]).then_inc(S["x_in"][p], 16)
                else:
                    sp.dma_start(xt[:, p, :], io["x_prompt"][0].rearrange("(t p) d -> t p d", p=P)[t]).then_inc(S["x_in"][p], 16)
                sp.dma_start(cs[:, p, :], io["c_rope"][t]).then_inc(cs_in[p], 16)

            load(0, 0)
            sp.dma_start(gq[:, :], io["g_q"][0:1, :].to_broadcast([P, QL])).then_inc(const_in, 16)
            sp.dma_start(gkv[:, :], io["g_kv"][0:1, :].to_broadcast([P, KL])).then_inc(const_in, 16)
            for j in range(4):
                sp.dma_start(cw[:, j, :], io["conv_w"][0, j].rearrange("(c p) -> p c", p=P), allow_slow_non_contiguous=True).then_inc(const_in, 16)
            for k in range(KD):
                sp.dma_start(w[:, k, :], io["w_in_e"][0, k * P:(k + 1) * P, :]).then_inc(w_in, 16)

            def step(t, p, i):
                if not last(t):
                    sp.wait_ge(S["xn"], t)
                    sp.wait_ge(lat, t)
                    load(t + 1, 1 - p)
                sp.wait_ge(silu_q, t + 1)
                sp.dma_start(scr["qkv"][t], cv[:, p, :, :]).then_inc(stored[p], 16)
                sp.wait_ge(act_out, (t + 1) * OUTS)
                sp.dma_start(scr["z"][t], z[:, p, :]).then_inc(stored[p], 16)
                sp.dma_start(scr["ba"][t], ba[:, p, :]).then_inc(stored[p], 16)
                sp.wait_ge(lat, t + 1)
                sp.dma_start(scr["cq"][t], cqn[:, p, :]).then_inc(stored[p], 16)
                if last(t):
                    ck, kr, n = io["s_ckv"][0, 0], io["s_kr"][0, 0], DEC
                else:
                    ck = io["p_ckv"][0, 0].rearrange("(t p) c -> t p c", p=P)[t]
                    kr, n = io["p_kr"][0, 0].rearrange("(t p) c -> t p c", p=P)[t], P
                sp.dma_start(ck, kvn[0:n, p, 0:KL]).then_inc(stored[p], 16)
                sp.dma_start(kr, kvn[0:n, p, KL:KL + ROPE]).then_inc(stored[p], 16)

            tiles_of(sp, step)
            for p in range(2):
                sp.wait_ge(stored[p], (TILES + 1 - p) // 2 * STORES * 16)

        @block.gpsimd
        def _(pool):
            def conv_rows(dst, at, cols):
                for j in range(3):
                    pool.dma_start(dst[0, 0, j].rearrange("(c p) -> p c", p=P), xp[:, :, at + j], allow_slow_non_contiguous=True).then_inc(cols, 16)

            def step(t, p, i):
                if isinstance(t, int) and t == NT - 1:
                    pool_norm(pool, t + 1)
                    pool.wait_ge(act_out, t * OUTS + 3)
                    conv_rows(io["p_conv"], P, hist_out)
                    pool.wait_ge(hist, NT)
                    for j in range(3):
                        pool.dma_start(xp[:, :, j], io["state_conv"][0, 0, j].rearrange("(c p) -> p c", p=P), allow_slow_non_contiguous=True).then_inc(hist_in, 16)
                elif last(t):
                    pool.wait_ge(act_out, t * OUTS + 3)
                    conv_rows(io["s_conv"], DEC, hist_out)
                else:
                    pool_norm(pool, t + 1)
                pool.wait_ge(lat_ms, t + 1)
                pool.tensor_tensor(rs2[:, :], ms2[:, :], keep["mhalf"][:, 0:2], ALU.pow).then_inc(lat_rs, 1)

            pool_norm(pool, 0)
            tiles_of(pool, step)
            pool.wait_ge(hist_out, 6 * 16)

        @block.scalar
        def _(act):
            def step(t, p, i):
                act.wait_ge(hist, t)
                if last(t):
                    act.wait_ge(hist_out, 3 * 16)
                for g in range(3):
                    act.wait_ge(proj, t * 7 + g + 1)
                    act.copy(xp[:, 4 * g:4 * g + 4, 3:], bank[g][:, :].rearrange("p (c t) -> p c t", c=4)).then_inc(act_out, 1)
                if not last(t):
                    act_hT(act, t + 1, 1 - p)
                act.wait_ge(proj, t * 7 + 4)
                act.wait_ge(stored[p], i * (STORES * 16))
                act.copy(ba[:, p, :], bank[3][:, 0:8])
                act.activation(z[:, p, 0:504], bank[3][:, 8:512], ACT.Silu).then_inc(act_out, 1)
                act.wait_ge(proj, t * 7 + 5)
                act.wait_ge(lat, t)
                act.activation(z[:, p, 504:512], bank[4][:, 0:8], ACT.Silu)
                act.copy(cq[:, :], bank[4][:, 8:392]).then_inc(act_out, 1)
                act.wait_ge(conv, t + 1)
                act.activation(cv[:, p, :, :], cv[:, p, :, :], ACT.Silu).then_inc(silu_q, 1)
                act.wait_ge(proj, t * 7 + 7)
                act.activation(z[:, p, 512:1024], bank[0][:, :], ACT.Silu).then_inc(act_out, 1)

            act.wait_ge(S["xT"], 1)
            act_hT(act, 0, 0)
            tiles_of(act, step)

        @block.tensor
        def _(pe):
            def step(t, p, i):
                pe.wait_ge(S["hT_a"], t + 1)
                pe.wait_ge(S["hT_v"], t + 1)
                pe.wait_ge(act_out, t * OUTS)
                for g in range(3):
                    for c in range(4 * g, 4 * g + 4):
                        for k in range(KD):
                            mm = pe.matmul(bank[g][:, (c % 4) * P:(c % 4 + 1) * P], w[:, k, c * P:(c + 1) * P],
                                           hT[:, p, k, :], start=k == 0, stop=k == KD - 1)
                    mm.then_inc(proj, 1)
                if not last(t):
                    pe_tr(pe, t + 1)
                for g, (a, b) in enumerate(EVEN_GROUPS):
                    dst = bank[0] if g == 3 else bank[3 + g]
                    if g == 2:
                        pe.wait_ge(kv_out, t)
                    if g == 3:
                        pe.wait_ge(act_out, t * OUTS + 1)
                    for k in range(KD):
                        mm = pe.matmul(dst[:, 0:b - a], hT[:, p, k, :], w[:, k, a:b], start=k == 0, stop=k == KD - 1)
                    mm.then_inc(proj, 1)

            pe_tr(pe, 0)
            pe.wait_ge(w_in, 16 * KD)
            tiles_of(pe, step)

        @block.vector
        def _(dve):
            def step(t, p, i):
                ln = Links(dve, link, 6, t)
                if not last(t):
                    dve_norm(dve, t + 1, 1 - p, i + p)
                dve.wait_ge(act_out, t * OUTS + 3)
                if last(t):
                    dve.wait_ge(hist_in, 3 * 16)
                dve.wait_ge(stored[p], i * (STORES * 16))
                for c in range(NCT):
                    u = dve.tensor_scalar(cv[:, p, c, :], xp[:, c, 0:P], cw[:, 0, c:c + 1], None, ALU.mult)
                for j in range(1, 4):
                    ln.link(u)
                    for c in range(NCT):
                        u = dve.scalar_tensor_tensor(out=cv[:, p, c, :], in0=xp[:, c, j:j + P], scalar=cw[:, j, c:c + 1],
                                                     in1=cv[:, p, c, :], op0=ALU.mult, op1=ALU.add)
                u.then_inc(conv, 1)
                dve.wait_ge(conv, t + 1)
                dve.tensor_copy(xp[:, :, 0:3], xp[:, :, P:P + 3]).then_inc(hist, 1)
                if not last(t):
                    dve_hT(dve, t + 1, 1 - p)
                dve.wait_ge(proj, t * 7 + 6)
                dve.tensor_copy(kv[:, :], bank[5][:, 0:KL + ROPE]).then_inc(kv_out, 1)
                dve.wait_ge(kv_out, t + 1)
                dve.wait_ge(act_out, t * OUTS + 5)
                dve.tensor_tensor_reduce(junk[:, 0:QL], cq[:, :], cq[:, :], 1.0 / QL, EPS, ALU.mult, ALU.add, ms2[:, 0:1])
                dve.tensor_tensor_reduce(junk[:, QL:QL + KL], kv[:, 0:KL], kv[:, 0:KL], 1.0 / KL, EPS, ALU.mult, ALU.add,
                                         ms2[:, 1:2]).then_inc(lat_ms, 1)
                dve.wait_ge(cs_in[p], (i + 1) * 16)
                dve.tensor_tensor(rt[:, 0, :], kv[:, KL:KL + ROPE], cs[:, p, 0:32], ALU.mult)
                dve.tensor_tensor(rt[:, 1, 0:16], kv[:, KL + 16:KL + 32], cs[:, p, 32:48], ALU.mult)
                ln.link(dve.tensor_tensor(rt[:, 1, 16:32], kv[:, KL:KL + 16], cs[:, p, 48:64], ALU.mult))
                ln.link(dve.tensor_tensor(kvn[:, p, KL:KL + ROPE], rt[:, 0, :], rt[:, 1, :], ALU.add))
                dve.wait_ge(lat_rs, t + 1)
                ln.link(dve.scalar_tensor_tensor(out=kvn[:, p, 0:KL], in0=kv[:, 0:KL], scalar=rs2[:, 1:2], in1=gkv[:, :],
                                                 op0=ALU.mult, op1=ALU.mult))
                dve.scalar_tensor_tensor(out=cqn[:, p, :], in0=cq[:, :], scalar=rs2[:, 0:1], in1=gq[:, :],
                                         op0=ALU.mult, op1=ALU.mult).then_inc(lat, 1)
                ln.end()

            dve.memset(xp[:, :, 0:3], 0.0)
            dve.wait_ge(const_in, 6 * 16)
            dve_norm(dve, 0, 0, 0)
            dve_hT(dve, 0, 0)
            tiles_of(dve, step)


def bc(ap, n):
    return ap.unsqueeze(2).to_broadcast([ap.shape[0], ap.shape[1], n])


def over_heads(ap, h):
    return ap.unsqueeze(1).to_broadcast([ap.shape[0], h, ap.shape[1]])


def since(eng, sem, n):
    if not (isinstance(n, int) and n <= 0):
        eng.wait_ge(sem, n)


def delta(nc, io, keep, scr):
    H = HA
    with ExitStack() as ctx:
        sb, ps, sem = stage(nc, ctx)
        sc = sb("d_sc", [P, 2, 3 * H, P])
        ba = sb("d_ba", [P, 2, 8])
        za = sb("d_za", [P, 2, H * P])
        dtb, nea, gna = sb("d_dtb", [P, H]), sb("d_nea", [P, H]), sb("d_gna", [P, P])
        x8, e8, u8, l4, w4 = (sb(f"d_{n}", [P, 8]) for n in ("x8", "e8", "u8", "l4", "w4"))
        xa, beta, g = sb("d_xa", [P, H]), sb("d_beta", [P, H]), sb("d_g", [P, H])
        gB = sb("d_gB", [P, H, P])
        g8, ge8, bg = sb("d_g8", [P, 8]), sb("d_ge8", [P, 8]), sb("d_bg", [P, H])
        EB, Dm, Em = sb("d_EB", [P, H, P]), sb("d_Dm", [P, H, P]), sb("d_Em", [P, H, P])
        eS = sb("d_eS", [P, 2, H, 2])
        qk, sq = sb("d_qk", [P, 2 * H, P]), sb("d_sq", [P, 2 * H, P])
        ss8, r8, qs8 = sb("d_ss8", [P, 8]), sb("d_r8", [P, 8]), sb("d_qs8", [P, 8])
        vb, kb, kd = sb("d_vb", [P, 2, H, P]), sb("d_kb", [P, 2, H, P]), sb("d_kd", [P, 2, H, P])
        qkT, qe = sb("d_qkT", [P, 2 * H, P]), sb("d_qe", [P, 2, H, P])
        M, MT, A = sb("d_M", [P, H, P]), sb("d_MT", [P, H, P]), sb("d_A", [P, 2, H, P])
        CT = sb("d_CT", [P, 2, 5, H, P])
        T, U, X = sb("d_T", [P, 2, H, P]), sb("d_U", [P, 2, H, P]), sb("d_X", [P, H, P])
        wT, u, vn = sb("d_wT", [P, H, P]), sb("d_u", [P, H, P]), sb("d_vn", [P, H, P])
        St = sb("d_S", [P, H, P])
        o, osq, gz = sb("d_o", [P, H, P]), sb("d_osq", [P, H, P]), sb("d_gz", [P, H, P])
        os4, or4 = sb("d_os4", [P, H]), sb("d_or4", [P, H])
        oT = sb("d_oT", [P, 2, H, P])
        A0, A1, A2, BX, BT, BU, BS, BO = (ps(f"d_b{i}") for i in range(8))
        names = ("x8 e8 u8 ln g gB gc gcB g8 t8 ge8 EB DE E12 mask qkvT qk_out v_out ss r8 qkn qkT qkT_out kbkd kk M A MT "
                 "MT_out T1 U1 wu wT_out u_out o_ps o_out os or4 gz og normed ogT oT_out beta qe bg").split()
        R = {n: sem("d_" + n) for n in names}
        CTs, Xs, Xo, YYs, TUs = sem("d_CTs"), sem("d_Xs"), sem("d_Xo"), sem("d_YYs"), sem("d_TUs")
        wSs, vns, kvs, Ss = sem("d_wSs"), sem("d_vns"), sem("d_kvs"), sem("d_Ss")
        in_, stored = [sem("d_in0"), sem("d_in1")], [sem("d_st0"), sem("d_st1")]
        z_in = [sem("d_z0"), sem("d_z1")]
        const_in, state_out, state_in, s0 = sem("d_const"), sem("d_s_out"), sem("d_s_in"), sem("d_s0")
        link, olink, plink, ea, qs_in = sem("d_link"), sem("d_olink"), sem("d_plink"), sem("d_ea"), sem("d_qs_in")
        block = ctx.enter_context(nc.Block())
        flat = lambda b: b.rearrange("p h t -> p (h t)")
        heads = lambda b: b[:, :].rearrange("p (h t) -> p h t", h=H)

        def state(ap):
            return ap.rearrange("h d e -> d h e")

        def steps_of(eng, step):
            step(-2, 0, -1, True, False, False)
            step(-1, 1, -1, True, True, False)
            with eng.Fori(0, NT // 2 - 1) as i:
                step(i * 2, 0, i, True, True, True)
                step(i * 2 + 1, 1, i, True, True, True)
            step(NT - 2, 0, NT // 2 - 1, True, True, True)
            step(NT - 1, 1, NT // 2 - 1, False, True, True)
            step(SAMPLE, 0, NT // 2, False, False, True)

        @block.sync
        def _(sp):
            sp.dma_start(dtb[:, :], io["dt_bias"][0:1, :].to_broadcast([P, H])).then_inc(const_in, 16)
            sp.dma_start(nea[:, :], io["a_log"][0:1, :].to_broadcast([P, H])).then_inc(const_in, 16)
            sp.dma_start(gna[:, :], io["g_norm_a"][0:1, :].to_broadcast([P, P])).then_inc(const_in, 16)

            def load(t, p, ahead=0):
                sp.dma_start(sc[:, p, :, :], scr["qkv"][ahead:][t]).then_inc(in_[p], 16)
                sp.dma_start(ba[:, p, :], scr["ba"][ahead:][t]).then_inc(in_[p], 16)

            def load_z(t, p, ahead=0):
                sp.dma_start(za[:, p, :], scr["z"][ahead:][t, :, 0:H * P]).then_inc(z_in[p], 16)

            load(0, 0)
            load(1, 1)
            load_z(0, 0)

            def step(t, p, i, operands, inverse, output):
                if not output:
                    return
                if operands and not (isinstance(t, int) and t + 3 > SAMPLE):
                    sp.wait_ge(R["x8"], t + 2)
                    sp.wait_ge(R["qkvT"], t * 3 + 6)
                    load(t, 1 - p, ahead=3)
                if not last(t):
                    sp.wait_ge(R["gz"], t)
                    load_z(t, 1 - p, ahead=1)
                sp.wait_ge(R["oT_out"], t + 1)
                sp.dma_start(scr["oa"][t], flat(oT[:, p, :, :])).then_inc(stored[p], 16)
                if isinstance(t, int) and t == NT - 1:
                    sp.wait_ge(Ss, 2 * NT)
                    sp.dma_start(state(io["p_delta"][0, 0]), St[:, :, :]).then_inc(state_out, 16)
                    sp.wait_ge(state_out, 16)
                    sp.dma_start(St[:, :, :], state(io["state_delta"][0, 0])).then_inc(state_in, 16)
                if last(t):
                    sp.wait_ge(Ss, 2 * NT + 1)
                    sp.dma_start(state(io["s_delta"][0, 0]), St[:, :, :]).then_inc(state_out, 16)

            sp.wait_ge(R["x8"], 1)
            sp.wait_ge(R["qkvT"], 3)
            load(2, 0)
            steps_of(sp, step)
            sp.wait_ge(state_out, 32)
            sp.wait_ge(stored[0], (TILES + 1) // 2 * 16)
            sp.wait_ge(stored[1], TILES // 2 * 16)

        @block.gpsimd
        def _(pool):
            def step(t, p, i, operands, inverse, output):
                a = t + 2
                if output:
                    pool.wait_ge(z_in[p], (i + 1) * 16)
                    pool.wait_ge(R["og"], t)
                    pool.tensor_tensor(gz[:, :, :], za[:, p, :].rearrange("p (h t) -> p h t", h=H), over_heads(gna[:, :], H), ALU.mult).then_inc(R["gz"], 1)
                if operands:
                    ln = Links(pool, plink, 4, a)
                    pool.wait_ge(R["ss"], a + 1)
                    ln.link(pool.tensor_tensor(r8[:, :], ss8[:, :], keep["mhalf"][:, :], ALU.pow))
                    pool.tensor_tensor(r8[:, :], r8[:, :], qs8[:, :], ALU.mult).then_inc(R["r8"], 1)
                    pool.wait_ge(R["E12"], a + 1)
                    ln.link(pool.tensor_tensor(Dm[:, :, :], Dm[:, :, :], over_heads(keep["strict"][:, :], H), ALU.mult))
                    pool.tensor_tensor(Dm[:, :, :], Dm[:, :, :], bc(beta[:, :], P), ALU.mult)
                    pool.tensor_tensor(Em[:, :, :], Em[:, :, :], over_heads(keep["cums"][:, :], H), ALU.mult).then_inc(R["mask"], 1)
                if output:
                    pool.wait_ge(R["os"], t + 1)
                    pool.tensor_tensor(or4[:, :], os4[:, :], keep["mhalf"][:, 0:H], ALU.pow).then_inc(R["or4"], 1)
                if operands:
                    pool.wait_ge(R["qkn"], a + 1)
                    pool.wait_ge(R["bg"], a + 1)
                    since(pool, kvs, (a - 1) * 2)
                    since(pool, R["wu"], a - 1)
                    pool.tensor_tensor(kb[:, p, :, :], qk[:, H:2 * H, :], bc(bg[:, :], P), ALU.mult)
                    pool.tensor_tensor(kd[:, p, :, :], qk[:, H:2 * H, :], bc(ge8[:, H:8], P), ALU.mult).then_inc(R["kbkd"], 1)
                    pool.wait_ge(R["M"], a + 1)
                    ln.link(pool.tensor_tensor(T[:, p, :, :], M[:, :, :], over_heads(keep["low1"][:, :], H), ALU.mult))
                    pool.tensor_tensor(T[:, p, :, :], over_heads(keep["ident"][:, :], H), T[:, p, :, :], ALU.subtract).then_inc(R["T1"], 1)
                    pool.wait_ge(R["MT_out"], a + 1)
                    ln.link(pool.tensor_tensor(U[:, p, :, :], MT[:, :, :], over_heads(keep["levels"][:, 0, :], H), ALU.mult))
                    pool.tensor_tensor(U[:, p, :, :], over_heads(keep["ident"][:, :], H), U[:, p, :, :], ALU.subtract).then_inc(R["U1"], 1)
                    for n in range(5):
                        pool.tensor_tensor(CT[:, p, n, :, :], MT[:, :, :], over_heads(keep["levels"][:, n + 1, :], H), ALU.mult).then_inc(CTs, 1)
                    ln.end()

            pool.memset(qs8[:, 0:H], float(DK) ** -0.5)
            pool.memset(qs8[:, H:8], 1.0).then_inc(qs_in, 1)
            pool.wait_ge(qs_in, 1)
            pool.wait_ge(const_in, 48)
            steps_of(pool, step)

        @block.scalar
        def _(act):
            def step(t, p, i, operands, inverse, output):
                a, b = t + 2, t + 1

                def X_out(n):
                    act.wait_ge(Xs, b * 5 + n + 1)
                    act.copy(flat(X[:, :, :]), BX[:, :]).then_inc(Xo, 1)

                if operands:
                    act.wait_ge(R["x8"], a + 1)
                    act.activation(e8[:, :], x8[:, :], ACT.Exp, scale=-1.0).then_inc(R["e8"], 1)
                if inverse:
                    X_out(0)
                if operands:
                    act.wait_ge(R["qkvT"], a * 3 + 2)
                    since(act, R["kbkd"], a)
                    act.copy(flat(qk[:, 0:H, :]), A0[:, :])
                    act.copy(flat(qk[:, H:2 * H, :]), A1[:, :]).then_inc(R["qk_out"], 1)
                    act.wait_ge(R["u8"], a + 1)
                    act.activation(l4[:, 0:H], u8[:, H:8], ACT.Ln).then_inc(R["ln"], 1)
                if inverse:
                    X_out(1)
                if operands:
                    act.wait_ge(R["gcB"], a + 1)
                    since(act, R["qe"], a)
                    act.activation(flat(EB[:, :, :]), A1[:, :], ACT.Exp).then_inc(R["EB"], 1)
                if inverse:
                    X_out(2)
                if operands:
                    act.wait_ge(R["t8"], a + 1)
                    since(act, R["kbkd"], a)
                    act.activation(ge8[:, :], g8[:, :], ACT.Exp).then_inc(R["ge8"], 1)
                    act.wait_ge(R["DE"], a + 1)
                    act.activation(Dm[:, :, :], Dm[:, :, :], ACT.Exp, scale=-1.0)
                    act.activation(Em[:, :, :], Em[:, :, :], ACT.Exp).then_inc(R["E12"], 1)
                if output:
                    act.wait_ge(R["o_ps"], t + 1)
                    act.copy(flat(o[:, :, :]), BO[:, :]).then_inc(R["o_out"], 1)
                if inverse:
                    X_out(3)
                if operands:
                    act.wait_ge(R["qkT"], a + 1)
                    act.copy(flat(qkT[:, 0:H, :]), A0[:, :])
                    act.copy(flat(qkT[:, H:2 * H, :]), A2[:, :]).then_inc(R["qkT_out"], 1)
                if inverse:
                    X_out(4)
                if operands:
                    act.wait_ge(R["MT"], a + 1)
                    since(act, CTs, a * 5)
                    act.copy(flat(MT[:, :, :]), A2[:, :]).then_inc(R["MT_out"], 1)
                if output:
                    act.wait_ge(R["ogT"], t + 1)
                    act.wait_ge(stored[p], i * 16)
                    act.copy(flat(oT[:, p, :, :]), BS[:, :]).then_inc(R["oT_out"], 1)
                if inverse:
                    act.wait_ge(R["wu"], b + 1)
                    since(act, vns, b * 2)
                    act.copy(flat(wT[:, :, :]), BX[:, :]).then_inc(R["wT_out"], 1)
                    act.copy(flat(u[:, :, :]), BT[:, :]).then_inc(R["u_out"], 1)

            act.wait_ge(const_in, 48)
            act.activation(nea[:, :], nea[:, :], ACT.Exp).then_inc(ea, 1)
            steps_of(act, step)

        @block.tensor
        def _(pe):
            ident, cums = keep["ident"], keep["cums"]

            def step(t, p, i, operands, inverse, output):
                a, b, pb = t + 2, t + 1, 1 - p

                def X_level(n):
                    pe.wait_ge(CTs, b * 5 + n + 1)
                    if n:
                        pe.wait_ge(TUs, b * 5 + n)
                    for h in range(H):
                        mm = pe.matmul(BX[:, h * P:(h + 1) * P], CT[:, pb, n, h, :], T[:, pb, h, :], start=True, stop=True)
                    mm.then_inc(Xs, 1)

                def TU_level(n):
                    pe.wait_ge(Xo, b * 5 + n + 1)
                    for h in range(H):
                        if n < 4:
                            pe.matmul(BT[:, h * P:(h + 1) * P], U[:, pb, h, :], X[:, h, :], start=True, stop=True)
                        mm = pe.matmul(BU[:, h * P:(h + 1) * P], X[:, h, :], U[:, pb, h, :], start=True, stop=True)
                    mm.then_inc(YYs, 1)

                def chunk(c):
                    lo, hi = c * CH, (c + 1) * CH
                    if c:
                        pe.wait_ge(Ss, t * 2 + 1)
                    elif not last(t):
                        pe.wait_ge(Ss, t * 2)
                    for h in range(H):
                        mm = pe.matmul(BS[lo:hi, h * P:(h + 1) * P], wT[:, h, lo:hi], St[:, h, :], start=True, stop=True)
                    mm.then_inc(wSs, 1)
                    for h in range(H):
                        pe.matmul(BO[lo:hi, h * P:(h + 1) * P], qe[:, p, h, lo:hi], St[:, h, :],
                                  start=h == 0, stop=False, skip_group_check=True)

                def into_state(c):
                    lo, hi = c * CH, (c + 1) * CH
                    pe.wait_ge(vns, t * 2 + c + 1)
                    if not (last(t) and c):
                        for h in range(H):
                            mm = pe.matmul(BS[:, h * P:(h + 1) * P], kd[lo:hi, p, h, :], vn[lo:hi, h, :], start=True, stop=True)
                        mm.then_inc(kvs, 1)

                if operands:
                    pe.wait_ge(in_[p], i * 32 + 64)
                    since(pe, R["A"], a)
                    since(pe, R["MT_out"], a)
                    for n, bank in enumerate((A0, A1, A2)):
                        for h in range(H):
                            mm = pe.transpose(bank[:, h * P:(h + 1) * P], sc[:, p, n * H + h, :], ident[:, :])
                        mm.then_inc(R["qkvT"], 1)
                if inverse:
                    pe.wait_ge(R["T1"], b + 1)
                    pe.wait_ge(R["U1"], b + 1)
                    since(pe, R["wT_out"], b)
                    X_level(0)
                if output:
                    pe.wait_ge(R["wT_out"], t + 1)
                    pe.wait_ge(R["qe"], t + 1)
                    pe.wait_ge(R["oT_out"], t)
                    pe.wait_ge(R["o_out"], t)
                    if last(t):
                        pe.wait_ge(state_in, 16)
                    else:
                        pe.wait_ge(s0, 1)
                    chunk(0)
                if inverse:
                    since(pe, R["u_out"], b)
                    TU_level(0)
                if output:
                    into_state(0)
                if inverse:
                    X_level(1)
                if operands:
                    pe.wait_ge(R["qk_out"], a + 1)
                    pe.wait_ge(R["g"], a + 1)
                    pe.matmul(A0[:, 0:H], cums[:, :], g[:, :], start=True, stop=True)
                    pe.matmul(A0[:, H:8], keep["blk"][:, :], g[:, :], start=True, stop=True).then_inc(R["gc"], 1)
                    pe.wait_ge(R["gB"], a + 1)
                    for h in range(H):
                        mm = pe.matmul(A1[:, h * P:(h + 1) * P], gB[:, h, :], cums[:, :], start=True, stop=True)
                    mm.then_inc(R["gcB"], 1)
                if inverse:
                    TU_level(1)
                if output:
                    chunk(1)
                if inverse:
                    X_level(2)
                if output:
                    into_state(1)
                    for h in range(H):
                        mm = pe.matmul(BO[:, h * P:(h + 1) * P], A[:, p, h, :], vn[:, h, :],
                                       start=False, stop=h == H - 1, skip_group_check=True)
                    mm.then_inc(R["o_ps"], 1)
                if inverse:
                    TU_level(2)
                if operands:
                    pe.wait_ge(R["qkn"], a + 1)
                    pe.wait_ge(R["g8"], a + 1)
                    pe.wait_ge(R["v_out"], a + 1)
                    for h in range(2 * H):
                        mm = pe.transpose((A0, A2)[h // H][:, h % H * P:(h % H + 1) * P], qk[:, h, :], ident[:, :])
                    mm.then_inc(R["qkT"], 1)
                if inverse:
                    X_level(3)
                    TU_level(3)
                if operands:
                    pe.wait_ge(R["qkT_out"], a + 1)
                    pe.wait_ge(R["DE"], a + 1)
                    for h in range(H):
                        pe.matmul(A1[:, h * P:(h + 1) * P], qkT[:, H + h, :], qkT[:, H + h, :], start=True, stop=True)
                        mm = pe.matmul(A0[:, h * P:(h + 1) * P], qkT[:, H + h, :], qkT[:, h, :], start=True, stop=True)
                    mm.then_inc(R["kk"], 1)
                if inverse:
                    X_level(4)
                if operands:
                    pe.wait_ge(R["M"], a + 1)
                    for h in range(H):
                        mm = pe.transpose(A2[:, h * P:(h + 1) * P], M[:, h, :], ident[:, :])
                    mm.then_inc(R["MT"], 1)
                if inverse:
                    TU_level(4)
                if output:
                    pe.wait_ge(R["og"], t + 1)
                    if not last(t):
                        pe.wait_ge(Ss, t * 2 + 2)
                    for h in range(H):
                        mm = pe.transpose(BS[:, h * P:(h + 1) * P], o[:, h, :], ident[:, :])
                    mm.then_inc(R["ogT"], 1)
                if inverse:
                    pe.wait_ge(TUs, b * 5 + 5)
                    pe.wait_ge(R["kbkd"], b + 1)
                    for h in range(H):
                        pe.matmul(BX[:, h * P:(h + 1) * P], kb[:, pb, h, :], U[:, pb, h, :], start=True, stop=True)
                        mm = pe.matmul(BT[:, h * P:(h + 1) * P], U[:, pb, h, :], vb[:, pb, h, :], start=True, stop=True)
                    mm.then_inc(R["wu"], 1)

            steps_of(pe, step)

        @block.vector
        def _(dve):
            def step(t, p, i, operands, inverse, output):
                a, b, pb = t + 2, t + 1, 1 - p
                ln, on = Links(dve, link, 7, a), Links(dve, olink, 2, t)

                def subtract(n):
                    dve.wait_ge(YYs, b * 5 + n + 1)
                    if n < 4:
                        dve.tensor_tensor(T[:, pb, :, :], T[:, pb, :, :], heads(BT), ALU.subtract)
                    dve.tensor_tensor(U[:, pb, :, :], U[:, pb, :, :], heads(BU), ALU.subtract).then_inc(TUs, 1)

                def new_values(c):
                    lo, hi = c * CH, (c + 1) * CH
                    dve.wait_ge(wSs, t * 2 + c + 1)
                    dve.tensor_tensor(flat(vn[lo:hi, :, :]), flat(u[lo:hi, :, :]), BS[lo:hi, :], ALU.subtract).then_inc(vns, 1)

                def update(c):
                    if not (last(t) and c):
                        dve.wait_ge(kvs, t * 2 + c + 1)
                        for h in range(H):
                            d = dve.scalar_tensor_tensor(out=St[:, h, :], in0=St[:, h, :], scalar=eS[:, p, h, c:c + 1],
                                                         in1=BS[:, h * P:(h + 1) * P], op0=ALU.mult, op1=ALU.add)
                        d.then_inc(Ss, 1)

                if operands:
                    dve.wait_ge(in_[p], i * 32 + 64)
                    dve.tensor_copy(x8[:, 0:H], ba[:, p, 0:H])
                    ln.link(dve.tensor_tensor(xa[:, :], ba[:, p, H:8], dtb[:, :], ALU.add))
                    dve.scalar_tensor_tensor(out=x8[:, H:8], in0=xa[:, :], scalar=-1.0, in1=xa[:, :], op0=ALU.mult, op1=ALU.max).then_inc(R["x8"], 1)
                    dve.wait_ge(R["e8"], a + 1)
                    dve.tensor_scalar(u8[:, :], e8[:, :], 1.0, None, ALU.add).then_inc(R["u8"], 1)
                    dve.wait_ge(R["u8"], a + 1)
                    since(dve, R["mask"], a)
                    dve.reciprocal(beta[:, :], u8[:, 0:H]).then_inc(R["beta"], 1)
                    ln.link(dve.tensor_scalar(w4[:, 0:H], u8[:, H:8], -1.0, None, ALU.add))
                    ln.link(dve.tensor_tensor(w4[:, 0:H], e8[:, H:8], w4[:, 0:H], ALU.subtract))
                if output:
                    dve.wait_ge(R["u_out"], t + 1)
                    new_values(0)
                if inverse:
                    subtract(0)
                if operands:
                    dve.wait_ge(R["ln"], a + 1)
                    ln.link(dve.tensor_tensor(w4[:, 0:H], w4[:, 0:H], l4[:, 0:H], ALU.add))
                    ln.link(dve.scalar_tensor_tensor(out=w4[:, 0:H], in0=xa[:, :], scalar=0.0, in1=w4[:, 0:H], op0=ALU.max, op1=ALU.add))
                    dve.scalar_tensor_tensor(out=g[:, :], in0=w4[:, 0:H], scalar=-1.0, in1=nea[:, :], op0=ALU.mult, op1=ALU.mult).then_inc(R["g"], 1)
                    dve.wait_ge(R["g"], a + 1)
                    dve.tensor_copy(gB[:, :, :], bc(g[:, :], P)).then_inc(R["gB"], 1)
                if output:
                    update(0)
                if operands:
                    dve.wait_ge(R["qk_out"], a + 1)
                    ln.link(dve.tensor_tensor(sq[:, :, :], qk[:, :, :], qk[:, :, :], ALU.mult))
                    ln.link(dve.tensor_reduce(ss8[:, :], sq[:, :, :], AX, ALU.add))
                    dve.tensor_scalar(ss8[:, :], ss8[:, :], EPS, None, ALU.add).then_inc(R["ss"], 1)
                if inverse:
                    subtract(1)
                if operands:
                    dve.wait_ge(R["qkvT"], a * 3 + 3)
                    dve.wait_ge(R["beta"], a + 1)
                    dve.tensor_tensor(vb[:, p, :, :], heads(A2), bc(beta[:, :], P), ALU.mult).then_inc(R["v_out"], 1)
                if output:
                    new_values(1)
                if operands:
                    dve.wait_ge(R["gc"], a + 1)
                    since(dve, R["ge8"], a)
                    dve.tensor_copy(g8[:, :], A0[:, 0:8]).then_inc(R["g8"], 1)
                    dve.wait_ge(R["g8"], a + 1)
                    dve.wait_ge(R["EB"], a + 1)
                    for h in range(H):
                        dve.tensor_scalar(Dm[:, h, :], A1[:, h * P:(h + 1) * P], g8[:, h:h + 1], 0.0, ALU.subtract, ALU.max)
                        d = dve.tensor_scalar(Em[:, h, :], A1[:, h * P:(h + 1) * P], g8[:, h:h + 1], 0.0, ALU.subtract, ALU.min)
                    d.then_inc(R["DE"], 1)
                    dve.tensor_tensor(g8[:, H:8], g8[:, H:8], g8[:, 0:H], ALU.subtract).then_inc(R["t8"], 1)
                    dve.wait_ge(R["r8"], a + 1)
                    dve.tensor_tensor(qk[:, :, :], qk[:, :, :], bc(r8[:, :], P), ALU.mult).then_inc(R["qkn"], 1)
                if inverse:
                    subtract(2)
                if output:
                    update(1)
                if operands:
                    dve.wait_ge(R["ge8"], a + 1)
                    dve.tensor_tensor(bg[:, :], beta[:, :], ge8[:, 0:H], ALU.mult).then_inc(R["bg"], 1)
                if output:
                    dve.wait_ge(R["o_out"], t + 1)
                    on.link(dve.tensor_tensor(osq[:, :, :], o[:, :, :], o[:, :, :], ALU.mult))
                    on.link(dve.tensor_reduce(os4[:, :], osq[:, :, :], AX, ALU.add))
                    dve.tensor_scalar(os4[:, :], os4[:, :], 1.0 / P, EPS, ALU.mult, ALU.add).then_inc(R["os"], 1)
                    on.end()
                if inverse:
                    subtract(3)
                if operands:
                    dve.wait_ge(R["qkT_out"], a + 1)
                    since(dve, R["o_ps"], a - 1)
                    dve.tensor_copy(eS[:, p, :, :], EB[:, :, CH - 1:P:CH])
                    dve.tensor_tensor(qe[:, p, :, :], qkT[:, 0:H, :], EB[:, :, :], ALU.mult).then_inc(R["qe"], 1)
                    dve.wait_ge(R["kk"], a + 1)
                    dve.wait_ge(R["mask"], a + 1)
                    dve.tensor_tensor(M[:, :, :], heads(A1), Dm[:, :, :], ALU.mult).then_inc(R["M"], 1)
                    dve.tensor_tensor(A[:, p, :, :], heads(A0), Em[:, :, :], ALU.mult).then_inc(R["A"], 1)
                    ln.end()
                if output:
                    dve.wait_ge(R["or4"], t + 1)
                    dve.wait_ge(R["gz"], t + 1)
                    dve.tensor_tensor(o[:, :, :], o[:, :, :], bc(or4[:, :], P), ALU.mult).then_inc(R["normed"], 1)
                    dve.wait_ge(R["normed"], t + 1)
                    dve.tensor_tensor(o[:, :, :], o[:, :, :], gz[:, :, :], ALU.mult).then_inc(R["og"], 1)
                if inverse:
                    subtract(4)

            dve.memset(St[:, :, :], 0.0).then_inc(s0, 1)
            dve.wait_ge(ea, 1)
            steps_of(dve, step)


def keys(nc, io, keep, scr, kT, V, sample):
    G = 4
    tag = "ks" if sample else "kp"
    with ExitStack() as ctx:
        sb, ps, sem = stage(nc, ctx)
        wk = sb(f"{tag}_w", [P, 2, HB * P])
        ck = sb(f"{tag}_ck", [P, 2, G, KL])
        kr = sb(f"{tag}_kr", [P, 2, G, HQ])
        cT = sb(f"{tag}_cT", [P, 2, 4 * P])
        bT = [ps(f"{tag}_t{i}") for i in range(3)]
        bK = [ps(f"{tag}_k{i}") for i in range(4)]
        w_in = sem(f"{tag}_w_in")
        in_ = [sem(f"{tag}_in0"), sem(f"{tag}_in1")]
        tr, tr_out, kr_out = sem(f"{tag}_tr"), sem(f"{tag}_tr_out"), sem(f"{tag}_kr_out")
        mmk, k_a, k_v, zeroed = sem(f"{tag}_mm"), sem(f"{tag}_k_a"), sem(f"{tag}_k_v"), sem(f"{tag}_zero")
        block = ctx.enter_context(nc.Block())
        if sample:
            ckd = io["cache_ckv"][0, 0].rearrange("(g j p) c -> g p j c", p=P, j=G)
            krd = io["cache_kr"][0, 0].rearrange("(g j p) c -> g p j c", p=P, j=G)
        else:
            ckd = io["p_ckv"][0, 0].rearrange("(g j p) c -> g p j c", p=P, j=G)
            krd = io["p_kr"][0, 0].rearrange("(g j p) c -> g p j c", p=P, j=G)

        @block.sync
        def _(sp):
            sp.dma_start(wk[:, :, :], io["w_ukv"][0].rearrange("(k p) n -> p k n", p=P)).then_inc(w_in, 16)
            sp.wait_ge(zeroed, 1)
            for g in range(4):
                p = g % 2
                if g >= 2:
                    sp.wait_ge(tr, g - 1)
                sp.dma_start(ck[:, p, :, :], ckd[g]).then_inc(in_[p], 16)
                sp.dma_start(kr[:, p, :, NOPE:HQ], krd[g]).then_inc(in_[p], 16)
            if sample:
                sp.wait_ge(tr, 3)
                sp.dma_start(ck[0:DEC, 0, 0, :], io["s_ckv"][0, 0]).then_inc(in_[0], 16)
                sp.dma_start(kr[0:DEC, 0, 0, NOPE:HQ], io["s_kr"][0, 0]).then_inc(in_[0], 16)

        N = 5 if sample else 4

        def parts(g):
            return (1, DEC) if g == 4 else (G, P)

        @block.tensor
        def _(pe):
            pe.wait_ge(w_in, 16)
            n = 0
            for g in range(N):
                p = g % 2
                tiles, rows = parts(g)
                width = (tiles - 1) * P + rows
                pe.wait_ge(in_[p], (g // 2 + 1) * 32)
                if g:
                    pe.wait_ge(tr_out, g)
                    pe.wait_ge(kr_out, g)
                for j in range(tiles):
                    for k in range(2):
                        pe.transpose(bT[k][:, j * P:j * P + rows], ck[0:rows, p, j, k * P:(k + 1) * P], keep["ident"][0:rows, 0:rows])
                    mm = pe.transpose(bT[2][0:HQ, j * P:j * P + rows], kr[0:rows, p, j, :], keep["ident"][0:rows, 0:rows])
                mm.then_inc(tr, 1)
                pe.wait_ge(tr_out, g + 1)
                for m in range(HB + tiles):
                    b = bK[n % 4]
                    if n >= 4:
                        if n % 2:
                            pe.wait_ge(k_v, (n - 4) // 2 + 1)
                        else:
                            pe.wait_ge(k_a, (n - 4) // 2 + 1)
                    for k in range(2):
                        if m < HB:
                            mm = pe.matmul(b[0:NOPE, 0:width], wk[:, k, m * P:m * P + NOPE], cT[:, k, 0:width], start=k == 0, stop=k == 1)
                        else:
                            j = m - HB
                            mm = pe.matmul(b[0:rows, :].rearrange("p (h e) -> p h e", h=HB), cT[:, k, j * P:j * P + rows],
                                           wk[:, k, :].rearrange("p (h e) -> p h e", h=HB)[:, :, NOPE:P], start=k == 0, stop=k == 1)
                    mm.then_inc(mmk, 1)
                    n += 1

        def drain(eng, copy, odd, done):
            def f(g, n):
                tiles, rows = parts(g)
                width = (tiles - 1) * P + rows
                for m in range(HB + tiles):
                    if n % 2 == odd:
                        eng.wait_ge(mmk, n + 1)
                        b = bK[n % 4]
                        if m < HB:
                            copy(kT[0:NOPE, m, g * G * P:g * G * P + width], b[0:NOPE, 0:width]).then_inc(done, 1)
                        else:
                            copy(V[0:rows, g * G + m - HB, :, 0:DV],
                                 b[0:rows, :].rearrange("p (h e) -> p h e", h=HB)).then_inc(done, 1)
                    n += 1
                return n
            return f

        @block.scalar
        def _(act):
            f, n = drain(act, act.copy, 0, k_a), 0
            for g in range(N):
                tiles, rows = parts(g)
                width = (tiles - 1) * P + rows
                act.wait_ge(tr, g + 1)
                if g:
                    act.wait_ge(mmk, n)
                act.copy(cT[:, 0, 0:width], bT[0][:, 0:width])
                act.copy(cT[:, 1, 0:width], bT[1][:, 0:width]).then_inc(tr_out, 1)
                n = f(g, n)

        @block.vector
        def _(dve):
            dve.memset(kr[:, :, :, 0:NOPE], 0.0).then_inc(zeroed, 1)
            dve.memset(V[:, :, :, DV:DV + 1], 1.0)
            f, n = drain(dve, dve.tensor_copy, 1, k_v), 0
            for g in range(N):
                tiles, rows = parts(g)
                width = (tiles - 1) * P + rows
                dve.wait_ge(tr, g + 1)
                dve.tensor_copy(kT[NOPE:HQ, :, g * G * P:g * G * P + width],
                                bT[2][NOPE:HQ, 0:width].unsqueeze(1).to_broadcast([ROPE, HB, width])).then_inc(kr_out, 1)
                n = f(g, n)


def attention(nc, io, keep, scr, kT, V, sample):
    tag = "s" if sample else "q"
    tiles = [SAMPLE] if sample else list(range(NT))
    with ExitStack() as ctx:
        sb, ps, sem0 = stage(nc, ctx)
        sem = lambda n: sem0(f"{tag}_{n}")
        wu = sb(f"{tag}_wu", [P, 3, HB * HQ])
        cq = sb(f"{tag}_cq", [P, 2, QL])
        cs = sb(f"{tag}_cs", [P, 2, 64])
        zb = sb(f"{tag}_zb", [P, 2, HB * DV])
        cqT = sb(f"{tag}_cqT", [P, 3, P])
        qb = sb(f"{tag}_qb", [P, HB, HQ])
        rt = sb(f"{tag}_rt", [P, 2, HB, ROPE])
        qT = sb(f"{tag}_qT", [P, HB, P])
        qc = sb(f"{tag}_qc", [P, 2, P])
        Pr = sb(f"{tag}_P", [P, 2, 17 * P])
        mx = sb(f"{tag}_mx", [P, 2, 8])
        PT = sb(f"{tag}_PT", [P, 2, 512])
        rc = sb(f"{tag}_rc", [P, 1])
        ob = sb(f"{tag}_ob", [P, HB * DV])
        obT = sb(f"{tag}_obT", [P, 2, 512])
        sps = ps(f"{tag}_sps", [P, 5, 512])
        tps = [ps(f"{tag}_t0"), ps(f"{tag}_t1")]
        ops = ps(f"{tag}_o")
        w_in = sem("w_in")
        in_, stored = [sem("in0"), sem("in1")], [sem("st0"), sem("st1")]
        cqt, cqt_out, qps, qb_out, roped, qbt, qT_out, zero = (sem(n) for n in ("cqt", "cqt_out", "qps", "qb_out", "roped", "qbt", "qT_out", "zero"))
        qc_r, sc_r, mx_r, exp_r, tr_r, pt_a, pt_v, pv_r, o_r, obt, obt_out, parts, inv, init = (
            sem(n) for n in ("qc", "scores", "max", "exp", "tr", "pt_a", "pt_v", "pv", "o", "obt", "obt_out", "parts", "inv", "init"))
        block = ctx.enter_context(nc.Block())
        scale = float(HQ) ** -0.5
        flat = sps[:, :, :].rearrange("p a b -> p (a b)")

        class Size:

            def __init__(self, t, m, prev):
                self.n = PAST + DEC if sample else (t + 1) * P
                self.own = 0 if sample else CH
                self.kt = -(-self.n // P)
                self.nb = -(-self.n // 512)
                self.ng = -(-self.kt // 4)
                self.na, self.nv = (self.ng + 1) // 2, self.ng // 2
                self.q0 = m * HB
                self.sc0 = prev.sc0 + HB * prev.nb if prev else 0
                self.tr0 = prev.tr0 + HB * prev.ng if prev else 0
                self.a0 = prev.a0 + HB * prev.na if prev else 0
                self.v0 = prev.v0 + HB * prev.nv if prev else 0

            def bank(self, b):
                return 512 * b, min(self.n, 512 * (b + 1))

        sizes = []
        for m, t in enumerate(tiles):
            sizes.append(Size(t, m, sizes[-1] if sizes else None))

        def heads(eng, body):
            with eng.Fori(0, HB // 2 - 1) as i:
                body(i * 2, 0, True)
                body(i * 2 + 1, 1, True)
            body(HB - 2, 0, True)
            body(HB - 1, 1, False)

        @block.sync
        def _(sp):
            sp.dma_start(wu[:, :, :], io["w_uq"][0].rearrange("(k p) n -> p k n", p=P)).then_inc(w_in, 16)

            def load(m):
                if m >= 2:
                    sp.wait_ge(obt, m - 1)
                sp.dma_start(cq[:, m % 2, :], scr["cq"][tiles[m]]).then_inc(in_[m % 2], 16)
                sp.dma_start(cs[:, m % 2, :], io["c_rope"][tiles[m]]).then_inc(in_[m % 2], 16)
                sp.dma_start(zb[:, m % 2, :], scr["z"][tiles[m], :, 512:1024]).then_inc(in_[m % 2], 16)

            load(0)
            for m, t in enumerate(tiles):
                if m + 1 < len(tiles):
                    load(m + 1)
                sp.wait_ge(obt_out, m + 1)
                sp.dma_start(scr["ob"][t], obT[:, m % 2, :]).then_inc(stored[m % 2], 16)
            for p in range(min(2, len(tiles))):
                sp.wait_ge(stored[p], (len(tiles) + 1 - p) // 2 * 16)

        @block.gpsimd
        def _(pool):
            for m, z in enumerate(sizes):
                if z.own:
                    if m:
                        pool.wait_ge(pv_r, z.q0)
                    for p in range(2):
                        u = pool.memset(Pr[0:CH, p, z.n - z.own:z.n], 0.0)
                    u.then_inc(zero, 1)
                elif z.n < z.kt * P:
                    for p in range(2):
                        u = pool.memset(Pr[:, p, z.n:z.kt * P], 0.0)
                    u.then_inc(zero, 1)
                pool.wait_ge(qT_out, m + 1)
                with pool.Fori(0, HB // 2) as i:
                    for p in range(2):
                        pool.wait_ge(sc_r, i * (2 * z.nb) + z.sc0)
                        pool.tensor_copy(qc[0:HQ, p, :], qT[0:HQ, i * 2 + p, :]).then_inc(qc_r, 1)

        @block.tensor
        def _(pe):
            pe.wait_ge(w_in, 16)
            ident = keep["ident"]
            for m, z in enumerate(sizes):
                pe.wait_ge(in_[m % 2], (m // 2 + 1) * 48)
                if m:
                    pe.wait_ge(obt_out, m)
                for k in range(3):
                    mm = pe.transpose(tps[0][:, k * P:(k + 1) * P], cq[:, m % 2, k * P:(k + 1) * P], ident[:, :])
                mm.then_inc(cqt, 1)
                pe.wait_ge(cqt_out, m + 1)
                for b in range(2):
                    for k in range(3):
                        mm = pe.matmul(tps[b][:, 0:384], cqT[:, k, :], wu[:, k, b * 384:(b + 1) * 384], start=k == 0, stop=k == 2)
                mm.then_inc(qps, 1)
                pe.wait_ge(roped, m + 1)
                for h in range(HB):
                    mm = pe.transpose(tps[h // 4][0:HQ, h % 4 * P:(h % 4 + 1) * P], qb[:, h, :], ident[:, :])
                mm.then_inc(qbt, 1)
                pe.wait_ge(qT_out, m + 1)

                def scores(h, p):
                    pe.wait_ge(qc_r, h + (z.q0 + 1))
                    for b in range(z.nb):
                        lo, hi = z.bank(b)
                        if isinstance(h, int) and h == 0:
                            pe.wait_ge(exp_r, z.sc0)
                        else:
                            pe.wait_ge(exp_r, h * z.nb + (z.sc0 + b + 1 - z.nb))
                        pe.matmul(sps[:, b, 0:hi - lo], qc[0:HQ, p, :], kT[0:HQ, h, lo:hi],
                                  start=True, stop=True).then_inc(sc_r, 1)

                def transposes(h, p, b):
                    n = (h * z.na if b % 2 == 0 else h * z.nv) + ((z.a0 if b % 2 == 0 else z.v0) + b // 2)
                    pe.wait_ge(pt_a if b % 2 == 0 else pt_v, n)
                    for j in range(4 * b, min(4 * b + 4, z.kt)):
                        mm = pe.transpose(tps[b % 2][:, (j % 4) * P:(j % 4 + 1) * P], Pr[:, p, j * P:(j + 1) * P], ident[:, :])
                    mm.then_inc(tr_r, 1)

                def product(h, b):
                    n = (h * z.na if b % 2 == 0 else h * z.nv) + ((z.a0 if b % 2 == 0 else z.v0) + b // 2 + 1)
                    pe.wait_ge(pt_a if b % 2 == 0 else pt_v, n)
                    if b == 0:
                        pe.wait_ge(o_r, h + z.q0)
                    for j in range(4 * b, min(4 * b + 4, z.kt)):
                        rows = min(P, z.n - j * P)
                        mm = pe.matmul(ops[:, 0:DV + 1], PT[0:rows, b % 2, (j % 4) * P:(j % 4 + 1) * P], V[0:rows, j, h, :],
                                       start=j == 0, stop=j == z.kt - 1)
                    if b == z.ng - 1:
                        mm.then_inc(pv_r, 1)

                def body(h, p, more):
                    if more:
                        scores(h + 1, 1 - p)
                    pe.wait_ge(exp_r, (h + 1) * z.nb + z.sc0)
                    transposes(h, p, 0)
                    for b in range(1, z.ng):
                        transposes(h, p, b)
                        product(h, b - 1)
                    product(h, z.ng - 1)

                scores(0, 0)
                heads(pe, body)
                pe.wait_ge(o_r, z.q0 + HB)
                for k in range(4):
                    mm = pe.transpose(tps[0][:, k * P:(k + 1) * P], ob[:, k * P:(k + 1) * P], ident[:, :])
                mm.then_inc(obt, 1)

        @block.scalar
        def _(act):
            for m, z in enumerate(sizes):
                act.wait_ge(cqt, m + 1)
                act.copy(cqT[:, :, :], tps[0][:, 0:384].rearrange("p (k t) -> p k t", k=3)).then_inc(cqt_out, 1)
                act.wait_ge(qps, m + 1)
                for b in range(2):
                    a = act.mul(qb[:, 4 * b:4 * b + 4, :], tps[b][:, 0:384].rearrange("p (h c) -> p h c", h=4), scale)
                a.then_inc(qb_out, 1)
                act.wait_ge(qbt, m + 1)
                for b in range(2):
                    a = act.copy(qT[0:HQ, 4 * b:4 * b + 4, :], tps[b][0:HQ, :].rearrange("p (h t) -> p h t", h=4))
                a.then_inc(qT_out, 1)

                def exps(h, p):
                    act.wait_ge(mx_r, h + (z.q0 + 1))
                    for b in range(z.nb):
                        lo, hi = z.bank(b)
                        own = z.own if b == z.nb - 1 else 0
                        a = act.activation(Pr[:, p, lo:hi - own], flat[:, lo:hi - own], ACT.Exp, bias=mx[:, p, 7:8])
                        if own:
                            a = act.activation(Pr[CH:P, p, hi - own:hi], flat[CH:P, hi - own:hi], ACT.Exp, bias=mx[CH:P, p, 7:8])
                        a.then_inc(exp_r, 1)

                def body(h, p, more):
                    for b in range(0, z.ng, 2):
                        act.wait_ge(tr_r, h * z.ng + (z.tr0 + b + 1))
                        w = min(4, z.kt - 4 * b) * P
                        act.copy(PT[:, 0, 0:w], tps[0][:, 0:w]).then_inc(pt_a, 1)
                    if more:
                        exps(h + 1, 1 - p)

                act.wait_ge(zero, m + 1)
                exps(0, 0)
                heads(act, body)
                act.wait_ge(obt, m + 1)
                if m >= 2:
                    act.wait_ge(stored[m % 2], m // 2 * 16)
                act.copy(obT[:, m % 2, :], tps[0][:, :]).then_inc(obt_out, 1)

        @block.vector
        def _(dve):
            dve.memset(mx[:, :, 0:1], -3.0e38).then_inc(init, 1)
            dve.wait_ge(init, 1)
            for m, z in enumerate(sizes):
                dve.wait_ge(qb_out, m + 1)
                dve.wait_ge(in_[m % 2], (m // 2 + 1) * 48)
                ck = over_heads(cs[:, m % 2, 0:32], HB)
                dve.tensor_tensor(rt[:, 0, :, :], qb[:, :, NOPE:HQ], ck, ALU.mult)
                dve.tensor_tensor(rt[:, 1, :, 0:16], qb[:, :, NOPE + 16:HQ], over_heads(cs[:, m % 2, 32:48], HB), ALU.mult)
                dve.tensor_tensor(rt[:, 1, :, 16:32], qb[:, :, NOPE:NOPE + 16], over_heads(cs[:, m % 2, 48:64], HB), ALU.mult).then_inc(init, 1)
                dve.wait_ge(init, m + 2)
                dve.tensor_tensor(qb[:, :, NOPE:HQ], rt[:, 0, :, :], rt[:, 1, :, :], ALU.add).then_inc(roped, 1)

                def maxima(h, p):
                    for b in range(z.nb):
                        lo, hi = z.bank(b)
                        own = z.own if b == z.nb - 1 else 0
                        dve.wait_ge(sc_r, h * z.nb + (z.sc0 + b + 1))
                        u = dve.tensor_reduce(mx[:, p, 1 + b:2 + b], flat[:, lo:hi - own], AX, ALU.max)
                        if own:
                            u = dve.tensor_reduce(mx[CH:P, p, 0:1], flat[CH:P, hi - own:hi], AX, ALU.max)
                    u.then_inc(parts, 1)
                    dve.wait_ge(parts, h + (z.q0 + 1))
                    dve.tensor_reduce(mx[:, p, 7:8], mx[:, p, 0:1 + z.nb], AX, ALU.max, negate=True).then_inc(mx_r, 1)

                def body(h, p, more):
                    if more:
                        maxima(h + 1, 1 - p)
                    for b in range(1, z.ng, 2):
                        dve.wait_ge(tr_r, h * z.ng + (z.tr0 + b + 1))
                        w = min(4, z.kt - 4 * b) * P
                        dve.tensor_copy(PT[:, 1, 0:w], tps[1][:, 0:w]).then_inc(pt_v, 1)
                    dve.wait_ge(pv_r, h + (z.q0 + 1))
                    dve.reciprocal(rc[:, :], ops[:, DV:DV + 1]).then_inc(inv, 1)
                    dve.wait_ge(inv, h + (z.q0 + 1))
                    dve.scalar_tensor_tensor(out=ob[:, :].rearrange("p (h e) -> p h e", h=HB)[:, h, :], in0=ops[:, 0:DV], scalar=rc[:, 0:1],
                                             in1=zb[:, m % 2, :].rearrange("p (h e) -> p h e", h=HB)[:, h, :],
                                             op0=ALU.mult, op1=ALU.mult).then_inc(o_r, 1)

                if m:
                    dve.wait_ge(obt, m)
                maxima(0, 0)
                heads(dve, body)


def gate_rows(nc, keep, layer, sb, sem, banks, gB, tag):
    dg = sb(f"{tag}_dg", [P, 2 * KD, P])
    diag, rows, got = sem(f"{tag}_diag"), sem(f"{tag}_rows"), sem(f"{tag}_got")

    def dve_part(dve):
        for n in range(2 * KD):
            c, k = n // KD, n % KD
            u = dve.tensor_scalar(dg[:, n, :], keep["ident"][:, :], keep["gg"][:, layer, c, k:k + 1], None, ALU.mult)
        u.then_inc(diag, 1)
        dve.wait_ge(rows, 1)
        for c in range(2):
            for j in range(2):
                u = dve.tensor_copy(gB[:, c, j * 512:(j + 1) * 512], banks[2 * c + j][:, :])
        u.then_inc(got, 1)
        dve.wait_ge(got, 1)

    def pe_part(pe):
        pe.wait_ge(diag, 1)
        for c in range(2):
            for j in range(2):
                mm = pe.matmul(banks[2 * c + j][:, :], keep["ones"][:, :], dg[:, c * KD + 4 * j:c * KD + 4 * j + 4, :],
                               start=True, stop=True)
        mm.then_inc(rows, 1)
        pe.wait_ge(got, 1)

    return dve_part, pe_part


def close_even(nc, io, keep, scr):
    with ExitStack() as ctx:
        sb, ps, sem = stage(nc, ctx)
        w = sb("c_w", [P, KD, D])
        oc = sb("c_oc", [P, 2, KD, P])
        xt = sb("c_xt", [P, 2, D])
        y = sb("c_y", [P, 2, D])
        junk = sb("c_junk", [P, D])
        gB = sb("c_gB", [P, 2, D])
        ms, rs = sb("c_ms", [P, 1]), sb("c_rs", [P, 1])
        bank = [ps(f"c_b{i}") for i in range(4)]
        w_in, mm_r, y_r, ms_r, rs_r, yn, out = (sem("c_" + n) for n in ("w_in", "mm", "y", "ms", "rs", "yn", "out"))
        in_, stored = [sem("c_in0"), sem("c_in1")], [sem("c_st0"), sem("c_st1")]
        dve_rows, pe_rows = gate_rows(nc, keep, 0, sb, sem, bank, gB, "c")
        block = ctx.enter_context(nc.Block())

        @block.sync
        def _(sp):
            def load(t, p):
                sp.dma_start(oc[:, p, 0:4, :], scr["oa"][t].rearrange("p (k t) -> p k t", k=4)).then_inc(in_[p], 16)
                sp.dma_start(oc[:, p, 4:8, :], scr["ob"][t].rearrange("p (k t) -> p k t", k=4)).then_inc(in_[p], 16)
                if last(t):
                    sp.dma_start(xt[0:DEC, p, :], io["x_sample"][0]).then_inc(in_[p], 16)
                else:
                    sp.dma_start(xt[:, p, :], io["x_prompt"][0].rearrange("(t p) d -> t p d", p=P)[t]).then_inc(in_[p], 16)

            load(0, 0)
            sp.dma_start(w[:, :, :], io["w_out_e"][0].rearrange("(k p) n -> p k n", p=P)).then_inc(w_in, 16)

            def step(t, p, i):
                if not last(t):
                    sp.wait_ge(out, t)
                    load(t + 1, 1 - p)
                sp.wait_ge(out, t + 1)
                sp.dma_start(scr["x1"][t], y[:, p, :]).then_inc(stored[p], 16)

            tiles_of(sp, step)
            sp.wait_ge(stored[0], (TILES + 1) // 2 * 16)
            sp.wait_ge(stored[1], TILES // 2 * 16)

        @block.gpsimd
        def _(pool):
            def step(t, p, i):
                pool.wait_ge(ms_r, t + 1)
                pool.tensor_tensor(rs[:, :], ms[:, :], keep["mhalf"][:, 0:1], ALU.pow).then_inc(rs_r, 1)
            tiles_of(pool, step)

        @block.scalar
        def _(act):
            def step(t, p, i):
                act.wait_ge(mm_r, t + 1)
                act.wait_ge(stored[p], i * 16)
                act.copy(y[:, p, 0:512], bank[2 * p][:, :])
                act.copy(y[:, p, 512:D], bank[2 * p + 1][:, :]).then_inc(y_r, 1)
            tiles_of(act, step)

        @block.tensor
        def _(pe):
            pe_rows(pe)
            pe.wait_ge(w_in, 16)

            def step(t, p, i):
                pe.wait_ge(in_[p], (i + 1) * 48)
                if p or isinstance(t, int):
                    pe.wait_ge(y_r, t - 1)
                else:
                    pe.wait_ge(y_r, t)
                for j in range(2):
                    for k in range(KD):
                        mm = pe.matmul(bank[2 * p + j][:, :], oc[:, p, k, :], w[:, k, j * 512:(j + 1) * 512], start=k == 0, stop=k == KD - 1)
                mm.then_inc(mm_r, 1)
            tiles_of(pe, step)

        @block.vector
        def _(dve):
            dve_rows(dve)

            def step(t, p, i):
                dve.wait_ge(y_r, t + 1)
                dve.tensor_tensor_reduce(junk[:, :], y[:, p, :], y[:, p, :], 1.0 / D, EPS, ALU.mult, ALU.add, ms[:, :]).then_inc(ms_r, 1)
                dve.wait_ge(rs_r, t + 1)
                dve.wait_ge(in_[p], (i + 1) * 48)
                dve.scalar_tensor_tensor(out=y[:, p, :], in0=y[:, p, :], scalar=rs[:, 0:1], in1=gB[:, cond(t), :],
                                         op0=ALU.mult, op1=ALU.mult).then_inc(yn, 1)
                dve.wait_ge(yn, t + 1)
                dve.tensor_tensor(y[:, p, :], y[:, p, :], xt[:, p, :], ALU.add).then_inc(out, 1)
            tiles_of(dve, step)


def in_odd(nc, io, keep, scr):
    with ExitStack() as ctx:
        sb, ps, sem = stage(nc, ctx)
        w = sb("e_w", [P, KD, IN_O])
        xt = sb("e_xt", [P, 2, D])
        xn = sb("e_xn", [P, D])
        hT = sb("e_hT", [P, 2, KD, P])
        r = sb("e_r", [P, 5, D])
        fg = sb("e_fg", [P, HC, P])
        sg = sb("e_sg", [P, HC, P])
        reset = sb("e_reset", [P, HC, P])
        ms, rs = sb("e_ms", [P, 1]), sb("e_rs", [P, 1])
        xps = [ps("e_x0"), ps("e_x1")]
        bank = [ps(f"e_p{i}") for i in range(4)]
        S = norm_sems(sem, "e")
        w_in, proj, a_out, v_out, fg_r, k_r, lf_r, G_r, init = (
            sem("e_" + n) for n in ("w_in", "proj", "a_out", "v_out", "fg", "k", "lf", "G", "init"))
        st = [sem(f"e_st{j}") for j in range(5)]
        dve_norm, pool_norm, pe_tr, act_hT, dve_hT = norm_transpose(1, keep, xt, xn, ms, rs, hT, xps, S)
        block = ctx.enter_context(nc.Block())
        flat = lambda b: b.rearrange("p h t -> p (h t)")
        part = lambda j, m: r[:, j, m * 512:(m + 1) * 512]

        @block.sync
        def _(sp):
            def load(t, p):
                sp.dma_start(xt[:, p, :], scr["x1"][t]).then_inc(S["x_in"][p], 16)

            load(0, 0)
            for k in range(KD):
                sp.dma_start(w[:, k, :], io["w_in_o"][0, k * P:(k + 1) * P, :]).then_inc(w_in, 16)

            def step(t, p, i):
                if not last(t):
                    sp.wait_ge(S["xn"], t)
                    load(t + 1, 1 - p)
                sp.wait_ge(a_out, t * 6 + 2)
                sp.dma_start(scr["qkg"][t, :, 0:D], r[:, 0, :]).then_inc(st[0], 16)
                sp.wait_ge(k_r, t + 1)
                sp.dma_start(scr["qkg"][t, :, D:2 * D], r[:, 1, :]).then_inc(st[1], 16)
                sp.wait_ge(v_out, t * 2 + 2)
                sp.dma_start(scr["iz"][t, :, 0:D], r[:, 3, :]).then_inc(st[3], 16)
                sp.wait_ge(G_r, t + 1)
                sp.dma_start(scr["qkg"][t, :, 2 * D:3 * D], r[:, 2, :]).then_inc(st[2], 16)
                sp.wait_ge(a_out, t * 6 + 6)
                sp.dma_start(scr["iz"][t, :, D:2 * D], r[:, 4, :]).then_inc(st[4], 16)

            tiles_of(sp, step)
            for j in range(5):
                sp.wait_ge(st[j], TILES * 16)

        @block.gpsimd
        def _(pool):
            def step(t, p, i):
                if not last(t):
                    pool_norm(pool, t + 1)
            pool_norm(pool, 0)
            tiles_of(pool, step)

        @block.scalar
        def _(act):
            def drain(t, n, dst, func):
                act.wait_ge(proj, t * 8 + n + 1)
                act.activation(dst, bank[n % 4][:, :], func).then_inc(a_out, 1)

            def step(t, p, i):
                act.wait_ge(st[0], t * 16)
                drain(t, 0, part(0, 0), ACT.Silu)
                drain(t, 1, part(0, 1), ACT.Silu)
                act.wait_ge(fg_r, t)
                drain(t, 2, flat(sg[:, 0:4, :]), ACT.Sigmoid)
                drain(t, 3, flat(sg[:, 4:8, :]), ACT.Sigmoid)
                if not last(t):
                    act_hT(act, t + 1, 1 - p)
                act.wait_ge(k_r, t + 1)
                act.activation(flat(fg[:, :, :]), flat(fg[:, :, :]), ACT.Ln).then_inc(lf_r, 1)
                act.wait_ge(st[4], t * 16)
                drain(t, 6, part(4, 0), ACT.Silu)
                drain(t, 7, part(4, 1), ACT.Silu)

            act_hT(act, 0, 0)
            tiles_of(act, step)

        @block.tensor
        def _(pe):
            def step(t, p, i):
                pe.wait_ge(S["hT_a"], t + 1)
                pe.wait_ge(S["hT_v"], t + 1)
                for n in range(8):
                    if n in (0, 1):
                        pe.wait_ge(v_out, t * 2)
                    elif n in (2, 3):
                        pe.wait_ge(a_out, t * 6)
                    else:
                        pe.wait_ge(a_out, t * 6 + (n - 3))
                    for c in range(4):
                        for k in range(KD):
                            if n < 4:
                                a = n * 512 + c * P
                                mm = pe.matmul(bank[n % 4][:, c * P:(c + 1) * P], w[:, k, a:a + P], hT[:, p, k, :], start=k == 0, stop=k == KD - 1)
                            elif c == 0:
                                mm = pe.matmul(bank[n % 4][:, :], hT[:, p, k, :], w[:, k, n * 512:(n + 1) * 512], start=k == 0, stop=k == KD - 1)
                    mm.then_inc(proj, 1)
                    if n == 3 and not last(t):
                        pe_tr(pe, t + 1)

            pe_tr(pe, 0)
            pe.wait_ge(w_in, 16 * KD)
            tiles_of(pe, step)

        @block.vector
        def _(dve):
            def step(t, p, i):
                if not last(t):
                    dve_norm(dve, t + 1, 1 - p, i + p)
                dve.wait_ge(a_out, t * 6 + 4)
                dve.wait_ge(G_r, t)
                for h in range(HC):
                    u = dve.tensor_scalar(fg[:, h, :], sg[:, h, :], keep["lb"][:, 1, h:h + 1], keep["lb"][:, 0, h:h + 1], ALU.mult, ALU.add)
                u.then_inc(fg_r, 1)
                dve.wait_ge(fg_r, t + 1)
                dve.wait_ge(st[1], t * 16)
                dve.tensor_scalar(r[:, 1, :], flat(fg[:, :, :]), -1.0, 1.0, ALU.mult, ALU.add).then_inc(k_r, 1)
                if not last(t):
                    dve_hT(dve, t + 1, 1 - p)
                dve.wait_ge(st[3], t * 16)
                for n in (4, 5):
                    dve.wait_ge(proj, t * 8 + n + 1)
                    dve.tensor_copy(part(3, n - 4), bank[n % 4][:, :]).then_inc(v_out, 1)
                dve.wait_ge(lf_r, t + 1)
                dve.wait_ge(st[2], t * 16)
                dve.tensor_tensor_scan(r[:, 2, :], flat(reset[:, :, :]), flat(fg[:, :, :]), 0.0, ALU.mult, ALU.add).then_inc(G_r, 1)

            dve.memset(reset[:, :, :], 1.0).then_inc(init, 1)
            dve.wait_ge(init, 1)
            dve.memset(reset[:, :, :].rearrange("p h (c t) -> p (h c) t", t=CH)[:, :, 0:1], 0.0).then_inc(init, 1)
            dve.wait_ge(init, 2)
            dve_norm(dve, 0, 0, 0)
            dve_hT(dve, 0, 0)
            tiles_of(dve, step)


def hgrn(nc, io, keep, scr):
    H = HC
    with ExitStack() as ctx:
        sb, ps, sem = stage(nc, ctx)
        w = sb("h_w", [P, KD, D])
        rq = sb("h_rq", [P, 2, 3, H, P])
        rz = sb("h_rz", [P, 2, 2, H, P])
        gB = sb("h_gB", [P, 2, D])
        gnc = sb("h_gnc", [P, P])
        EG = sb("h_EG", [P, 2, H, P])
        DL, EL = sb("h_DL", [P, 2, 512]), sb("h_EL", [P, 2, 2, 512])
        KLv, QLv = sb("h_KL", [P, 2, H, P]), sb("h_QL", [P, 2, 512])
        A = sb("h_A", [P, 2, H, P])
        kdT, kd, qe = sb("h_kdT", [P, H, P]), sb("h_kd", [P, 2, H, P]), sb("h_qe", [P, 2, H, P])
        St = sb("h_S", [P, H, P])
        o, osq = sb("h_o", [P, H, P]), sb("h_osq", [P, H, P])
        os8, or8 = sb("h_os8", [P, 8]), sb("h_or8", [P, 8])
        oT = sb("h_oT", [P, H, P])
        xt, y = sb("h_xt", [P, D]), sb("h_y", [P, D])
        ms, rs, hold = sb("h_ms", [P, 1]), sb("h_rs", [P, 1]), sb("h_hold", [P, 6])
        bank = [ps(f"h_b{i}") for i in range(8)]
        names = "EG fin tail kd kdt kd_out dq dg qe o_ps o_out gate on sum os or normed og ogt oT_out mm y ms rs yn out".split()
        R = {n: sem("h_" + n) for n in names}
        dls, els, kqs, scs, Ac = (sem("h_" + n) for n in ("dl", "el", "kq", "sc", "Ac"))
        Ss, kSs, qSs = sem("h_Ss"), sem("h_kSs"), sem("h_qSs")
        q_in, z_in = [sem("h_q_in0"), sem("h_q_in1")], [sem("h_z_in0"), sem("h_z_in1")]
        x_in, stored = sem("h_x_in"), sem("h_stored")
        const_in, state_out, state_in, init = sem("h_const"), sem("h_so"), sem("h_si"), sem("h_init")
        dve_rows, pe_rows = gate_rows(nc, keep, 1, sb, sem, bank, gB, "h")
        block = ctx.enter_context(nc.Block())
        flat = lambda b: b.rearrange("p h t -> p (h t)")
        heads4 = lambda b: b[:, :].rearrange("p (h t) -> p h t", h=4)
        state = lambda ap: ap.rearrange("h d e -> d h e")

        def halves(ap, b):
            return ap.rearrange("p h (n a b) -> p (h n) a b", a=2, b=b)

        @block.sync
        def _(sp):
            sp.dma_start(gnc[:, :], io["g_norm_c"][0:1, :].to_broadcast([P, P])).then_inc(const_in, 16)

            def load_q(t, p, ahead=0):
                sp.dma_start(rq[:, p, :, :, :], scr["qkg"][ahead:][t].rearrange("p (j h t) -> p j h t", j=3, h=H)).then_inc(q_in[p], 16)

            def load_z(t, p, ahead=0):
                sp.dma_start(rz[:, p, :, :, :], scr["iz"][ahead:][t].rearrange("p (j h t) -> p j h t", j=2, h=H)).then_inc(z_in[p], 16)

            def store_y(t):
                sp.wait_ge(R["out"], t + 1)
                if last(t):
                    sp.dma_start(io["y_sample"][0], y[0:DEC, :]).then_inc(stored, 16)
                else:
                    sp.dma_start(io["y_prompt"][0].rearrange("(t p) d -> t p d", p=P)[t], y[:, :]).then_inc(stored, 16)

            load_q(0, 0)
            load_z(0, 0)
            load_q(1, 1)
            sp.dma_start(w[:, :, :], io["w_out_o"][0].rearrange("(k p) n -> p k n", p=P)).then_inc(const_in, 16)

            def step(t, p, i, first=False):
                if not (isinstance(t, int) and t + 2 > SAMPLE):
                    sp.wait_ge(R["qe"], t + 1)
                    sp.wait_ge(Ac, t * 6 + 6)
                    load_q(t, p, ahead=2)
                if not last(t):
                    sp.wait_ge(R["og"], t)
                    sp.wait_ge(R["o_ps"], t)
                    load_z(t, 1 - p, ahead=1)
                if isinstance(t, int) and t == NT - 1:
                    sp.wait_ge(Ss, 2 * NT)
                    sp.dma_start(state(io["p_hgrn"][0, 0]), St[:, :, :]).then_inc(state_out, 16)
                    sp.wait_ge(state_out, 16)
                    sp.wait_ge(R["o_ps"], NT)
                    sp.dma_start(St[:, :, :], state(io["state_hgrn"][0, 0])).then_inc(state_in, 16)
                if last(t):
                    sp.wait_ge(Ss, 2 * NT + 1)
                    sp.dma_start(state(io["s_hgrn"][0, 0]), St[:, :, :]).then_inc(state_out, 16)
                if not first:
                    store_y(t - 1)
                sp.dma_start(xt[:, :], scr["x1"][t]).then_inc(x_in, 16)

            after_first(sp, step)
            store_y(SAMPLE)
            sp.wait_ge(state_out, 32)
            sp.wait_ge(stored, TILES * 16)

        @block.gpsimd
        def _(pool):
            def inner(u, p, i):
                pool.wait_ge(R["EG"], u + 1)
                pool.tensor_tensor(qe[:, p, :, :], rq[:, p, 0, :, :], EG[:, p, :, :], ALU.mult).then_inc(R["qe"], 1)

            def close(t):
                pool.wait_ge(R["ms"], t + 1)
                pool.tensor_tensor(rs[:, :], ms[:, :], keep["mhalf"][:, 0:1], ALU.pow).then_inc(R["rs"], 1)

            def step(t, p, i, first=False):
                pool.wait_ge(z_in[p], (i + 1) * 16)
                pool.tensor_tensor(rz[:, p, 1, :, :], rz[:, p, 1, :, :], over_heads(gnc[:, :], H), ALU.mult).then_inc(R["gate"], 1)
                if not last(t):
                    pool.wait_ge(R["o_ps"], t)
                    inner(t + 1, 1 - p, i + p)
                if not first:
                    close(t - 1)
                pool.wait_ge(R["os"], t + 1)
                pool.tensor_tensor(or8[:, :], os8[:, :], keep["mhalf"][:, :], ALU.pow).then_inc(R["or"], 1)

            pool.wait_ge(const_in, 32)
            inner(0, 0, 0)
            after_first(pool, step)
            close(SAMPLE)

        @block.scalar
        def _(act):
            def decays(u, p, i):
                act.wait_ge(R["tail"], u + 1)
                act.activation(flat(kdT[:, :, :]), flat(kdT[:, :, :]), ACT.Exp).then_inc(R["fin"], 1)
                act.activation(flat(EG[:, p, :, :]), flat(rq[:, p, 2, :, :]), ACT.Exp).then_inc(R["EG"], 1)

            def level(u, n):
                act.wait_ge(dls, u * 6 + n + 1)
                act.activation(EL[:, n % 2, :, :], DL[:, :, :], ACT.Exp).then_inc(els, 1)

            def kd_rows(u, p):
                act.wait_ge(R["kdt"], u + 1)
                act.copy(flat(kd[:, p, 0:4, :]), bank[4][:, :])
                act.copy(flat(kd[:, p, 4:8, :]), bank[5][:, :]).then_inc(R["kd_out"], 1)

            def close(t):
                act.wait_ge(R["mm"], t + 1)
                act.wait_ge(stored, t * 16)
                act.copy(y[:, 0:512], bank[2][:, :])
                act.copy(y[:, 512:D], bank[3][:, :]).then_inc(R["y"], 1)

            def step(t, p, i, first=False):
                more = not last(t)
                if more:
                    act.wait_ge(Ss, t * 2)
                    decays(t + 1, 1 - p, i + p)
                if not first:
                    close(t - 1)
                if more:
                    level(t + 1, 0)
                    kd_rows(t + 1, 1 - p)
                    level(t + 1, 1)
                    level(t + 1, 2)
                act.wait_ge(R["o_ps"], t + 1)
                act.copy(flat(o[:, 0:4, :]), bank[6][:, :])
                act.copy(flat(o[:, 4:8, :]), bank[7][:, :]).then_inc(R["o_out"], 1)
                if more:
                    level(t + 1, 3)
                    level(t + 1, 4)
                act.wait_ge(R["ogt"], t + 1)
                act.copy(flat(oT[:, 0:4, :]), bank[2][:, :])
                act.copy(flat(oT[:, 4:8, :]), bank[3][:, :]).then_inc(R["oT_out"], 1)
                if more:
                    level(t + 1, 5)

            decays(0, 0, 0)
            level(0, 0)
            kd_rows(0, 0)
            for n in range(1, 6):
                level(0, n)
            after_first(act, step)
            close(SAMPLE)

        @block.tensor
        def _(pe):
            pe_rows(pe)
            pe.wait_ge(const_in, 32)
            pe.wait_ge(init, 1)
            ident = keep["ident"]

            def diagonal(u, p, i):
                pe.wait_ge(q_in[p], (i + 1) * 16)
                pe.wait_ge(R["kd_out"], u)
                for h in range(H):
                    mm = pe.matmul(bank[4 + h // 4][:, h % 4 * P:(h % 4 + 1) * P], rq[:, p, 1, h, :], rq[:, p, 0, h, :], start=True, stop=True)
                mm.then_inc(R["dq"], 1)

            def kd_transposes(u):
                pe.wait_ge(R["kd"], u + 1)
                pe.wait_ge(R["dg"], u + 1)
                for h in range(H):
                    mm = pe.transpose(bank[4 + h // 4][:, h % 4 * P:(h % 4 + 1) * P], kdT[:, h, :], ident[:, :])
                mm.then_inc(R["kdt"], 1)

            def level(u, n):
                pe.wait_ge(kqs, u * 6 + n + 1)
                if n >= 2:
                    pe.wait_ge(Ac, u * 6 + n - 1)
                else:
                    pe.wait_ge(Ac, u * 6)
                for h in range(H):
                    mm = pe.matmul(bank[n % 2][:, h * CH:(h + 1) * CH], KLv[:, n % 2, h, :], QLv[:, n % 2, h * CH:(h + 1) * CH],
                                   start=True, stop=True)
                mm.then_inc(scs, 1)

            def chunk(t, p, c):
                lo, hi = c * CH, (c + 1) * CH
                if c:
                    pe.wait_ge(Ss, t * 2 + 1)
                elif not last(t):
                    pe.wait_ge(Ss, t * 2)
                else:
                    pe.wait_ge(state_in, 16)
                for h in range(H):
                    mm = pe.matmul(bank[6 + h // 4][lo:hi, h % 4 * P:(h % 4 + 1) * P], qe[:, p, h, lo:hi], St[:, h, :],
                                   start=h % 4 == 0, stop=False, skip_group_check=True)
                mm.then_inc(qSs, 1)
                if not (last(t) and c):
                    for h in range(H):
                        mm = pe.matmul(bank[2 + h // 4][:, h % 4 * P:(h % 4 + 1) * P], kd[lo:hi, p, h, :], rz[lo:hi, p, 0, h, :],
                                       start=True, stop=True)
                    mm.then_inc(kSs, 1)

            def project(t, j):
                for k in range(KD):
                    mm = pe.matmul(bank[2 + j][:, :], oT[:, k, :], w[:, k, j * 512:(j + 1) * 512], start=k == 0, stop=k == KD - 1)
                if j:
                    mm.then_inc(R["mm"], 1)

            def step(t, p, i, first=False):
                more = not last(t)
                if more:
                    diagonal(t + 1, 1 - p, i + p)
                pe.wait_ge(z_in[p], (i + 1) * 16)
                pe.wait_ge(R["y"], t)
                pe.wait_ge(R["o_out"], t)
                pe.wait_ge(R["kd_out"], t + 1)
                pe.wait_ge(R["qe"], t + 1)
                chunk(t, p, 0)
                if more:
                    kd_transposes(t + 1)
                    level(t + 1, 0)
                chunk(t, p, 1)
                pe.wait_ge(Ac, t * 6 + 6)
                for h in range(H):
                    mm = pe.matmul(bank[6 + h // 4][:, h % 4 * P:(h % 4 + 1) * P], A[:, p, h, :], rz[:, p, 0, h, :],
                                   start=False, stop=h % 4 == 3, skip_group_check=True)
                mm.then_inc(R["o_ps"], 1)
                if more:
                    for n in (1, 2, 3):
                        level(t + 1, n)
                    pe.wait_ge(Ss, t * 2 + 2)
                else:
                    pe.wait_ge(Ss, t * 2 + 1)
                pe.wait_ge(R["og"], t + 1)
                for h in range(H):
                    mm = pe.transpose(bank[2 + h // 4][:, h % 4 * P:(h % 4 + 1) * P], o[:, h, :], ident[:, :])
                mm.then_inc(R["ogt"], 1)
                if more:
                    level(t + 1, 4)
                pe.wait_ge(R["oT_out"], t + 1)
                project(t, 0)
                if more:
                    level(t + 1, 5)
                project(t, 1)

            diagonal(0, 0, 0)
            kd_transposes(0)
            for n in range(6):
                level(0, n)
            after_first(pe, step)

        @block.vector
        def _(dve):
            dve_rows(dve)
            dve.memset(KLv[:, :, :, :], 0.0)
            dve.memset(St[:, :, :], 0.0).then_inc(init, 1)
            dve.wait_ge(init, 1)

            def tail(u, p, i):
                dve.wait_ge(q_in[p], (i + 1) * 16)
                dve.wait_ge(R["kdt"], u)
                Gc = rq[:, p, 2, :, :].rearrange("p h (c t) -> p (h c) t", t=CH)
                dve.tensor_tensor(kdT[:, :, :].rearrange("p h (c t) -> p (h c) t", t=CH), Gc[:, :, CH - 1:CH].to_broadcast([P, 2 * H, CH]), Gc,
                                  ALU.subtract).then_inc(R["tail"], 1)

            def differences(u, p, n):
                b = LEVELS[n]
                g = halves(rq[:, p, 2, :, :], b)
                mid = g[:, :, 0, b - 1:b].to_broadcast([P, 512 // b, b])
                dve.tensor_tensor(DL[:, 0, :].rearrange("p (n b) -> p n b", b=b), mid, g[:, :, 0, :], ALU.subtract)
                dve.tensor_tensor(DL[:, 1, :].rearrange("p (n b) -> p n b", b=b), g[:, :, 1, :], mid, ALU.subtract).then_inc(dls, 1)

            def diagonal(u, p):
                dve.wait_ge(R["dq"], u + 1)
                for j in range(2):
                    v = dve.tensor_tensor(A[:, p, 4 * j:4 * j + 4, :], heads4(bank[4 + j]), over_heads(keep["ident"][:, :], 4), ALU.mult)
                v.then_inc(R["dg"], 1)
                dve.wait_ge(R["fin"], u + 1)
                dve.tensor_tensor(kdT[:, :, :], rq[:, p, 1, :, :], kdT[:, :, :], ALU.mult).then_inc(R["kd"], 1)

            def operands(u, p, n):
                b = LEVELS[n]
                dve.wait_ge(els, u * 6 + n + 1)
                if n >= 2:
                    dve.wait_ge(scs, u * 6 + n - 1)
                dve.tensor_tensor(halves(KLv[:, n % 2, :, :], b)[:, :, 0, :], halves(rq[:, p, 1, :, :], b)[:, :, 0, :],
                                  EL[:, n % 2, 0, :].rearrange("p (n b) -> p n b", b=b), ALU.mult)
                dve.tensor_tensor(QLv[:, n % 2, :].rearrange("p (n b) -> p n b", b=b), halves(rq[:, p, 0, :, :], b)[:, :, 1, :],
                                  EL[:, n % 2, 1, :].rearrange("p (n b) -> p n b", b=b), ALU.mult).then_inc(kqs, 1)

            def take(u, p, n):
                b = LEVELS[n]
                dve.wait_ge(scs, u * 6 + n + 1)
                if n:
                    dve.wait_ge(Ac, u * 6 + n)
                dve.memset(hold[:, n:n + 1], 0.0)
                dst = A[:, p, :, :].rearrange("p h (n a b) -> p h n a b", a=2, b=b)[:, :, :, 1, :]
                src = bank[n % 2][:, :].rearrange("p (h n b) -> p h n b", h=H, b=b)
                mask = keep["levels"][:, n, :].bitcast(I32).rearrange("p (n a b) -> p n a b", a=2, b=b)[:, :, 1, :]
                dve.copy_predicated(dst, mask.unsqueeze(1).to_broadcast([P, H, CH // b, b]), src).then_inc(Ac, 1)

            def update(t, p, c):
                if not (last(t) and c):
                    dve.wait_ge(qSs, t * 2 + c + 1)
                    dve.wait_ge(kSs, t * 2 + c + 1)
                    for h in range(H):
                        v = dve.scalar_tensor_tensor(out=St[:, h, :], in0=St[:, h, :], scalar=EG[:, p, h, (c + 1) * CH - 1:(c + 1) * CH],
                                                     in1=bank[2 + h // 4][:, h % 4 * P:(h % 4 + 1) * P], op0=ALU.mult, op1=ALU.add)
                    v.then_inc(Ss, 1)

            def slot(u, p, n):
                operands(u, p, n)
                if n < 5:
                    differences(u, p, n + 1)
                if n:
                    take(u, p, n - 1)

            def squares(t):
                dve.wait_ge(R["o_out"], t + 1)
                dve.tensor_tensor(osq[:, :, :], o[:, :, :], o[:, :, :], ALU.mult).then_inc(R["on"], 1)
                dve.wait_ge(R["on"], t + 1)
                dve.tensor_reduce(os8[:, :], osq[:, :, :], AX, ALU.add).then_inc(R["sum"], 1)
                dve.wait_ge(R["sum"], t + 1)
                dve.tensor_scalar(os8[:, :], os8[:, :], 1.0 / P, EPS, ALU.mult, ALU.add).then_inc(R["os"], 1)

            def gated(t, p):
                dve.wait_ge(R["or"], t + 1)
                dve.tensor_tensor(o[:, :, :], o[:, :, :], bc(or8[:, :], P), ALU.mult).then_inc(R["normed"], 1)
                dve.wait_ge(R["normed"], t + 1)
                dve.wait_ge(R["gate"], t + 1)
                dve.tensor_tensor(o[:, :, :], o[:, :, :], rz[:, p, 1, :, :], ALU.mult).then_inc(R["og"], 1)

            def close(t):
                dve.wait_ge(R["y"], t + 1)
                dve.tensor_tensor_reduce(flat(osq[:, :, :]), y[:, :], y[:, :], 1.0 / D, EPS, ALU.mult, ALU.add, ms[:, :]).then_inc(R["ms"], 1)
                dve.wait_ge(R["rs"], t + 1)
                dve.wait_ge(x_in, (t + 1) * 16)
                dve.scalar_tensor_tensor(out=y[:, :], in0=y[:, :], scalar=rs[:, 0:1], in1=gB[:, cond(t), :],
                                         op0=ALU.mult, op1=ALU.mult).then_inc(R["yn"], 1)
                dve.wait_ge(R["yn"], t + 1)
                dve.tensor_tensor(y[:, :], y[:, :], xt[:, :], ALU.add).then_inc(R["out"], 1)

            def step(t, p, i, first=False):
                u, pu = t + 1, 1 - p
                more = not last(t)
                if more:
                    tail(u, pu, i + p)
                    differences(u, pu, 0)
                    dve.wait_ge(R["o_ps"], t)
                    diagonal(u, pu)
                update(t, p, 0)
                if more:
                    slot(u, pu, 0)
                update(t, p, 1)
                if more:
                    slot(u, pu, 1)
                if not first:
                    close(t - 1)
                if more:
                    slot(u, pu, 2)
                squares(t)
                if more:
                    slot(u, pu, 3)
                gated(t, p)
                if more:
                    slot(u, pu, 4)
                    slot(u, pu, 5)
                    take(u, pu, 5)

            tail(0, 0, 0)
            differences(0, 0, 0)
            diagonal(0, 0)
            for n in range(6):
                slot(0, 0, n)
            take(0, 0, 5)
            after_first(dve, step)
            close(SAMPLE)


def program(nc, io):
    scr = {n: nc.dram_tensor("scr_" + n, list(s), F32, kind="Internal").ap() for n, s in (
        ("qkv", (TILES, P, NCT, P)), ("z", (TILES, P, D)), ("ba", (TILES, P, 8)), ("cq", (TILES, P, QL)),
        ("oa", (TILES, P, 512)), ("ob", (TILES, P, 512)), ("x1", (TILES, P, D)), ("qkg", (TILES, P, 3 * D)), ("iz", (TILES, P, 2 * D)))}
    with ExitStack() as ctx:
        keep = {n: ctx.enter_context(nc.sbuf_tensor("k_" + n, list(s), F32)) for n, s in (
            ("ident", (P, P)), ("cums", (P, P)), ("strict", (P, P)), ("blk", (P, P)), ("low1", (P, P)),
            ("levels", (P, 6, P)), ("ones", (P, P)), ("mhalf", (P, 8)), ("lb", (P, 2, KD)),
            ("mA", (P, 2, 2, KD)), ("mB", (P, 2, 2, KD)), ("gg", (P, 2, 2, KD)))}
        modulation(nc, io, keep)
        in_even(nc, io, keep, scr)
        delta(nc, io, keep, scr)
        with ExitStack() as kv:
            kT = kv.enter_context(nc.sbuf_tensor("kT", [P, HB, PAST + DEC], F32))
            V = kv.enter_context(nc.sbuf_tensor("V", [P, NT + 1, HB, DV + 1], F32))
            for sample in (False, True):
                keys(nc, io, keep, scr, kT, V, sample)
                attention(nc, io, keep, scr, kT, V, sample)
        close_even(nc, io, keep, scr)
        in_odd(nc, io, keep, scr)
        hgrn(nc, io, keep, scr)


INS = ("x_prompt x_sample c_prompt c_sample cache_ckv cache_kr state_delta state_conv state_hgrn w_ada b_ada g_pre g_post "
       "w_in_e conv_w a_log dt_bias g_norm_a g_q w_uq g_kv w_ukv w_out_e w_in_o lb_logits g_norm_c w_out_o").split()
OUTS = (("y_prompt", (1, SEQ, D)), ("y_sample", (1, DEC, D)), ("p_delta", (1, 1, HA, DK, DK)), ("p_conv", (1, 1, 3, QKV)),
        ("p_ckv", (1, 1, SEQ, KL)), ("p_kr", (1, 1, SEQ, ROPE)), ("p_hgrn", (1, 1, HC, P, P)),
        ("s_delta", (1, 1, HA, DK, DK)), ("s_conv", (1, 1, 3, QKV)), ("s_ckv", (1, 1, DEC, KL)), ("s_kr", (1, 1, DEC, ROPE)),
        ("s_hgrn", (1, 1, HC, P, P)))


def constants():
    import numpy as np
    a = np.arange(P)
    same = (a[:, None] // CH) == (a[None, :] // CH)
    levels = np.zeros((P, 6, P), np.float32)
    for n, b in enumerate(LEVELS):
        block = (a[:, None] // (2 * b)) == (a[None, :] // (2 * b))
        levels[:, n, :] = block & (a[:, None] // b % 2 == 0) & (a[None, :] // b % 2 == 1)
    half = ROPE // 2
    inv = (np.float32(10000.0) ** (-np.arange(half, dtype=np.float32) / np.float32(half))).astype(np.float32)
    ang = np.arange(TILES * P, dtype=np.float32)[:, None] * inv[None, :]
    cos, sin = np.cos(ang).astype(np.float32), np.sin(ang).astype(np.float32)
    rope = np.concatenate([cos, cos, -sin, sin], axis=1).reshape(TILES, P, 64)
    return {
        "c_ident": np.eye(P, dtype=np.float32),
        "c_cums": (same & (a[:, None] <= a[None, :])).astype(np.float32),
        "c_blk": same.astype(np.float32),
        "c_strict": (same & (a[:, None] > a[None, :])).astype(np.float32),
        "c_low1": np.ascontiguousarray(levels[:, 0, :].T),
        "c_levels": levels,
        "c_rope": rope,
    }


def kernel(**inputs):
    import numpy as np
    import concourse.bacc as bacc
    from concourse.bass_utils import run_bass_kernel_spmd

    nc = bacc.Bacc("TRN2", target_bir_lowering=False, num_devices=1)
    arrays = {n: np.ascontiguousarray(inputs[n]) for n in INS}
    arrays.update(constants())
    io = {n: nc.dram_tensor(n, a.shape, F32, kind="ExternalInput").ap() for n, a in arrays.items()}
    for n, s in OUTS:
        io[n] = nc.dram_tensor(n, s, F32, kind="ExternalOutput").ap()
    program(nc, io)
    r = run_bass_kernel_spmd(nc, [arrays], core_ids=[0])
    return tuple(r.results[0][n] for n, _ in OUTS)
```

```python
from contextlib import ExitStack

import concourse.bass as bass
from concourse import mybir

F32 = mybir.dt.float32
I32 = mybir.dt.int32
ALU = mybir.AluOpType
ACT = mybir.ActivationFunctionType
AX = mybir.AxisListType.X

P = 128
D = 1024
KD = D // P
SEQ = 2048
NT = SEQ // P
TILES = NT + 1
SAMPLE = NT
DEC = 64
CH = 64
PAST = 2048
EPS = 1e-6
HA, DK = 4, 128
QKV = 3 * HA * DK
NCT = QKV // P
HB, NOPE, ROPE, DV = 8, 64, 32, 64
HQ = NOPE + ROPE
QL, KL = 384, 256
IN_E = 3240
HC = 8
IN_O = 4096
LEVELS = (1, 2, 4, 8, 16, 32)
TOK = QKV
EVEN_GROUPS = ((1536, 2048), (2048, 2440), (2440, 2728), (2728, 3240))


RING = 5
AHEAD = 6


class Links:

    def __init__(self, eng, sem, per, tile):
        self.eng, self.sem, self.per, self.k = eng, sem, per, 0
        self.base = tile * per

    def did(self, ins):
        ins.then_inc(self.sem, 1)
        self.k += 1
        return self.k

    def need(self, k):
        self.eng.wait_ge(self.sem, self.base + k)

    def link(self, ins):
        self.need(self.did(ins))

    def end(self):
        assert self.k == self.per, self.k


def stage(nc, ctx):
    def sb(name, shape, dt=F32):
        return ctx.enter_context(nc.sbuf_tensor(name, shape, dt))

    def ps(name, shape=(P, 512)):
        return ctx.enter_context(nc.psum_tensor(name, list(shape), F32))

    sems = []

    def sem(name):
        sems.append(nc.alloc_semaphore(name))
        return sems[-1]

    def clear():
        nc.clear_and_free_semaphores(sems)
        nc.all_engine_barrier()

    ctx.callback(clear)
    return sb, ps, sem


def tiles_of(eng, body):
    with eng.Fori(0, NT // 2 - 1) as i:
        body(i * 2, 0, i)
        body(i * 2 + 1, 1, i)
    body(NT - 2, 0, NT // 2 - 1)
    body(NT - 1, 1, NT // 2 - 1)
    body(SAMPLE, 0, NT // 2)


def after_first(eng, body):
    body(0, 0, 0, first=True)
    body(1, 1, 0)
    with eng.Fori(1, NT // 2 - 1) as i:
        body(i * 2, 0, i)
        body(i * 2 + 1, 1, i)
    body(NT - 2, 0, NT // 2 - 1)
    body(NT - 1, 1, NT // 2 - 1)
    body(SAMPLE, 0, NT // 2)


def last(t):
    return isinstance(t, int) and t == SAMPLE


def cond(t):
    return 1 if last(t) else 0


def modulation(nc, io, keep, w_even, even_in):
    with ExitStack() as ctx:
        sb, ps, sem = stage(nc, ctx)
        cT = sb("cT", [P, 2, KD])
        scT = sb("scT", [P, KD, 2])
        wa = sb("wa", [P, RING, 3 * D])
        rows = sb("rows", [2, 3 * D])
        bT = sb("bT", [P, 2, 24])
        gpre = sb("gpre", [P, 2, KD])
        gpost = sb("gpost", [P, 2, KD])
        lb = sb("lbl", [P, 2, KD])
        lt = sb("lt", [P, 4, KD])
        md = sb("md", [P, 2, 24, 2])
        mrow = ps("mrow", [2, 6, 512])
        mps = ps("mps", [P, 2, 512])
        consts = sem("m_consts")
        weights = sem("m_weights")
        w_in = [sem(f"m_w{k}") for k in range(RING)]
        rows_out, turned = sem("m_rows_out"), sem("m_turned")
        silu = sem("m_silu")
        used = sem("m_used")
        link = sem("m_link")
        lexp = sem("m_lexp")
        lmax = sem("m_lmax")
        block = ctx.enter_context(nc.Block())

        @block.sync
        def _(sp):
            for j, c in enumerate((io["c_prompt"], io["c_sample"])):
                sp.dma_start(cT[:, j, :], c.rearrange("a (k p) -> p (a k)", p=P), allow_slow_non_contiguous=True).then_inc(consts, 16)
            sp.dma_start(keep["ident"][:, :], io["c_ident"]).then_inc(consts, 16)
            sp.dma_start(keep["cums"][:, :], io["c_cums"]).then_inc(consts, 16)
            sp.dma_start(keep["blk"][:, :], io["c_blk"]).then_inc(consts, 16)
            sp.dma_start(keep["low1"][:, :], io["c_low1"]).then_inc(consts, 16)
            sp.dma_start(keep["strict"][:, :], io["c_strict"]).then_inc(consts, 16)
            sp.dma_start(keep["levels"][:, :, :], io["c_levels"]).then_inc(consts, 16)
            for n in range(2 * KD):
                if n >= RING:
                    sp.wait_ge(used, n - RING + 1)
                sp.dma_start(wa[:, n % RING, :], io["w_ada"][n // KD, n % KD * P:(n % KD + 1) * P, :]).then_inc(w_in[n % RING], 16)

        @block.gpsimd
        def _(pool):
            for l in range(2):
                pool.dma_start(gpre[:, l, :], io["g_pre"][l].rearrange("(k p) -> p k", p=P), allow_slow_non_contiguous=True).then_inc(weights, 16)
                pool.dma_start(gpost[:, l, :], io["g_post"][l].rearrange("(k p) -> p k", p=P), allow_slow_non_contiguous=True).then_inc(weights, 16)
                pool.dma_start(bT[:, l, :], io["b_ada"][l].rearrange("(k p) -> p k", p=P), allow_slow_non_contiguous=True).then_inc(weights, 16)
                pool.dma_start(lb[:, l, :], io["lb_logits"][l].rearrange("(k p) -> p k", p=P), allow_slow_non_contiguous=True).then_inc(weights, 16)
            pool.memset(keep["ones"][:, :], 1.0)
            pool.memset(keep["mhalf"][:, :], -0.5).then_inc(silu, 1)
            pool.wait_ge(used, KD)
            for k in range(KD):
                pool.dma_start(w_even[:, k, :], io["w_in_e"][0, k * P:(k + 1) * P, :]).then_inc(even_in, 16)

        @block.scalar
        def _(act):
            act.wait_ge(consts, 8 * 16)
            for j in range(2):
                act.activation(scT[:, :, j], cT[:, j, :], ACT.Silu).then_inc(silu, 1)
            act.wait_ge(lmax, 1)
            act.activation(lt[:, 1:3, :], lt[:, 1:3, :], ACT.Exp).then_inc(lexp, 1)
            for l in range(2):
                act.wait_ge(used, (l + 1) * KD)
                if l:
                    act.wait_ge(turned, 1)
                act.copy(rows[:, :], mrow[:, :, :].rearrange("p a b -> p (a b)")).then_inc(rows_out, 1)

        @block.tensor
        def _(pe):
            pe.wait_ge(silu, 3)

            def turn(l):
                for ct in range(24):
                    mm = pe.transpose(mps[:, l, 2 * ct:2 * ct + 2], rows[:, ct * P:(ct + 1) * P], keep["ident"][0:2, 0:2])
                mm.then_inc(turned, 1)

            for l in range(2):
                if l:
                    pe.wait_ge(rows_out, l)
                for k in range(KD):
                    n = l * KD + k
                    pe.wait_ge(w_in[n % RING], (n // RING + 1) * 16)
                    for j in range(6):
                        mm = pe.matmul(mrow[:, j, :], scT[:, k, :], wa[:, n % RING, j * 512:(j + 1) * 512], start=k == 0, stop=k == KD - 1)
                    mm.then_inc(used, 1)
                    if n == KD:
                        turn(0)
            pe.wait_ge(rows_out, 2)
            turn(1)

        @block.vector
        def _(dve):
            ln = Links(dve, link, 11, 0)
            dve.wait_ge(weights, 8 * 16)
            dve.wait_ge(consts, 8 * 16)
            ln.link(dve.tensor_tensor(lt[:, 0, :], lb[:, 0, :], lb[:, 1, :], ALU.max))
            for l in range(2):
                t = dve.tensor_tensor(lt[:, 1 + l, :], lb[:, l, :], lt[:, 0, :], ALU.subtract)
            t.then_inc(lmax, 1)
            dve.wait_ge(lexp, 1)
            ln.link(dve.tensor_tensor(lt[:, 0, :], lt[:, 1, :], lt[:, 2, :], ALU.add))
            ln.link(dve.reciprocal(lt[:, 3, :], lt[:, 0, :]))
            ln.link(dve.tensor_tensor(lt[:, 1, :], lt[:, 1, :], lt[:, 3, :], ALU.mult))
            ln.link(dve.tensor_tensor(lt[:, 2, :], lt[:, 2, :], lt[:, 3, :], ALU.mult))
            ln.link(dve.tensor_tensor(lt[:, 2, :], lt[:, 2, :], lt[:, 1, :], ALU.add))
            ln.link(dve.tensor_tensor(keep["lb"][:, 0, :], lt[:, 2, :], lt[:, 1, :], ALU.subtract))
            ln.link(dve.tensor_scalar(keep["lb"][:, 1, :], keep["lb"][:, 0, :], -1.0, 1.0, ALU.mult, ALU.add))
            dve.wait_ge(turned, 2)
            for l in range(2):
                t = dve.tensor_tensor(md[:, l, :, :], mps[:, l, 0:48].rearrange("p (a b) -> p a b", b=2),
                                      bT[:, l, :].unsqueeze(2).to_broadcast([P, 24, 2]), ALU.add)
            ln.link(t)
            for l in range(2):
                for c in range(2):
                    t = dve.tensor_scalar(keep["mA"][:, l, c, :], md[:, l, 8:16, c], 1.0, None, ALU.add)
                    dve.tensor_copy(keep["mB"][:, l, c, :], md[:, l, 0:8, c])
                    u = dve.tensor_tensor(keep["gg"][:, l, c, :], md[:, l, 16:24, c], gpost[:, l, :], ALU.mult)
            ln.link(u)
            for l in range(2):
                for c in range(2):
                    t = dve.tensor_tensor(keep["mA"][:, l, c, :], keep["mA"][:, l, c, :], gpre[:, l, :], ALU.mult)
            ln.link(t)
            ln.end()


def norm_transpose(layer, keep, xt, xn, ms, rs, hT, xps, S):

    def dve_norm(dve, t, p, i):
        dve.wait_ge(S["x_in"][p], (i + 1) * 16)
        dve.wait_ge(S["xT"], t * 2)
        dve.tensor_tensor_reduce(xn[:, :], xt[:, p, :], xt[:, p, :], 1.0 / D, EPS,
                                 ALU.mult, ALU.add, ms[:, 0:1]).then_inc(S["x_ms"], 1)
        dve.wait_ge(S["x_rs"], t + 1)
        dve.tensor_scalar(xn[:, :], xt[:, p, :], rs[:, 0:1], None, ALU.mult).then_inc(S["xn"], 1)

    def pool_norm(pool, t):
        pool.wait_ge(S["x_ms"], t + 1)
        pool.tensor_tensor(rs[:, 0:1], ms[:, 0:1], keep["mhalf"][:, 0:1], ALU.pow).then_inc(S["x_rs"], 1)

    def pe_transposes(pe, t):
        pe.wait_ge(S["xn"], t + 1)
        pe.wait_ge(S["hT_a"], t)
        pe.wait_ge(S["hT_v"], t)
        for k in range(KD):
            mm = pe.transpose(xps[k // 4][:, (k % 4) * P:(k % 4 + 1) * P], xn[:, k * P:(k + 1) * P], keep["ident"][:, :])
            if k % 4 == 3:
                mm.then_inc(S["xT"], 1)

    def act_hT(act, t, p):
        act.wait_ge(S["xT"], t * 2 + 1)
        for k in range(4):
            u = act.activation(hT[:, p, k, :], xps[0][:, k * P:(k + 1) * P], ACT.Identity,
                               bias=keep["mB"][:, layer, cond(t), k:k + 1], scale=keep["mA"][:, layer, cond(t), k:k + 1])
        u.then_inc(S["hT_a"], 1)

    def dve_hT(dve, t, p):
        dve.wait_ge(S["xT"], t * 2 + 2)
        for k in range(4, 8):
            u = dve.tensor_scalar(hT[:, p, k, :], xps[1][:, (k - 4) * P:(k - 3) * P],
                                  keep["mA"][:, layer, cond(t), k:k + 1], keep["mB"][:, layer, cond(t), k:k + 1],
                                  ALU.mult, ALU.add)
        u.then_inc(S["hT_v"], 1)

    return dve_norm, pool_norm, pe_transposes, act_hT, dve_hT


def norm_sems(sem, tag):
    S = {n: sem(f"{tag}_{n}") for n in ("x_ms", "x_rs", "xn", "xT", "hT_a", "hT_v")}
    S["x_in"] = [sem(f"{tag}_x_in0"), sem(f"{tag}_x_in1")]
    return S


def in_even(nc, io, keep, scr, w, w_in):
    with ExitStack() as ctx:
        sb, ps, sem = stage(nc, ctx)
        xt = sb("a_xt", [P, 2, D])
        xn = sb("a_xn", [P, D])
        hT = sb("a_hT", [P, 2, KD, P])
        xp = sb("a_xp", [P, NCT, P + 3])
        cv = sb("a_cv", [P, 2, NCT, P])
        z = sb("a_z", [P, 2, D])
        ba = sb("a_ba", [P, 2, 8])
        cq = sb("a_cq", [P, QL])
        kv = sb("a_kv", [P, KL + ROPE])
        cqn = sb("a_cqn", [P, 2, QL])
        kvn = sb("a_kvn", [P, 2, KL + ROPE])
        junk = sb("a_junk", [P, QL + KL])
        cs = sb("a_cs", [P, 2, 64])
        rt = sb("a_rt", [P, 2, ROPE])
        cw = sb("a_cw", [P, 4, NCT])
        gq = sb("a_gq", [P, QL])
        gkv = sb("a_gkv", [P, KL])
        ms = sb("a_ms", [P, 1])
        rs = sb("a_rs", [P, 1])
        ms2 = sb("a_ms2", [P, 2])
        rs2 = sb("a_rs2", [P, 2])
        xps = [ps("a_x0"), ps("a_x1")]
        bank = [ps(f"a_p{i}") for i in range(6)]
        S = norm_sems(sem, "a")
        cs_in = [sem("a_cs_in0"), sem("a_cs_in1")]
        stored = [sem("a_stored0"), sem("a_stored1")]
        const_in = sem("a_const_in")
        proj, act_out, kv_out = sem("a_proj"), sem("a_act_out"), sem("a_kv_out")
        conv, silu_q, hist = sem("a_conv"), sem("a_silu_q"), sem("a_hist")
        lat_ms, lat_rs, lat = sem("a_lat_ms"), sem("a_lat_rs"), sem("a_lat")
        link, hist_in, hist_out = sem("a_link"), sem("a_hist_in"), sem("a_hist_out")
        dve_norm, pool_norm, pe_tr, act_hT, dve_hT = norm_transpose(0, keep, xt, xn, ms, rs, hT, xps, S)
        block = ctx.enter_context(nc.Block())
        STORES = 6
        OUTS = 6

        @block.sync
        def _(sp):
            def load(t, p):
                if last(t):
                    sp.dma_start(xt[0:DEC, p, :], io["x_sample"][0]).then_inc(S["x_in"][p], 16)
                else:
                    sp.dma_start(xt[:, p, :], io["x_prompt"][0].rearrange("(t p) d -> t p d", p=P)[t]).then_inc(S["x_in"][p], 16)
                sp.dma_start(cs[:, p, :], io["c_rope"][t]).then_inc(cs_in[p], 16)

            load(0, 0)
            sp.dma_start(gq[:, :], io["g_q"][0:1, :].to_broadcast([P, QL])).then_inc(const_in, 16)
            sp.dma_start(gkv[:, :], io["g_kv"][0:1, :].to_broadcast([P, KL])).then_inc(const_in, 16)
            for j in range(4):
                sp.dma_start(cw[:, j, :], io["conv_w"][0, j].rearrange("(c p) -> p c", p=P), allow_slow_non_contiguous=True).then_inc(const_in, 16)

            def step(t, p, i):
                if not last(t):
                    sp.wait_ge(S["xn"], t)
                    sp.wait_ge(lat, t)
                    load(t + 1, 1 - p)
                sp.wait_ge(silu_q, t + 1)
                sp.dma_start(scr["qkv"][t], cv[:, p, :, :]).then_inc(stored[p], 16)
                sp.wait_ge(act_out, (t + 1) * OUTS)
                sp.dma_start(scr["z"][t], z[:, p, :]).then_inc(stored[p], 16)
                sp.dma_start(scr["ba"][t], ba[:, p, :]).then_inc(stored[p], 16)
                sp.wait_ge(lat, t + 1)
                sp.dma_start(scr["cq"][t], cqn[:, p, :]).then_inc(stored[p], 16)
                if last(t):
                    ck, kr, n = io["s_ckv"][0, 0], io["s_kr"][0, 0], DEC
                else:
                    ck = io["p_ckv"][0, 0].rearrange("(t p) c -> t p c", p=P)[t]
                    kr, n = io["p_kr"][0, 0].rearrange("(t p) c -> t p c", p=P)[t], P
                sp.dma_start(ck, kvn[0:n, p, 0:KL]).then_inc(stored[p], 16)
                sp.dma_start(kr, kvn[0:n, p, KL:KL + ROPE]).then_inc(stored[p], 16)

            tiles_of(sp, step)
            for p in range(2):
                sp.wait_ge(stored[p], (TILES + 1 - p) // 2 * STORES * 16)

        @block.gpsimd
        def _(pool):
            def conv_rows(dst, at, cols):
                for j in range(3):
                    pool.dma_start(dst[0, 0, j].rearrange("(c p) -> p c", p=P), xp[:, :, at + j], allow_slow_non_contiguous=True).then_inc(cols, 16)

            def step(t, p, i):
                if isinstance(t, int) and t == NT - 1:
                    pool_norm(pool, t + 1)
                    pool.wait_ge(act_out, t * OUTS + 3)
                    conv_rows(io["p_conv"], P, hist_out)
                    pool.wait_ge(hist, NT)
                    for j in range(3):
                        pool.dma_start(xp[:, :, j], io["state_conv"][0, 0, j].rearrange("(c p) -> p c", p=P), allow_slow_non_contiguous=True).then_inc(hist_in, 16)
                elif last(t):
                    pool.wait_ge(act_out, t * OUTS + 3)
                    conv_rows(io["s_conv"], DEC, hist_out)
                else:
                    pool_norm(pool, t + 1)
                pool.wait_ge(lat_ms, t + 1)
                pool.tensor_tensor(rs2[:, :], ms2[:, :], keep["mhalf"][:, 0:2], ALU.pow).then_inc(lat_rs, 1)

            pool_norm(pool, 0)
            tiles_of(pool, step)
            pool.wait_ge(hist_out, 6 * 16)

        @block.scalar
        def _(act):
            def step(t, p, i):
                act.wait_ge(hist, t)
                if last(t):
                    act.wait_ge(hist_out, 3 * 16)
                for g in range(3):
                    act.wait_ge(proj, t * 7 + g + 1)
                    act.copy(xp[:, 4 * g:4 * g + 4, 3:], bank[g][:, :].rearrange("p (c t) -> p c t", c=4)).then_inc(act_out, 1)
                if not last(t):
                    act_hT(act, t + 1, 1 - p)
                act.wait_ge(proj, t * 7 + 4)
                act.wait_ge(stored[p], i * (STORES * 16))
                act.copy(ba[:, p, :], bank[3][:, 0:8])
                act.activation(z[:, p, 0:504], bank[3][:, 8:512], ACT.Silu).then_inc(act_out, 1)
                act.wait_ge(proj, t * 7 + 5)
                act.wait_ge(lat, t)
                act.activation(z[:, p, 504:512], bank[4][:, 0:8], ACT.Silu)
                act.copy(cq[:, :], bank[4][:, 8:392]).then_inc(act_out, 1)
                act.wait_ge(conv, t + 1)
                act.activation(cv[:, p, :, :], cv[:, p, :, :], ACT.Silu).then_inc(silu_q, 1)
                act.wait_ge(proj, t * 7 + 7)
                act.activation(z[:, p, 512:1024], bank[0][:, :], ACT.Silu).then_inc(act_out, 1)

            act.wait_ge(S["xT"], 1)
            act_hT(act, 0, 0)
            tiles_of(act, step)

        @block.tensor
        def _(pe):
            def step(t, p, i):
                pe.wait_ge(S["hT_a"], t + 1)
                pe.wait_ge(S["hT_v"], t + 1)
                pe.wait_ge(act_out, t * OUTS)
                for g in range(3):
                    for c in range(4 * g, 4 * g + 4):
                        for k in range(KD):
                            mm = pe.matmul(bank[g][:, (c % 4) * P:(c % 4 + 1) * P], w[:, k, c * P:(c + 1) * P],
                                           hT[:, p, k, :], start=k == 0, stop=k == KD - 1)
                    mm.then_inc(proj, 1)
                if not last(t):
                    pe_tr(pe, t + 1)
                for g, (a, b) in enumerate(EVEN_GROUPS):
                    dst = bank[0] if g == 3 else bank[3 + g]
                    if g == 2:
                        pe.wait_ge(kv_out, t)
                    if g == 3:
                        pe.wait_ge(act_out, t * OUTS + 1)
                    for k in range(KD):
                        mm = pe.matmul(dst[:, 0:b - a], hT[:, p, k, :], w[:, k, a:b], start=k == 0, stop=k == KD - 1)
                    mm.then_inc(proj, 1)

            pe_tr(pe, 0)
            pe.wait_ge(w_in, 16 * KD)
            tiles_of(pe, step)

        @block.vector
        def _(dve):
            def step(t, p, i):
                ln = Links(dve, link, 6, t)
                if not last(t):
                    dve_norm(dve, t + 1, 1 - p, i + p)
                dve.wait_ge(act_out, t * OUTS + 3)
                if last(t):
                    dve.wait_ge(hist_in, 3 * 16)
                dve.wait_ge(stored[p], i * (STORES * 16))
                for c in range(NCT):
                    u = dve.tensor_scalar(cv[:, p, c, :], xp[:, c, 0:P], cw[:, 0, c:c + 1], None, ALU.mult)
                for j in range(1, 4):
                    ln.link(u)
                    for c in range(NCT):
                        u = dve.scalar_tensor_tensor(out=cv[:, p, c, :], in0=xp[:, c, j:j + P], scalar=cw[:, j, c:c + 1],
                                                     in1=cv[:, p, c, :], op0=ALU.mult, op1=ALU.add)
                u.then_inc(conv, 1)
                dve.wait_ge(conv, t + 1)
                dve.tensor_copy(xp[:, :, 0:3], xp[:, :, P:P + 3]).then_inc(hist, 1)
                if not last(t):
                    dve_hT(dve, t + 1, 1 - p)
                dve.wait_ge(proj, t * 7 + 6)
                dve.tensor_copy(kv[:, :], bank[5][:, 0:KL + ROPE]).then_inc(kv_out, 1)
                dve.wait_ge(kv_out, t + 1)
                dve.wait_ge(act_out, t * OUTS + 5)
                dve.tensor_tensor_reduce(junk[:, 0:QL], cq[:, :], cq[:, :], 1.0 / QL, EPS, ALU.mult, ALU.add, ms2[:, 0:1])
                dve.tensor_tensor_reduce(junk[:, QL:QL + KL], kv[:, 0:KL], kv[:, 0:KL], 1.0 / KL, EPS, ALU.mult, ALU.add,
                                         ms2[:, 1:2]).then_inc(lat_ms, 1)
                dve.wait_ge(cs_in[p], (i + 1) * 16)
                dve.tensor_tensor(rt[:, 0, :], kv[:, KL:KL + ROPE], cs[:, p, 0:32], ALU.mult)
                dve.tensor_tensor(rt[:, 1, 0:16], kv[:, KL + 16:KL + 32], cs[:, p, 32:48], ALU.mult)
                ln.link(dve.tensor_tensor(rt[:, 1, 16:32], kv[:, KL:KL + 16], cs[:, p, 48:64], ALU.mult))
                ln.link(dve.tensor_tensor(kvn[:, p, KL:KL + ROPE], rt[:, 0, :], rt[:, 1, :], ALU.add))
                dve.wait_ge(lat_rs, t + 1)
                ln.link(dve.scalar_tensor_tensor(out=kvn[:, p, 0:KL], in0=kv[:, 0:KL], scalar=rs2[:, 1:2], in1=gkv[:, :],
                                                 op0=ALU.mult, op1=ALU.mult))
                dve.scalar_tensor_tensor(out=cqn[:, p, :], in0=cq[:, :], scalar=rs2[:, 0:1], in1=gq[:, :],
                                         op0=ALU.mult, op1=ALU.mult).then_inc(lat, 1)
                ln.end()

            dve.memset(xp[:, :, 0:3], 0.0)
            dve.wait_ge(const_in, 6 * 16)
            dve_norm(dve, 0, 0, 0)
            dve_hT(dve, 0, 0)
            tiles_of(dve, step)


def bc(ap, n):
    return ap.unsqueeze(2).to_broadcast([ap.shape[0], ap.shape[1], n])


def over_heads(ap, h):
    return ap.unsqueeze(1).to_broadcast([ap.shape[0], h, ap.shape[1]])


def since(eng, sem, n):
    if not (isinstance(n, int) and n <= 0):
        eng.wait_ge(sem, n)


def delta(nc, io, keep, scr):
    H = HA
    with ExitStack() as ctx:
        sb, ps, sem = stage(nc, ctx)
        sc = sb("d_sc", [P, 2, 3 * H, P])
        ba = sb("d_ba", [P, 2, 8])
        za = sb("d_za", [P, 2, H * P])
        dtb, nea, gna = sb("d_dtb", [P, H]), sb("d_nea", [P, H]), sb("d_gna", [P, P])
        x8, e8, u8, l4, w4 = (sb(f"d_{n}", [P, 8]) for n in ("x8", "e8", "u8", "l4", "w4"))
        xa, beta, g = sb("d_xa", [P, H]), sb("d_beta", [P, H]), sb("d_g", [P, H])
        gB = sb("d_gB", [P, H, P])
        g8, ge8, bg = sb("d_g8", [P, 8]), sb("d_ge8", [P, 8]), sb("d_bg", [P, H])
        EB, Dm, Em = sb("d_EB", [P, H, P]), sb("d_Dm", [P, H, P]), sb("d_Em", [P, H, P])
        eS = sb("d_eS", [P, 2, H, 2])
        qk, sq = sb("d_qk", [P, 2 * H, P]), sb("d_sq", [P, 2 * H, P])
        ss8, r8, qs8 = sb("d_ss8", [P, 8]), sb("d_r8", [P, 8]), sb("d_qs8", [P, 8])
        vb, kb, kd = sb("d_vb", [P, 2, H, P]), sb("d_kb", [P, 2, H, P]), sb("d_kd", [P, 2, H, P])
        qkT, qe = sb("d_qkT", [P, 2 * H, P]), sb("d_qe", [P, 2, H, P])
        M, MT, A = sb("d_M", [P, H, P]), sb("d_MT", [P, H, P]), sb("d_A", [P, 2, H, P])
        CT = sb("d_CT", [P, 2, 5, H, P])
        T, U, X = sb("d_T", [P, 2, H, P]), sb("d_U", [P, 2, H, P]), sb("d_X", [P, H, P])
        wT, u, vn = sb("d_wT", [P, H, P]), sb("d_u", [P, H, P]), sb("d_vn", [P, H, P])
        St = sb("d_S", [P, H, P])
        o, osq, gz = sb("d_o", [P, H, P]), sb("d_osq", [P, H, P]), sb("d_gz", [P, H, P])
        os4, or4 = sb("d_os4", [P, H]), sb("d_or4", [P, H])
        oT = sb("d_oT", [P, 2, H, P])
        A0, A1, A2, BX, BT, BU, BS, BO = (ps(f"d_b{i}") for i in range(8))
        names = ("x8 e8 u8 ln g gB gc gcB g8 t8 ge8 EB DE E12 mask qkvT qk_out v_out ss r8 qkn qkT qkT_out kbkd kk M A MT "
                 "MT_out T1 U1 wu wT_out u_out o_ps o_out os or4 gz og normed ogT oT_out beta qe bg").split()
        R = {n: sem("d_" + n) for n in names}
        CTs, Xs, Xo, YYs, TUs = sem("d_CTs"), sem("d_Xs"), sem("d_Xo"), sem("d_YYs"), sem("d_TUs")
        wSs, vns, kvs, Ss = sem("d_wSs"), sem("d_vns"), sem("d_kvs"), sem("d_Ss")
        in_, stored = [sem("d_in0"), sem("d_in1")], [sem("d_st0"), sem("d_st1")]
        z_in = [sem("d_z0"), sem("d_z1")]
        const_in, state_out, state_in, s0 = sem("d_const"), sem("d_s_out"), sem("d_s_in"), sem("d_s0")
        link, olink, plink, ea, qs_in = sem("d_link"), sem("d_olink"), sem("d_plink"), sem("d_ea"), sem("d_qs_in")
        block = ctx.enter_context(nc.Block())
        flat = lambda b: b.rearrange("p h t -> p (h t)")
        heads = lambda b: b[:, :].rearrange("p (h t) -> p h t", h=H)

        def state(ap):
            return ap.rearrange("h d e -> d h e")

        def steps_of(eng, step):
            step(-2, 0, -1, True, False, False)
            step(-1, 1, -1, True, True, False)
            with eng.Fori(0, NT // 2 - 1) as i:
                step(i * 2, 0, i, True, True, True)
                step(i * 2 + 1, 1, i, True, True, True)
            step(NT - 2, 0, NT // 2 - 1, True, True, True)
            step(NT - 1, 1, NT // 2 - 1, False, True, True)
            step(SAMPLE, 0, NT // 2, False, False, True)

        @block.sync
        def _(sp):
            sp.dma_start(dtb[:, :], io["dt_bias"][0:1, :].to_broadcast([P, H])).then_inc(const_in, 16)
            sp.dma_start(nea[:, :], io["a_log"][0:1, :].to_broadcast([P, H])).then_inc(const_in, 16)
            sp.dma_start(gna[:, :], io["g_norm_a"][0:1, :].to_broadcast([P, P])).then_inc(const_in, 16)

            def load(t, p, ahead=0):
                sp.dma_start(sc[:, p, :, :], scr["qkv"][ahead:][t]).then_inc(in_[p], 16)
                sp.dma_start(ba[:, p, :], scr["ba"][ahead:][t]).then_inc(in_[p], 16)

            def load_z(t, p, ahead=0):
                sp.dma_start(za[:, p, :], scr["z"][ahead:][t, :, 0:H * P]).then_inc(z_in[p], 16)

            load(0, 0)
            load(1, 1)
            load_z(0, 0)

            def step(t, p, i, operands, inverse, output):
                if not output:
                    return
                if operands and not (isinstance(t, int) and t + 3 > SAMPLE):
                    sp.wait_ge(R["x8"], t + 2)
                    sp.wait_ge(R["qkvT"], t * 3 + 6)
                    load(t, 1 - p, ahead=3)
                if not last(t):
                    sp.wait_ge(R["gz"], t)
                    load_z(t, 1 - p, ahead=1)
                sp.wait_ge(R["oT_out"], t + 1)
                sp.dma_start(scr["oa"][t], flat(oT[:, p, :, :])).then_inc(stored[p], 16)
                if isinstance(t, int) and t == NT - 1:
                    sp.wait_ge(Ss, 2 * NT)
                    sp.dma_start(state(io["p_delta"][0, 0]), St[:, :, :]).then_inc(state_out, 16)
                    sp.wait_ge(state_out, 16)
                    sp.dma_start(St[:, :, :], state(io["state_delta"][0, 0])).then_inc(state_in, 16)
                if last(t):
                    sp.wait_ge(Ss, 2 * NT + 1)
                    sp.dma_start(state(io["s_delta"][0, 0]), St[:, :, :]).then_inc(state_out, 16)

            sp.wait_ge(R["x8"], 1)
            sp.wait_ge(R["qkvT"], 3)
            load(2, 0)
            steps_of(sp, step)
            sp.wait_ge(state_out, 32)
            sp.wait_ge(stored[0], (TILES + 1) // 2 * 16)
            sp.wait_ge(stored[1], TILES // 2 * 16)

        @block.gpsimd
        def _(pool):
            def step(t, p, i, operands, inverse, output):
                a = t + 2
                if output:
                    pool.wait_ge(z_in[p], (i + 1) * 16)
                    pool.wait_ge(R["og"], t)
                    pool.tensor_tensor(gz[:, :, :], za[:, p, :].rearrange("p (h t) -> p h t", h=H), over_heads(gna[:, :], H), ALU.mult).then_inc(R["gz"], 1)
                if operands:
                    ln = Links(pool, plink, 4, a)
                    pool.wait_ge(R["ss"], a + 1)
                    ln.link(pool.tensor_tensor(r8[:, :], ss8[:, :], keep["mhalf"][:, :], ALU.pow))
                    pool.tensor_tensor(r8[:, :], r8[:, :], qs8[:, :], ALU.mult).then_inc(R["r8"], 1)
                    pool.wait_ge(R["E12"], a + 1)
                    ln.link(pool.tensor_tensor(Dm[:, :, :], Dm[:, :, :], over_heads(keep["strict"][:, :], H), ALU.mult))
                    pool.tensor_tensor(Dm[:, :, :], Dm[:, :, :], bc(beta[:, :], P), ALU.mult)
                    pool.tensor_tensor(Em[:, :, :], Em[:, :, :], over_heads(keep["cums"][:, :], H), ALU.mult).then_inc(R["mask"], 1)
                if output:
                    pool.wait_ge(R["os"], t + 1)
                    pool.tensor_tensor(or4[:, :], os4[:, :], keep["mhalf"][:, 0:H], ALU.pow).then_inc(R["or4"], 1)
                if operands:
                    pool.wait_ge(R["qkn"], a + 1)
                    pool.wait_ge(R["bg"], a + 1)
                    since(pool, kvs, (a - 1) * 2)
                    since(pool, R["wu"], a - 1)
                    pool.tensor_tensor(kb[:, p, :, :], qk[:, H:2 * H, :], bc(bg[:, :], P), ALU.mult)
                    pool.tensor_tensor(kd[:, p, :, :], qk[:, H:2 * H, :], bc(ge8[:, H:8], P), ALU.mult).then_inc(R["kbkd"], 1)
                    pool.wait_ge(R["M"], a + 1)
                    ln.link(pool.tensor_tensor(T[:, p, :, :], M[:, :, :], over_heads(keep["low1"][:, :], H), ALU.mult))
                    pool.tensor_tensor(T[:, p, :, :], over_heads(keep["ident"][:, :], H), T[:, p, :, :], ALU.subtract).then_inc(R["T1"], 1)
                    pool.wait_ge(R["MT_out"], a + 1)
                    ln.link(pool.tensor_tensor(U[:, p, :, :], MT[:, :, :], over_heads(keep["levels"][:, 0, :], H), ALU.mult))
                    pool.tensor_tensor(U[:, p, :, :], over_heads(keep["ident"][:, :], H), U[:, p, :, :], ALU.subtract).then_inc(R["U1"], 1)
                    for n in range(5):
                        pool.tensor_tensor(CT[:, p, n, :, :], MT[:, :, :], over_heads(keep["levels"][:, n + 1, :], H), ALU.mult).then_inc(CTs, 1)
                    ln.end()

            pool.memset(qs8[:, 0:H], float(DK) ** -0.5)
            pool.memset(qs8[:, H:8], 1.0).then_inc(qs_in, 1)
            pool.wait_ge(qs_in, 1)
            pool.wait_ge(const_in, 48)
            steps_of(pool, step)

        @block.scalar
        def _(act):
            def step(t, p, i, operands, inverse, output):
                a, b = t + 2, t + 1

                def X_out(n):
                    act.wait_ge(Xs, b * 5 + n + 1)
                    act.copy(flat(X[:, :, :]), BX[:, :]).then_inc(Xo, 1)

                if operands:
                    act.wait_ge(R["x8"], a + 1)
                    act.activation(e8[:, :], x8[:, :], ACT.Exp, scale=-1.0).then_inc(R["e8"], 1)
                if inverse:
                    X_out(0)
                if operands:
                    act.wait_ge(R["qkvT"], a * 3 + 2)
                    since(act, R["kbkd"], a)
                    act.copy(flat(qk[:, 0:H, :]), A0[:, :])
                    act.copy(flat(qk[:, H:2 * H, :]), A1[:, :]).then_inc(R["qk_out"], 1)
                    act.wait_ge(R["u8"], a + 1)
                    act.activation(l4[:, 0:H], u8[:, H:8], ACT.Ln).then_inc(R["ln"], 1)
                if inverse:
                    X_out(1)
                if operands:
                    act.wait_ge(R["gcB"], a + 1)
                    since(act, R["qe"], a)
                    act.activation(flat(EB[:, :, :]), A1[:, :], ACT.Exp).then_inc(R["EB"], 1)
                if inverse:
                    X_out(2)
                if operands:
                    act.wait_ge(R["t8"], a + 1)
                    since(act, R["kbkd"], a)
                    act.activation(ge8[:, :], g8[:, :], ACT.Exp).then_inc(R["ge8"], 1)
                    act.wait_ge(R["DE"], a + 1)
                    act.activation(Dm[:, :, :], Dm[:, :, :], ACT.Exp, scale=-1.0)
                    act.activation(Em[:, :, :], Em[:, :, :], ACT.Exp).then_inc(R["E12"], 1)
                if output:
                    act.wait_ge(R["o_ps"], t + 1)
                    act.copy(flat(o[:, :, :]), BO[:, :]).then_inc(R["o_out"], 1)
                if inverse:
                    X_out(3)
                if operands:
                    act.wait_ge(R["qkT"], a + 1)
                    act.copy(flat(qkT[:, 0:H, :]), A0[:, :])
                    act.copy(flat(qkT[:, H:2 * H, :]), A2[:, :]).then_inc(R["qkT_out"], 1)
                if inverse:
                    X_out(4)
                if operands:
                    act.wait_ge(R["MT"], a + 1)
                    since(act, CTs, a * 5)
                    act.copy(flat(MT[:, :, :]), A2[:, :]).then_inc(R["MT_out"], 1)
                if output:
                    act.wait_ge(R["ogT"], t + 1)
                    act.wait_ge(stored[p], i * 16)
                    act.copy(flat(oT[:, p, :, :]), BS[:, :]).then_inc(R["oT_out"], 1)
                if inverse:
                    act.wait_ge(R["wu"], b + 1)
                    since(act, vns, b * 2)
                    act.copy(flat(wT[:, :, :]), BX[:, :]).then_inc(R["wT_out"], 1)
                    act.copy(flat(u[:, :, :]), BT[:, :]).then_inc(R["u_out"], 1)

            act.wait_ge(const_in, 48)
            act.activation(nea[:, :], nea[:, :], ACT.Exp).then_inc(ea, 1)
            steps_of(act, step)

        @block.tensor
        def _(pe):
            ident, cums = keep["ident"], keep["cums"]

            def step(t, p, i, operands, inverse, output):
                a, b, pb = t + 2, t + 1, 1 - p

                def X_level(n):
                    pe.wait_ge(CTs, b * 5 + n + 1)
                    if n:
                        pe.wait_ge(TUs, b * 5 + n)
                    for h in range(H):
                        mm = pe.matmul(BX[:, h * P:(h + 1) * P], CT[:, pb, n, h, :], T[:, pb, h, :], start=True, stop=True)
                    mm.then_inc(Xs, 1)

                def TU_level(n):
                    pe.wait_ge(Xo, b * 5 + n + 1)
                    for h in range(H):
                        if n < 4:
                            pe.matmul(BT[:, h * P:(h + 1) * P], U[:, pb, h, :], X[:, h, :], start=True, stop=True)
                        mm = pe.matmul(BU[:, h * P:(h + 1) * P], X[:, h, :], U[:, pb, h, :], start=True, stop=True)
                    mm.then_inc(YYs, 1)

                def chunk(c):
                    lo, hi = c * CH, (c + 1) * CH
                    if c:
                        pe.wait_ge(Ss, t * 2 + 1)
                    elif not last(t):
                        pe.wait_ge(Ss, t * 2)
                    for h in range(H):
                        mm = pe.matmul(BS[lo:hi, h * P:(h + 1) * P], wT[:, h, lo:hi], St[:, h, :], start=True, stop=True)
                    mm.then_inc(wSs, 1)
                    for h in range(H):
                        pe.matmul(BO[lo:hi, h * P:(h + 1) * P], qe[:, p, h, lo:hi], St[:, h, :],
                                  start=h == 0, stop=False, skip_group_check=True)

                def into_state(c):
                    lo, hi = c * CH, (c + 1) * CH
                    pe.wait_ge(vns, t * 2 + c + 1)
                    if not (last(t) and c):
                        for h in range(H):
                            mm = pe.matmul(BS[:, h * P:(h + 1) * P], kd[lo:hi, p, h, :], vn[lo:hi, h, :], start=True, stop=True)
                        mm.then_inc(kvs, 1)

                if operands:
                    pe.wait_ge(in_[p], i * 32 + 64)
                    since(pe, R["A"], a)
                    since(pe, R["MT_out"], a)
                    for n, bank in enumerate((A0, A1, A2)):
                        for h in range(H):
                            mm = pe.transpose(bank[:, h * P:(h + 1) * P], sc[:, p, n * H + h, :], ident[:, :])
                        mm.then_inc(R["qkvT"], 1)
                if inverse:
                    pe.wait_ge(R["T1"], b + 1)
                    pe.wait_ge(R["U1"], b + 1)
                    since(pe, R["wT_out"], b)
                    X_level(0)
                if output:
                    pe.wait_ge(R["wT_out"], t + 1)
                    pe.wait_ge(R["qe"], t + 1)
                    pe.wait_ge(R["oT_out"], t)
                    pe.wait_ge(R["o_out"], t)
                    if last(t):
                        pe.wait_ge(state_in, 16)
                    else:
                        pe.wait_ge(s0, 1)
                    chunk(0)
                if inverse:
                    since(pe, R["u_out"], b)
                    TU_level(0)
                if output:
                    into_state(0)
                if inverse:
                    X_level(1)
                if operands:
                    pe.wait_ge(R["qk_out"], a + 1)
                    pe.wait_ge(R["g"], a + 1)
                    pe.matmul(A0[:, 0:H], cums[:, :], g[:, :], start=True, stop=True)
                    pe.matmul(A0[:, H:8], keep["blk"][:, :], g[:, :], start=True, stop=True).then_inc(R["gc"], 1)
                    pe.wait_ge(R["gB"], a + 1)
                    for h in range(H):
                        mm = pe.matmul(A1[:, h * P:(h + 1) * P], gB[:, h, :], cums[:, :], start=True, stop=True)
                    mm.then_inc(R["gcB"], 1)
                if inverse:
                    TU_level(1)
                if output:
                    chunk(1)
                if inverse:
                    X_level(2)
                if output:
                    into_state(1)
                    for h in range(H):
                        mm = pe.matmul(BO[:, h * P:(h + 1) * P], A[:, p, h, :], vn[:, h, :],
                                       start=False, stop=h == H - 1, skip_group_check=True)
                    mm.then_inc(R["o_ps"], 1)
                if inverse:
                    TU_level(2)
                if operands:
                    pe.wait_ge(R["qkn"], a + 1)
                    pe.wait_ge(R["g8"], a + 1)
                    pe.wait_ge(R["v_out"], a + 1)
                    for h in range(2 * H):
                        mm = pe.transpose((A0, A2)[h // H][:, h % H * P:(h % H + 1) * P], qk[:, h, :], ident[:, :])
                    mm.then_inc(R["qkT"], 1)
                if inverse:
                    X_level(3)
                    TU_level(3)
                if operands:
                    pe.wait_ge(R["qkT_out"], a + 1)
                    pe.wait_ge(R["DE"], a + 1)
                    for h in range(H):
                        pe.matmul(A1[:, h * P:(h + 1) * P], qkT[:, H + h, :], qkT[:, H + h, :], start=True, stop=True)
                        mm = pe.matmul(A0[:, h * P:(h + 1) * P], qkT[:, H + h, :], qkT[:, h, :], start=True, stop=True)
                    mm.then_inc(R["kk"], 1)
                if inverse:
                    X_level(4)
                if operands:
                    pe.wait_ge(R["M"], a + 1)
                    for h in range(H):
                        mm = pe.transpose(A2[:, h * P:(h + 1) * P], M[:, h, :], ident[:, :])
                    mm.then_inc(R["MT"], 1)
                if inverse:
                    TU_level(4)
                if output:
                    pe.wait_ge(R["og"], t + 1)
                    if not last(t):
                        pe.wait_ge(Ss, t * 2 + 2)
                    for h in range(H):
                        mm = pe.transpose(BS[:, h * P:(h + 1) * P], o[:, h, :], ident[:, :])
                    mm.then_inc(R["ogT"], 1)
                if inverse:
                    pe.wait_ge(TUs, b * 5 + 5)
                    pe.wait_ge(R["kbkd"], b + 1)
                    for h in range(H):
                        pe.matmul(BX[:, h * P:(h + 1) * P], kb[:, pb, h, :], U[:, pb, h, :], start=True, stop=True)
                        mm = pe.matmul(BT[:, h * P:(h + 1) * P], U[:, pb, h, :], vb[:, pb, h, :], start=True, stop=True)
                    mm.then_inc(R["wu"], 1)

            steps_of(pe, step)

        @block.vector
        def _(dve):
            def step(t, p, i, operands, inverse, output):
                a, b, pb = t + 2, t + 1, 1 - p
                ln, on = Links(dve, link, 7, a), Links(dve, olink, 2, t)

                def subtract(n):
                    dve.wait_ge(YYs, b * 5 + n + 1)
                    if n < 4:
                        dve.tensor_tensor(T[:, pb, :, :], T[:, pb, :, :], heads(BT), ALU.subtract)
                    dve.tensor_tensor(U[:, pb, :, :], U[:, pb, :, :], heads(BU), ALU.subtract).then_inc(TUs, 1)

                def new_values(c):
                    lo, hi = c * CH, (c + 1) * CH
                    dve.wait_ge(wSs, t * 2 + c + 1)
                    dve.tensor_tensor(flat(vn[lo:hi, :, :]), flat(u[lo:hi, :, :]), BS[lo:hi, :], ALU.subtract).then_inc(vns, 1)

                def update(c):
                    if not (last(t) and c):
                        dve.wait_ge(kvs, t * 2 + c + 1)
                        for h in range(H):
                            d = dve.scalar_tensor_tensor(out=St[:, h, :], in0=St[:, h, :], scalar=eS[:, p, h, c:c + 1],
                                                         in1=BS[:, h * P:(h + 1) * P], op0=ALU.mult, op1=ALU.add)
                        d.then_inc(Ss, 1)

                if operands:
                    dve.wait_ge(in_[p], i * 32 + 64)
                    dve.tensor_copy(x8[:, 0:H], ba[:, p, 0:H])
                    ln.link(dve.tensor_tensor(xa[:, :], ba[:, p, H:8], dtb[:, :], ALU.add))
                    dve.scalar_tensor_tensor(out=x8[:, H:8], in0=xa[:, :], scalar=-1.0, in1=xa[:, :], op0=ALU.mult, op1=ALU.max).then_inc(R["x8"], 1)
                    dve.wait_ge(R["e8"], a + 1)
                    dve.tensor_scalar(u8[:, :], e8[:, :], 1.0, None, ALU.add).then_inc(R["u8"], 1)
                    dve.wait_ge(R["u8"], a + 1)
                    since(dve, R["mask"], a)
                    dve.reciprocal(beta[:, :], u8[:, 0:H]).then_inc(R["beta"], 1)
                    ln.link(dve.tensor_scalar(w4[:, 0:H], u8[:, H:8], -1.0, None, ALU.add))
                    ln.link(dve.tensor_tensor(w4[:, 0:H], e8[:, H:8], w4[:, 0:H], ALU.subtract))
                if output:
                    dve.wait_ge(R["u_out"], t + 1)
                    new_values(0)
                if inverse:
                    subtract(0)
                if operands:
                    dve.wait_ge(R["ln"], a + 1)
                    ln.link(dve.tensor_tensor(w4[:, 0:H], w4[:, 0:H], l4[:, 0:H], ALU.add))
                    ln.link(dve.scalar_tensor_tensor(out=w4[:, 0:H], in0=xa[:, :], scalar=0.0, in1=w4[:, 0:H], op0=ALU.max, op1=ALU.add))
                    dve.scalar_tensor_tensor(out=g[:, :], in0=w4[:, 0:H], scalar=-1.0, in1=nea[:, :], op0=ALU.mult, op1=ALU.mult).then_inc(R["g"], 1)
                    dve.wait_ge(R["g"], a + 1)
                    dve.tensor_copy(gB[:, :, :], bc(g[:, :], P)).then_inc(R["gB"], 1)
                if output:
                    update(0)
                if operands:
                    dve.wait_ge(R["qk_out"], a + 1)
                    ln.link(dve.tensor_tensor(sq[:, :, :], qk[:, :, :], qk[:, :, :], ALU.mult))
                    ln.link(dve.tensor_reduce(ss8[:, :], sq[:, :, :], AX, ALU.add))
                    dve.tensor_scalar(ss8[:, :], ss8[:, :], EPS, None, ALU.add).then_inc(R["ss"], 1)
                if inverse:
                    subtract(1)
                if operands:
                    dve.wait_ge(R["qkvT"], a * 3 + 3)
                    dve.wait_ge(R["beta"], a + 1)
                    dve.tensor_tensor(vb[:, p, :, :], heads(A2), bc(beta[:, :], P), ALU.mult).then_inc(R["v_out"], 1)
                if output:
                    new_values(1)
                if operands:
                    dve.wait_ge(R["gc"], a + 1)
                    since(dve, R["ge8"], a)
                    dve.tensor_copy(g8[:, :], A0[:, 0:8]).then_inc(R["g8"], 1)
                    dve.wait_ge(R["g8"], a + 1)
                    dve.wait_ge(R["EB"], a + 1)
                    for h in range(H):
                        dve.tensor_scalar(Dm[:, h, :], A1[:, h * P:(h + 1) * P], g8[:, h:h + 1], 0.0, ALU.subtract, ALU.max)
                        d = dve.tensor_scalar(Em[:, h, :], A1[:, h * P:(h + 1) * P], g8[:, h:h + 1], 0.0, ALU.subtract, ALU.min)
                    d.then_inc(R["DE"], 1)
                    dve.tensor_tensor(g8[:, H:8], g8[:, H:8], g8[:, 0:H], ALU.subtract).then_inc(R["t8"], 1)
                    dve.wait_ge(R["r8"], a + 1)
                    dve.tensor_tensor(qk[:, :, :], qk[:, :, :], bc(r8[:, :], P), ALU.mult).then_inc(R["qkn"], 1)
                if inverse:
                    subtract(2)
                if output:
                    update(1)
                if operands:
                    dve.wait_ge(R["ge8"], a + 1)
                    dve.tensor_tensor(bg[:, :], beta[:, :], ge8[:, 0:H], ALU.mult).then_inc(R["bg"], 1)
                if output:
                    dve.wait_ge(R["o_out"], t + 1)
                    on.link(dve.tensor_tensor(osq[:, :, :], o[:, :, :], o[:, :, :], ALU.mult))
                    on.link(dve.tensor_reduce(os4[:, :], osq[:, :, :], AX, ALU.add))
                    dve.tensor_scalar(os4[:, :], os4[:, :], 1.0 / P, EPS, ALU.mult, ALU.add).then_inc(R["os"], 1)
                    on.end()
                if inverse:
                    subtract(3)
                if operands:
                    dve.wait_ge(R["qkT_out"], a + 1)
                    since(dve, R["o_ps"], a - 1)
                    dve.tensor_copy(eS[:, p, :, :], EB[:, :, CH - 1:P:CH])
                    dve.tensor_tensor(qe[:, p, :, :], qkT[:, 0:H, :], EB[:, :, :], ALU.mult).then_inc(R["qe"], 1)
                    dve.wait_ge(R["kk"], a + 1)
                    dve.wait_ge(R["mask"], a + 1)
                    dve.tensor_tensor(M[:, :, :], heads(A1), Dm[:, :, :], ALU.mult).then_inc(R["M"], 1)
                    dve.tensor_tensor(A[:, p, :, :], heads(A0), Em[:, :, :], ALU.mult).then_inc(R["A"], 1)
                    ln.end()
                if output:
                    dve.wait_ge(R["or4"], t + 1)
                    dve.wait_ge(R["gz"], t + 1)
                    dve.tensor_tensor(o[:, :, :], o[:, :, :], bc(or4[:, :], P), ALU.mult).then_inc(R["normed"], 1)
                    dve.wait_ge(R["normed"], t + 1)
                    dve.tensor_tensor(o[:, :, :], o[:, :, :], gz[:, :, :], ALU.mult).then_inc(R["og"], 1)
                if inverse:
                    subtract(4)

            dve.memset(St[:, :, :], 0.0).then_inc(s0, 1)
            dve.wait_ge(ea, 1)
            steps_of(dve, step)


def keys(nc, io, keep, scr, kT, V, sample):
    G = 4
    tag = "ks" if sample else "kp"
    with ExitStack() as ctx:
        sb, ps, sem = stage(nc, ctx)
        wk = sb(f"{tag}_w", [P, 2, HB * P])
        ck = sb(f"{tag}_ck", [P, 2, G, KL])
        kr = sb(f"{tag}_kr", [P, 2, G, HQ])
        cT = sb(f"{tag}_cT", [P, 2, 4 * P])
        bT = [ps(f"{tag}_t{i}") for i in range(3)]
        bK = [ps(f"{tag}_k{i}") for i in range(4)]
        w_in = sem(f"{tag}_w_in")
        in_ = [sem(f"{tag}_in0"), sem(f"{tag}_in1")]
        tr, tr_out, kr_out = sem(f"{tag}_tr"), sem(f"{tag}_tr_out"), sem(f"{tag}_kr_out")
        mmk, k_a, k_v, zeroed = sem(f"{tag}_mm"), sem(f"{tag}_k_a"), sem(f"{tag}_k_v"), sem(f"{tag}_zero")
        block = ctx.enter_context(nc.Block())
        if sample:
            ckd = io["cache_ckv"][0, 0].rearrange("(g j p) c -> g p j c", p=P, j=G)
            krd = io["cache_kr"][0, 0].rearrange("(g j p) c -> g p j c", p=P, j=G)
        else:
            ckd = io["p_ckv"][0, 0].rearrange("(g j p) c -> g p j c", p=P, j=G)
            krd = io["p_kr"][0, 0].rearrange("(g j p) c -> g p j c", p=P, j=G)

        @block.sync
        def _(sp):
            for k in range(2):
                sp.dma_start(wk[:, k, :], io["w_ukv"][0, k * P:(k + 1) * P, :]).then_inc(w_in, 16)
            sp.wait_ge(zeroed, 1)
            for g in range(4):
                p = g % 2
                if g >= 2:
                    sp.wait_ge(tr, g - 1)
                sp.dma_start(ck[:, p, :, :], ckd[g]).then_inc(in_[p], 16)
                sp.dma_start(kr[:, p, :, NOPE:HQ], krd[g]).then_inc(in_[p], 16)
            if sample:
                sp.wait_ge(tr, 3)
                sp.dma_start(ck[0:DEC, 0, 0, :], io["s_ckv"][0, 0]).then_inc(in_[0], 16)
                sp.dma_start(kr[0:DEC, 0, 0, NOPE:HQ], io["s_kr"][0, 0]).then_inc(in_[0], 16)

        N = 5 if sample else 4

        def parts(g):
            return (1, DEC) if g == 4 else (G, P)

        @block.tensor
        def _(pe):
            pe.wait_ge(w_in, 2 * 16)
            n = 0
            for g in range(N):
                p = g % 2
                tiles, rows = parts(g)
                width = (tiles - 1) * P + rows
                pe.wait_ge(in_[p], (g // 2 + 1) * 32)
                if g:
                    pe.wait_ge(tr_out, g)
                    pe.wait_ge(kr_out, g)
                for j in range(tiles):
                    for k in range(2):
                        pe.transpose(bT[k][:, j * P:j * P + rows], ck[0:rows, p, j, k * P:(k + 1) * P], keep["ident"][0:rows, 0:rows])
                    mm = pe.transpose(bT[2][0:HQ, j * P:j * P + rows], kr[0:rows, p, j, :], keep["ident"][0:rows, 0:rows])
                mm.then_inc(tr, 1)
                pe.wait_ge(tr_out, g + 1)
                for m in range(HB + tiles):
                    b = bK[n % 4]
                    if n >= 4:
                        if n % 2:
                            pe.wait_ge(k_v, (n - 4) // 2 + 1)
                        else:
                            pe.wait_ge(k_a, (n - 4) // 2 + 1)
                    for k in range(2):
                        if m < HB:
                            mm = pe.matmul(b[0:NOPE, 0:width], wk[:, k, m * P:m * P + NOPE], cT[:, k, 0:width], start=k == 0, stop=k == 1)
                        else:
                            j = m - HB
                            mm = pe.matmul(b[0:rows, :].rearrange("p (h e) -> p h e", h=HB), cT[:, k, j * P:j * P + rows],
                                           wk[:, k, :].rearrange("p (h e) -> p h e", h=HB)[:, :, NOPE:P], start=k == 0, stop=k == 1)
                    mm.then_inc(mmk, 1)
                    n += 1

        def drain(eng, copy, odd, done):
            def f(g, n):
                tiles, rows = parts(g)
                width = (tiles - 1) * P + rows
                for m in range(HB + tiles):
                    if n % 2 == odd:
                        eng.wait_ge(mmk, n + 1)
                        b = bK[n % 4]
                        if m < HB:
                            copy(kT[0:NOPE, m, g * G * P:g * G * P + width], b[0:NOPE, 0:width]).then_inc(done, 1)
                        else:
                            copy(V[0:rows, g * G + m - HB, :, 0:DV],
                                 b[0:rows, :].rearrange("p (h e) -> p h e", h=HB)).then_inc(done, 1)
                    n += 1
                return n
            return f

        @block.scalar
        def _(act):
            f, n = drain(act, act.copy, 0, k_a), 0
            for g in range(N):
                tiles, rows = parts(g)
                width = (tiles - 1) * P + rows
                act.wait_ge(tr, g + 1)
                if g:
                    act.wait_ge(mmk, n)
                act.copy(cT[:, 0, 0:width], bT[0][:, 0:width])
                act.copy(cT[:, 1, 0:width], bT[1][:, 0:width]).then_inc(tr_out, 1)
                n = f(g, n)

        @block.vector
        def _(dve):
            dve.memset(kr[:, :, :, 0:NOPE], 0.0).then_inc(zeroed, 1)
            dve.memset(V[:, :, :, DV:DV + 1], 1.0)
            f, n = drain(dve, dve.tensor_copy, 1, k_v), 0
            for g in range(N):
                tiles, rows = parts(g)
                width = (tiles - 1) * P + rows
                dve.wait_ge(tr, g + 1)
                dve.tensor_copy(kT[NOPE:HQ, :, g * G * P:g * G * P + width],
                                bT[2][NOPE:HQ, 0:width].unsqueeze(1).to_broadcast([ROPE, HB, width])).then_inc(kr_out, 1)
                n = f(g, n)


def attention(nc, io, keep, scr, kT, V, sample):
    tag = "s" if sample else "q"
    tiles = [SAMPLE] if sample else list(range(NT))
    with ExitStack() as ctx:
        sb, ps, sem0 = stage(nc, ctx)
        sem = lambda n: sem0(f"{tag}_{n}")
        wu = sb(f"{tag}_wu", [P, 3, HB * HQ])
        cq = sb(f"{tag}_cq", [P, 2, QL])
        cs = sb(f"{tag}_cs", [P, 2, 64])
        zb = sb(f"{tag}_zb", [P, 2, HB * DV])
        cqT = sb(f"{tag}_cqT", [P, 3, P])
        qb = sb(f"{tag}_qb", [P, HB, HQ])
        rt = sb(f"{tag}_rt", [P, 2, HB, ROPE])
        qT = sb(f"{tag}_qT", [P, 2, HB, P])
        qc = sb(f"{tag}_qc", [P, 2, P])
        Pr = sb(f"{tag}_P", [P, 2, 17 * P])
        mx = sb(f"{tag}_mx", [P, 2, 8])
        PT = sb(f"{tag}_PT", [P, 2, 512])
        rc = sb(f"{tag}_rc", [P, 1])
        ob = sb(f"{tag}_ob", [P, 2, HB * DV])
        obT = sb(f"{tag}_obT", [P, 2, 512])
        sps = ps(f"{tag}_sps", [P, 5, 512])
        tps = [ps(f"{tag}_t0"), ps(f"{tag}_t1")]
        ops = ps(f"{tag}_o")
        w_in = sem("w_in")
        q_in, z_in, stored = ([sem(n + "0"), sem(n + "1")] for n in ("q_in", "z_in", "st"))
        cqt, cqt_out, qps, qb_out, roped, qbt, qT_out, zero = (sem(n) for n in ("cqt", "cqt_out", "qps", "qb_out", "roped", "qbt", "qT_out", "zero"))
        qc_r, sc_r, mx_r, exp_r, tr_r, pt_a, pt_v, pv_r, o_r, obt, obt_out, parts, inv, init = (
            sem(n) for n in ("qc", "scores", "max", "exp", "tr", "pt_a", "pt_v", "pv", "o", "obt", "obt_out", "parts", "inv", "init"))
        block = ctx.enter_context(nc.Block())
        scale = float(HQ) ** -0.5
        flat = sps[:, :, :].rearrange("p a b -> p (a b)")
        spare = sps[:, 4, :]

        class Size:

            def __init__(self, t, m, prev):
                self.m = m
                self.n = PAST + DEC if sample else (t + 1) * P
                self.own = 0 if sample else CH
                self.kt = -(-self.n // P)
                self.nb = -(-self.n // 512)
                self.two = self.nb <= 2
                self.ng = -(-self.kt // 4)
                self.na, self.nv = (self.ng + 1) // 2, self.ng // 2
                self.q0 = m * HB
                self.sc0 = prev.sc0 + HB * prev.nb if prev else 0
                self.tr0 = prev.tr0 + HB * prev.ng if prev else 0
                self.a0 = prev.a0 + HB * prev.na if prev else 0
                self.v0 = prev.v0 + HB * prev.nv if prev else 0

            def bank(self, b):
                return 512 * b, min(self.n, 512 * (b + 1))

            def at(self, p):
                return 1024 * p if self.two else 0

        sizes = []
        for m, t in enumerate(tiles):
            sizes.append(Size(t, m, sizes[-1] if sizes else None))
        after = lambda z: sizes[z.m + 1] if z.m + 1 < len(sizes) else None

        def heads(eng, body, between):
            between(0)
            with eng.Fori(0, HB // 4) as i:
                body(i * 2, 0)
                body(i * 2 + 1, 1)
            for h in range(HB // 2, HB):
                between(h)
                body(h, h % 2)

        @block.sync
        def _(sp):
            for k in range(3):
                sp.dma_start(wu[:, k, :], io["w_uq"][0, k * P:(k + 1) * P, :]).then_inc(w_in, 16)

            def load_q(m):
                sp.dma_start(cq[:, m % 2, :], scr["cq"][tiles[m]]).then_inc(q_in[m % 2], 16)
                sp.dma_start(cs[:, m % 2, :], io["c_rope"][tiles[m]]).then_inc(q_in[m % 2], 16)

            def load_z(m):
                sp.dma_start(zb[:, m % 2, :], scr["z"][tiles[m], :, 512:1024]).then_inc(z_in[m % 2], 16)

            def store(m):
                sp.wait_ge(obt_out, m + 1)
                sp.dma_start(scr["ob"][tiles[m]], obT[:, m % 2, :]).then_inc(stored[m % 2], 16)

            load_q(0)
            load_z(0)
            if len(tiles) > 1:
                load_q(1)
            for z in sizes:
                m = z.m
                if after(z):
                    if m:
                        sp.wait_ge(o_r, z.q0)
                    load_z(m + 1)
                if m + 2 < len(tiles):
                    sp.wait_ge(roped, m + 1)
                    load_q(m + 2)
                if m:
                    store(m - 1)
            store(len(tiles) - 1)
            for p in range(min(2, len(tiles))):
                sp.wait_ge(stored[p], (len(tiles) + 1 - p) // 2 * 16)

        @block.gpsimd
        def _(pool):
            for z in sizes:
                for p in range(2):
                    if z.own:
                        u = pool.memset(Pr[0:CH, p, z.n - z.own:z.n], 0.0)
                    elif z.n < z.kt * P:
                        u = pool.memset(Pr[:, p, z.n:z.kt * P], 0.0)
            u.then_inc(zero, 1)
            for z in sizes:
                pool.wait_ge(qT_out, z.m + 1)
                with pool.Fori(0, HB // 2) as i:
                    for p in range(2):
                        pool.wait_ge(sc_r, i * (2 * z.nb) + z.sc0)
                        pool.tensor_copy(qc[0:HQ, p, :], qT[0:HQ, z.m % 2, i * 2 + p, :]).then_inc(qc_r, 1)

        @block.tensor
        def _(pe):
            pe.wait_ge(w_in, 3 * 16)
            ident = keep["ident"]

            def latents(m):
                pe.wait_ge(q_in[m % 2], (m // 2 + 1) * 32)
                if m:
                    pe.wait_ge(qT_out, m)
                for k in range(3):
                    mm = pe.transpose(spare[:, k * P:(k + 1) * P], cq[:, m % 2, k * P:(k + 1) * P], ident[:, :])
                mm.then_inc(cqt, 1)

            def queries(m):
                pe.wait_ge(cqt_out, m + 1)
                for b, bank in ((1, tps[1]), (0, spare)):
                    for k in range(3):
                        mm = pe.matmul(bank[:, 0:384], cqT[:, k, :], wu[:, k, b * 384:(b + 1) * 384], start=k == 0, stop=k == 2)
                    mm.then_inc(qps, 1)

            def queries_T(m):
                pe.wait_ge(roped, m + 1)
                for h in range(HB):
                    mm = pe.transpose((spare, tps[1])[h // 4][0:HQ, h % 4 * P:(h % 4 + 1) * P], qb[:, h, :], ident[:, :])
                mm.then_inc(qbt, 1)

            def outputs_T(m):
                pe.wait_ge(o_r, (m + 1) * HB)
                for k in range(4):
                    mm = pe.transpose(tps[0][:, k * P:(k + 1) * P], ob[:, m % 2, k * P:(k + 1) * P], ident[:, :])
                mm.then_inc(obt, 1)

            def scores(z, h, p):
                pe.wait_ge(qc_r, h + (z.q0 + 1))
                for b in range(z.nb):
                    lo, hi = z.bank(b)
                    if isinstance(h, int) and h == 0:
                        if not z.two:
                            pe.wait_ge(exp_r, z.sc0)
                    elif not z.two:
                        pe.wait_ge(exp_r, h * z.nb + (z.sc0 + b + 1 - z.nb))
                    pe.matmul(flat[:, z.at(p) + lo:z.at(p) + hi], qc[0:HQ, p, :], kT[0:HQ, h, lo:hi],
                              start=True, stop=True).then_inc(sc_r, 1)

            def step(z):
                more = after(z)

                def transposes(h, p, b):
                    n = (h * z.na if b % 2 == 0 else h * z.nv) + ((z.a0 if b % 2 == 0 else z.v0) + b // 2)
                    pe.wait_ge(pt_a if b % 2 == 0 else pt_v, n)
                    if isinstance(h, int) and h == 4 and b == 0 and z.m:
                        pe.wait_ge(obt_out, z.m)
                    if isinstance(h, int) and h == 4 and b == 1 and more:
                        pe.wait_ge(qb_out, 2 * z.m + 3)
                    if isinstance(h, int) and h == 6 and b == 1 and more:
                        pe.wait_ge(qT_out, z.m + 2)
                    for j in range(4 * b, min(4 * b + 4, z.kt)):
                        mm = pe.transpose(tps[b % 2][:, (j % 4) * P:(j % 4 + 1) * P], Pr[:, p, j * P:(j + 1) * P], ident[:, :])
                    mm.then_inc(tr_r, 1)

                def product(h, b):
                    n = (h * z.na if b % 2 == 0 else h * z.nv) + ((z.a0 if b % 2 == 0 else z.v0) + b // 2 + 1)
                    pe.wait_ge(pt_a if b % 2 == 0 else pt_v, n)
                    if b == 0:
                        pe.wait_ge(o_r, h + z.q0)
                    for j in range(4 * b, min(4 * b + 4, z.kt)):
                        rows = min(P, z.n - j * P)
                        mm = pe.matmul(ops[:, 0:DV + 1], PT[0:rows, b % 2, (j % 4) * P:(j % 4 + 1) * P], V[0:rows, j, h, :],
                                       start=j == 0, stop=j == z.kt - 1)
                    if b == z.ng - 1:
                        mm.then_inc(pv_r, 1)

                def body(h, p):
                    if not (isinstance(h, int) and h == HB - 1):
                        scores(z, h + 1, 1 - p)
                    elif more:
                        scores(more, 0, 0)
                    pe.wait_ge(exp_r, (h + 1) * z.nb + z.sc0)
                    transposes(h, p, 0)
                    for b in range(1, z.ng):
                        transposes(h, p, b)
                        product(h, b - 1)
                    product(h, z.ng - 1)

                def between(h):
                    if h == 0 and more:
                        latents(z.m + 1)
                    if h == 4 and z.m:
                        outputs_T(z.m - 1)
                    if h == 4 and more:
                        queries(z.m + 1)
                    if h == 6 and more:
                        queries_T(z.m + 1)

                heads(pe, body, between)

            latents(0)
            queries(0)
            queries_T(0)
            pe.wait_ge(qT_out, 1)
            scores(sizes[0], 0, 0)
            for z in sizes:
                step(z)
            outputs_T(len(tiles) - 1)

        @block.scalar
        def _(act):
            def latents(m):
                act.wait_ge(cqt, m + 1)
                act.copy(cqT[:, :, :], spare[:, 0:384].rearrange("p (k t) -> p k t", k=3)).then_inc(cqt_out, 1)

            def queries(m):
                for n, (b, bank) in enumerate(((1, tps[1]), (0, spare))):
                    act.wait_ge(qps, 2 * m + n + 1)
                    act.mul(qb[:, 4 * b:4 * b + 4, :], bank[:, 0:384].rearrange("p (h c) -> p h c", h=4), scale).then_inc(qb_out, 1)

            def queries_T(m):
                act.wait_ge(qbt, m + 1)
                for b, bank in enumerate((spare, tps[1])):
                    a = act.copy(qT[0:HQ, m % 2, 4 * b:4 * b + 4, :], bank[0:HQ, :].rearrange("p (h t) -> p h t", h=4))
                a.then_inc(qT_out, 1)

            def outputs_T(m):
                act.wait_ge(obt, m + 1)
                if m >= 2:
                    act.wait_ge(stored[m % 2], m // 2 * 16)
                act.copy(obT[:, m % 2, :], tps[0][:, :]).then_inc(obt_out, 1)

            def exps(z, h, p):
                act.wait_ge(mx_r, h + (z.q0 + 1))
                for b in range(z.nb):
                    lo, hi = z.bank(b)
                    at = z.at(p)
                    own = z.own if b == z.nb - 1 else 0
                    a = act.activation(Pr[:, p, lo:hi - own], flat[:, at + lo:at + hi - own], ACT.Exp, bias=mx[:, p, 7:8])
                    if own:
                        a = act.activation(Pr[CH:P, p, hi - own:hi], flat[CH:P, at + hi - own:at + hi], ACT.Exp, bias=mx[CH:P, p, 7:8])
                    a.then_inc(exp_r, 1)

            def step(z):
                more = after(z)

                def body(h, p):
                    for b in range(0, z.ng, 2):
                        act.wait_ge(tr_r, h * z.ng + (z.tr0 + b + 1))
                        w = min(4, z.kt - 4 * b) * P
                        act.copy(PT[:, 0, 0:w], tps[0][:, 0:w]).then_inc(pt_a, 1)
                    if not (isinstance(h, int) and h == HB - 1):
                        exps(z, h + 1, 1 - p)
                    elif more:
                        exps(more, 0, 0)

                def between(h):
                    if h == 0 and more:
                        latents(z.m + 1)
                    if h == 4 and z.m:
                        outputs_T(z.m - 1)
                    if h == 4 and more:
                        queries(z.m + 1)
                    if h == 6 and more:
                        queries_T(z.m + 1)

                heads(act, body, between)

            latents(0)
            queries(0)
            queries_T(0)
            act.wait_ge(zero, 1)
            exps(sizes[0], 0, 0)
            for z in sizes:
                step(z)
            outputs_T(len(tiles) - 1)

        @block.vector
        def _(dve):
            dve.memset(mx[:, :, 0:1], -3.0e38).then_inc(init, 1)
            dve.wait_ge(init, 1)

            def rotate(m):
                dve.wait_ge(qb_out, 2 * m + 2)
                dve.wait_ge(q_in[m % 2], (m // 2 + 1) * 32)
                ck = over_heads(cs[:, m % 2, 0:32], HB)
                dve.tensor_tensor(rt[:, 0, :, :], qb[:, :, NOPE:HQ], ck, ALU.mult)
                dve.tensor_tensor(rt[:, 1, :, 0:16], qb[:, :, NOPE + 16:HQ], over_heads(cs[:, m % 2, 32:48], HB), ALU.mult)
                dve.tensor_tensor(rt[:, 1, :, 16:32], qb[:, :, NOPE:NOPE + 16], over_heads(cs[:, m % 2, 48:64], HB), ALU.mult).then_inc(init, 1)
                dve.wait_ge(init, m + 2)
                dve.tensor_tensor(qb[:, :, NOPE:HQ], rt[:, 0, :, :], rt[:, 1, :, :], ALU.add).then_inc(roped, 1)

            def maxima(z, h, p):
                for b in range(z.nb):
                    lo, hi = z.bank(b)
                    at = z.at(p)
                    own = z.own if b == z.nb - 1 else 0
                    dve.wait_ge(sc_r, h * z.nb + (z.sc0 + b + 1))
                    u = dve.tensor_reduce(mx[:, p, 1 + b:2 + b], flat[:, at + lo:at + hi - own], AX, ALU.max)
                    if own:
                        u = dve.tensor_reduce(mx[CH:P, p, 0:1], flat[CH:P, at + hi - own:at + hi], AX, ALU.max)
                u.then_inc(parts, 1)
                dve.wait_ge(parts, h + (z.q0 + 1))
                dve.tensor_reduce(mx[:, p, 7:8], mx[:, p, 0:1 + z.nb], AX, ALU.max, negate=True).then_inc(mx_r, 1)

            def step(z):
                m, more = z.m, after(z)
                gate = zb[:, m % 2, :].rearrange("p (h e) -> p h e", h=HB)
                out = ob[:, m % 2, :].rearrange("p (h e) -> p h e", h=HB)

                def body(h, p):
                    if not (isinstance(h, int) and h == HB - 1):
                        maxima(z, h + 1, 1 - p)
                    elif more:
                        maxima(more, 0, 0)
                    for b in range(1, z.ng, 2):
                        dve.wait_ge(tr_r, h * z.ng + (z.tr0 + b + 1))
                        w = min(4, z.kt - 4 * b) * P
                        dve.tensor_copy(PT[:, 1, 0:w], tps[1][:, 0:w]).then_inc(pt_v, 1)
                    dve.wait_ge(pv_r, h + (z.q0 + 1))
                    dve.reciprocal(rc[:, :], ops[:, DV:DV + 1]).then_inc(inv, 1)
                    dve.wait_ge(inv, h + (z.q0 + 1))
                    dve.scalar_tensor_tensor(out=out[:, h, :], in0=ops[:, 0:DV], scalar=rc[:, 0:1], in1=gate[:, h, :],
                                             op0=ALU.mult, op1=ALU.mult).then_inc(o_r, 1)

                def between(h):
                    if h == 5 and more:
                        rotate(m + 1)

                dve.wait_ge(z_in[m % 2], (m // 2 + 1) * 16)
                if m >= 2:
                    dve.wait_ge(obt, m - 1)
                heads(dve, body, between)

            rotate(0)
            maxima(sizes[0], 0, 0)
            for z in sizes:
                step(z)


def gate_rows(nc, keep, layer, sb, sem, banks, gB, tag):
    dg = sb(f"{tag}_dg", [P, 2 * KD, P])
    diag, rows, got = sem(f"{tag}_diag"), sem(f"{tag}_rows"), sem(f"{tag}_got")

    def dve_part(dve):
        for n in range(2 * KD):
            c, k = n // KD, n % KD
            u = dve.tensor_scalar(dg[:, n, :], keep["ident"][:, :], keep["gg"][:, layer, c, k:k + 1], None, ALU.mult)
        u.then_inc(diag, 1)
        dve.wait_ge(rows, 1)
        for c in range(2):
            for j in range(2):
                u = dve.tensor_copy(gB[:, c, j * 512:(j + 1) * 512], banks[2 * c + j][:, :])
        u.then_inc(got, 1)
        dve.wait_ge(got, 1)

    def pe_part(pe):
        pe.wait_ge(diag, 1)
        for c in range(2):
            for j in range(2):
                mm = pe.matmul(banks[2 * c + j][:, :], keep["ones"][:, :], dg[:, c * KD + 4 * j:c * KD + 4 * j + 4, :],
                               start=True, stop=True)
        mm.then_inc(rows, 1)
        pe.wait_ge(got, 1)

    return dve_part, pe_part


def close_even(nc, io, keep, scr, w_ahead, ahead_in):
    with ExitStack() as ctx:
        sb, ps, sem = stage(nc, ctx)
        w = sb("c_w", [P, KD, D])
        oc = sb("c_oc", [P, 2, KD, P])
        xt = sb("c_xt", [P, 2, D])
        y = sb("c_y", [P, 2, D])
        junk = sb("c_junk", [P, D])
        gB = sb("c_gB", [P, 2, D])
        ms, rs = sb("c_ms", [P, 1]), sb("c_rs", [P, 1])
        bank = [ps(f"c_b{i}") for i in range(4)]
        w_in, mm_r, y_r, ms_r, rs_r, yn, out = (sem("c_" + n) for n in ("w_in", "mm", "y", "ms", "rs", "yn", "out"))
        in_, stored = [sem("c_in0"), sem("c_in1")], [sem("c_st0"), sem("c_st1")]
        dve_rows, pe_rows = gate_rows(nc, keep, 0, sb, sem, bank, gB, "c")
        block = ctx.enter_context(nc.Block())

        @block.sync
        def _(sp):
            def load(t, p):
                sp.dma_start(oc[:, p, 0:4, :], scr["oa"][t].rearrange("p (k t) -> p k t", k=4)).then_inc(in_[p], 16)
                sp.dma_start(oc[:, p, 4:8, :], scr["ob"][t].rearrange("p (k t) -> p k t", k=4)).then_inc(in_[p], 16)
                if last(t):
                    sp.dma_start(xt[0:DEC, p, :], io["x_sample"][0]).then_inc(in_[p], 16)
                else:
                    sp.dma_start(xt[:, p, :], io["x_prompt"][0].rearrange("(t p) d -> t p d", p=P)[t]).then_inc(in_[p], 16)

            load(0, 0)
            for k in range(KD):
                sp.dma_start(w[:, k, :], io["w_out_e"][0, k * P:(k + 1) * P, :]).then_inc(w_in, 16)

            def step(t, p, i):
                if not last(t):
                    sp.wait_ge(out, t)
                    load(t + 1, 1 - p)
                sp.wait_ge(out, t + 1)
                sp.dma_start(scr["x1"][t], y[:, p, :]).then_inc(stored[p], 16)

            tiles_of(sp, step)
            sp.wait_ge(stored[0], (TILES + 1) // 2 * 16)
            sp.wait_ge(stored[1], TILES // 2 * 16)

        @block.gpsimd
        def _(pool):
            def step(t, p, i):
                pool.wait_ge(ms_r, t + 1)
                pool.tensor_tensor(rs[:, :], ms[:, :], keep["mhalf"][:, 0:1], ALU.pow).then_inc(rs_r, 1)

            pool.wait_ge(w_in, KD * 16)
            for k in range(AHEAD):
                pool.dma_start(w_ahead[:, k, :], io["w_in_o"][0, k * P:(k + 1) * P, :]).then_inc(ahead_in, 16)
            tiles_of(pool, step)

        @block.scalar
        def _(act):
            def step(t, p, i):
                act.wait_ge(mm_r, t + 1)
                act.wait_ge(stored[p], i * 16)
                act.copy(y[:, p, 0:512], bank[2 * p][:, :])
                act.copy(y[:, p, 512:D], bank[2 * p + 1][:, :]).then_inc(y_r, 1)
            tiles_of(act, step)

        @block.tensor
        def _(pe):
            pe_rows(pe)
            pe.wait_ge(w_in, KD * 16)

            def step(t, p, i):
                pe.wait_ge(in_[p], (i + 1) * 48)
                if p or isinstance(t, int):
                    pe.wait_ge(y_r, t - 1)
                else:
                    pe.wait_ge(y_r, t)
                for j in range(2):
                    for k in range(KD):
                        mm = pe.matmul(bank[2 * p + j][:, :], oc[:, p, k, :], w[:, k, j * 512:(j + 1) * 512], start=k == 0, stop=k == KD - 1)
                mm.then_inc(mm_r, 1)
            tiles_of(pe, step)

        @block.vector
        def _(dve):
            dve_rows(dve)

            def step(t, p, i):
                dve.wait_ge(y_r, t + 1)
                dve.tensor_tensor_reduce(junk[:, :], y[:, p, :], y[:, p, :], 1.0 / D, EPS, ALU.mult, ALU.add, ms[:, :]).then_inc(ms_r, 1)
                dve.wait_ge(rs_r, t + 1)
                dve.wait_ge(in_[p], (i + 1) * 48)
                dve.scalar_tensor_tensor(out=y[:, p, :], in0=y[:, p, :], scalar=rs[:, 0:1], in1=gB[:, cond(t), :],
                                         op0=ALU.mult, op1=ALU.mult).then_inc(yn, 1)
                dve.wait_ge(yn, t + 1)
                dve.tensor_tensor(y[:, p, :], y[:, p, :], xt[:, p, :], ALU.add).then_inc(out, 1)
            tiles_of(dve, step)


def in_odd(nc, io, keep, scr, w_ahead, ahead_in):
    with ExitStack() as ctx:
        sb, ps, sem = stage(nc, ctx)
        w_rest = sb("e_w", [P, KD - AHEAD, IN_O])
        w = [w_ahead[:, k, :] if k < AHEAD else w_rest[:, k - AHEAD, :] for k in range(KD)]
        xt = sb("e_xt", [P, 2, D])
        xn = sb("e_xn", [P, D])
        hT = sb("e_hT", [P, 2, KD, P])
        r = sb("e_r", [P, 5, D])
        fg = sb("e_fg", [P, HC, P])
        sg = sb("e_sg", [P, HC, P])
        reset = sb("e_reset", [P, HC, P])
        ms, rs = sb("e_ms", [P, 1]), sb("e_rs", [P, 1])
        xps = [ps("e_x0"), ps("e_x1")]
        bank = [ps(f"e_p{i}") for i in range(4)]
        S = norm_sems(sem, "e")
        w_in, proj, a_out, v_out, fg_r, k_r, lf_r, G_r, init = (
            sem("e_" + n) for n in ("w_in", "proj", "a_out", "v_out", "fg", "k", "lf", "G", "init"))
        st = [sem(f"e_st{j}") for j in range(5)]
        dve_norm, pool_norm, pe_tr, act_hT, dve_hT = norm_transpose(1, keep, xt, xn, ms, rs, hT, xps, S)
        block = ctx.enter_context(nc.Block())
        flat = lambda b: b.rearrange("p h t -> p (h t)")
        part = lambda j, m: r[:, j, m * 512:(m + 1) * 512]

        @block.sync
        def _(sp):
            def load(t, p):
                sp.dma_start(xt[:, p, :], scr["x1"][t]).then_inc(S["x_in"][p], 16)

            load(0, 0)
            for k in range(AHEAD, KD):
                sp.dma_start(w[k], io["w_in_o"][0, k * P:(k + 1) * P, :]).then_inc(w_in, 16)

            def step(t, p, i):
                if not last(t):
                    sp.wait_ge(S["xn"], t)
                    load(t + 1, 1 - p)
                sp.wait_ge(a_out, t * 6 + 2)
                sp.dma_start(scr["qkg"][t, :, 0:D], r[:, 0, :]).then_inc(st[0], 16)
                sp.wait_ge(k_r, t + 1)
                sp.dma_start(scr["qkg"][t, :, D:2 * D], r[:, 1, :]).then_inc(st[1], 16)
                sp.wait_ge(v_out, t * 2 + 2)
                sp.dma_start(scr["iz"][t, :, 0:D], r[:, 3, :]).then_inc(st[3], 16)
                sp.wait_ge(G_r, t + 1)
                sp.dma_start(scr["qkg"][t, :, 2 * D:3 * D], r[:, 2, :]).then_inc(st[2], 16)
                sp.wait_ge(a_out, t * 6 + 6)
                sp.dma_start(scr["iz"][t, :, D:2 * D], r[:, 4, :]).then_inc(st[4], 16)

            tiles_of(sp, step)
            for j in range(5):
                sp.wait_ge(st[j], TILES * 16)

        @block.gpsimd
        def _(pool):
            def step(t, p, i):
                if not last(t):
                    pool_norm(pool, t + 1)
            pool_norm(pool, 0)
            tiles_of(pool, step)

        @block.scalar
        def _(act):
            def drain(t, n, dst, func):
                act.wait_ge(proj, t * 8 + n + 1)
                act.activation(dst, bank[n % 4][:, :], func).then_inc(a_out, 1)

            def step(t, p, i):
                act.wait_ge(st[0], t * 16)
                drain(t, 0, part(0, 0), ACT.Silu)
                drain(t, 1, part(0, 1), ACT.Silu)
                act.wait_ge(fg_r, t)
                drain(t, 2, flat(sg[:, 0:4, :]), ACT.Sigmoid)
                drain(t, 3, flat(sg[:, 4:8, :]), ACT.Sigmoid)
                if not last(t):
                    act_hT(act, t + 1, 1 - p)
                act.wait_ge(k_r, t + 1)
                act.activation(flat(fg[:, :, :]), flat(fg[:, :, :]), ACT.Ln).then_inc(lf_r, 1)
                act.wait_ge(st[4], t * 16)
                drain(t, 6, part(4, 0), ACT.Silu)
                drain(t, 7, part(4, 1), ACT.Silu)

            act_hT(act, 0, 0)
            tiles_of(act, step)

        @block.tensor
        def _(pe):
            def step(t, p, i):
                pe.wait_ge(S["hT_a"], t + 1)
                pe.wait_ge(S["hT_v"], t + 1)
                for n in range(8):
                    if n in (0, 1):
                        pe.wait_ge(v_out, t * 2)
                    elif n in (2, 3):
                        pe.wait_ge(a_out, t * 6)
                    else:
                        pe.wait_ge(a_out, t * 6 + (n - 3))
                    for c in range(4):
                        for k in range(KD):
                            if n < 4:
                                a = n * 512 + c * P
                                mm = pe.matmul(bank[n % 4][:, c * P:(c + 1) * P], w[k][:, a:a + P], hT[:, p, k, :], start=k == 0, stop=k == KD - 1)
                            elif c == 0:
                                mm = pe.matmul(bank[n % 4][:, :], hT[:, p, k, :], w[k][:, n * 512:(n + 1) * 512], start=k == 0, stop=k == KD - 1)
                    mm.then_inc(proj, 1)
                    if n == 3 and not last(t):
                        pe_tr(pe, t + 1)

            pe_tr(pe, 0)
            pe.wait_ge(ahead_in, 16 * AHEAD)
            pe.wait_ge(w_in, 16 * (KD - AHEAD))
            tiles_of(pe, step)

        @block.vector
        def _(dve):
            def step(t, p, i):
                if not last(t):
                    dve_norm(dve, t + 1, 1 - p, i + p)
                dve.wait_ge(a_out, t * 6 + 4)
                dve.wait_ge(G_r, t)
                for h in range(HC):
                    u = dve.tensor_scalar(fg[:, h, :], sg[:, h, :], keep["lb"][:, 1, h:h + 1], keep["lb"][:, 0, h:h + 1], ALU.mult, ALU.add)
                u.then_inc(fg_r, 1)
                dve.wait_ge(fg_r, t + 1)
                dve.wait_ge(st[1], t * 16)
                dve.tensor_scalar(r[:, 1, :], flat(fg[:, :, :]), -1.0, 1.0, ALU.mult, ALU.add).then_inc(k_r, 1)
                if not last(t):
                    dve_hT(dve, t + 1, 1 - p)
                dve.wait_ge(st[3], t * 16)
                for n in (4, 5):
                    dve.wait_ge(proj, t * 8 + n + 1)
                    dve.tensor_copy(part(3, n - 4), bank[n % 4][:, :]).then_inc(v_out, 1)
                dve.wait_ge(lf_r, t + 1)
                dve.wait_ge(st[2], t * 16)
                dve.tensor_tensor_scan(r[:, 2, :], flat(reset[:, :, :]), flat(fg[:, :, :]), 0.0, ALU.mult, ALU.add).then_inc(G_r, 1)

            dve.memset(reset[:, :, :], 1.0).then_inc(init, 1)
            dve.wait_ge(init, 1)
            dve.memset(reset[:, :, :].rearrange("p h (c t) -> p (h c) t", t=CH)[:, :, 0:1], 0.0).then_inc(init, 1)
            dve.wait_ge(init, 2)
            dve_norm(dve, 0, 0, 0)
            dve_hT(dve, 0, 0)
            tiles_of(dve, step)


def hgrn(nc, io, keep, scr):
    H = HC
    with ExitStack() as ctx:
        sb, ps, sem = stage(nc, ctx)
        w = sb("h_w", [P, KD, D])
        rq = sb("h_rq", [P, 2, 3, H, P])
        rz = sb("h_rz", [P, 2, 2, H, P])
        gB = sb("h_gB", [P, 2, D])
        gnc = sb("h_gnc", [P, P])
        EG = sb("h_EG", [P, 2, H, P])
        DL, EL = sb("h_DL", [P, 2, 512]), sb("h_EL", [P, 2, 2, 512])
        KLv, QLv = sb("h_KL", [P, 2, H, P]), sb("h_QL", [P, 2, 512])
        A = sb("h_A", [P, 2, H, P])
        kdT, kd, qe = sb("h_kdT", [P, H, P]), sb("h_kd", [P, 2, H, P]), sb("h_qe", [P, 2, H, P])
        St = sb("h_S", [P, H, P])
        o, osq = sb("h_o", [P, H, P]), sb("h_osq", [P, H, P])
        os8, or8 = sb("h_os8", [P, 8]), sb("h_or8", [P, 8])
        oT = sb("h_oT", [P, H, P])
        xt, y = sb("h_xt", [P, D]), sb("h_y", [P, D])
        ms, rs, hold = sb("h_ms", [P, 1]), sb("h_rs", [P, 1]), sb("h_hold", [P, 6])
        bank = [ps(f"h_b{i}") for i in range(8)]
        names = "EG fin tail kd kdt kd_out dq dg qe o_ps o_out gate on sum os or normed og ogt oT_out mm y ms rs yn out".split()
        R = {n: sem("h_" + n) for n in names}
        dls, els, kqs, scs, Ac = (sem("h_" + n) for n in ("dl", "el", "kq", "sc", "Ac"))
        Ss, kSs, qSs = sem("h_Ss"), sem("h_kSs"), sem("h_qSs")
        q_in, z_in = [sem("h_q_in0"), sem("h_q_in1")], [sem("h_z_in0"), sem("h_z_in1")]
        x_in, stored = sem("h_x_in"), sem("h_stored")
        const_in, state_out, state_in, init = sem("h_const"), sem("h_so"), sem("h_si"), sem("h_init")
        dve_rows, pe_rows = gate_rows(nc, keep, 1, sb, sem, bank, gB, "h")
        block = ctx.enter_context(nc.Block())
        flat = lambda b: b.rearrange("p h t -> p (h t)")
        heads4 = lambda b: b[:, :].rearrange("p (h t) -> p h t", h=4)
        state = lambda ap: ap.rearrange("h d e -> d h e")

        def halves(ap, b):
            return ap.rearrange("p h (n a b) -> p (h n) a b", a=2, b=b)

        @block.sync
        def _(sp):
            sp.dma_start(gnc[:, :], io["g_norm_c"][0:1, :].to_broadcast([P, P])).then_inc(const_in, 16)

            def load_q(t, p, ahead=0):
                sp.dma_start(rq[:, p, :, :, :], scr["qkg"][ahead:][t].rearrange("p (j h t) -> p j h t", j=3, h=H)).then_inc(q_in[p], 16)

            def load_z(t, p, ahead=0):
                sp.dma_start(rz[:, p, :, :, :], scr["iz"][ahead:][t].rearrange("p (j h t) -> p j h t", j=2, h=H)).then_inc(z_in[p], 16)

            def store_y(t):
                sp.wait_ge(R["out"], t + 1)
                if last(t):
                    sp.dma_start(io["y_sample"][0], y[0:DEC, :]).then_inc(stored, 16)
                else:
                    sp.dma_start(io["y_prompt"][0].rearrange("(t p) d -> t p d", p=P)[t], y[:, :]).then_inc(stored, 16)

            load_q(0, 0)
            load_z(0, 0)
            load_q(1, 1)
            sp.dma_start(w[:, :, :], io["w_out_o"][0].rearrange("(k p) n -> p k n", p=P)).then_inc(const_in, 16)

            def step(t, p, i, first=False):
                if not (isinstance(t, int) and t + 2 > SAMPLE):
                    sp.wait_ge(R["qe"], t + 1)
                    sp.wait_ge(Ac, t * 6 + 6)
                    load_q(t, p, ahead=2)
                if not last(t):
                    sp.wait_ge(R["og"], t)
                    sp.wait_ge(R["o_ps"], t)
                    load_z(t, 1 - p, ahead=1)
                if isinstance(t, int) and t == NT - 1:
                    sp.wait_ge(Ss, 2 * NT)
                    sp.dma_start(state(io["p_hgrn"][0, 0]), St[:, :, :]).then_inc(state_out, 16)
                    sp.wait_ge(state_out, 16)
                    sp.wait_ge(R["o_ps"], NT)
                    sp.dma_start(St[:, :, :], state(io["state_hgrn"][0, 0])).then_inc(state_in, 16)
                if last(t):
                    sp.wait_ge(Ss, 2 * NT + 1)
                    sp.dma_start(state(io["s_hgrn"][0, 0]), St[:, :, :]).then_inc(state_out, 16)
                if not (isinstance(t, int) and t < 2):
                    store_y(t - 2)
                if not first:
                    sp.dma_start(xt[:, :], scr["x1"][t - 1]).then_inc(x_in, 16)

            after_first(sp, step)
            store_y(SAMPLE - 1)
            sp.dma_start(xt[:, :], scr["x1"][SAMPLE]).then_inc(x_in, 16)
            store_y(SAMPLE)
            sp.wait_ge(state_out, 32)
            sp.wait_ge(stored, TILES * 16)

        @block.gpsimd
        def _(pool):
            def inner(u, p, i):
                pool.wait_ge(R["EG"], u + 1)
                pool.tensor_tensor(qe[:, p, :, :], rq[:, p, 0, :, :], EG[:, p, :, :], ALU.mult).then_inc(R["qe"], 1)

            def close(t):
                pool.wait_ge(R["ms"], t + 1)
                pool.tensor_tensor(rs[:, :], ms[:, :], keep["mhalf"][:, 0:1], ALU.pow).then_inc(R["rs"], 1)

            def step(t, p, i, first=False):
                pool.wait_ge(z_in[p], (i + 1) * 16)
                pool.tensor_tensor(rz[:, p, 1, :, :], rz[:, p, 1, :, :], over_heads(gnc[:, :], H), ALU.mult).then_inc(R["gate"], 1)
                if not last(t):
                    pool.wait_ge(R["o_ps"], t)
                    inner(t + 1, 1 - p, i + p)
                if not (isinstance(t, int) and t < 2):
                    close(t - 2)
                pool.wait_ge(R["os"], t + 1)
                pool.tensor_tensor(or8[:, :], os8[:, :], keep["mhalf"][:, :], ALU.pow).then_inc(R["or"], 1)

            pool.wait_ge(const_in, 32)
            inner(0, 0, 0)
            after_first(pool, step)
            close(SAMPLE - 1)
            close(SAMPLE)

        @block.scalar
        def _(act):
            def decays(u, p, i):
                act.wait_ge(R["tail"], u + 1)
                act.activation(flat(kdT[:, :, :]), flat(kdT[:, :, :]), ACT.Exp).then_inc(R["fin"], 1)
                act.activation(flat(EG[:, p, :, :]), flat(rq[:, p, 2, :, :]), ACT.Exp).then_inc(R["EG"], 1)

            def level(u, n):
                act.wait_ge(dls, u * 6 + n + 1)
                act.activation(EL[:, n % 2, :, :], DL[:, :, :], ACT.Exp).then_inc(els, 1)

            def kd_rows(u, p):
                act.wait_ge(R["kdt"], u + 1)
                act.copy(flat(kd[:, p, 0:4, :]), bank[4][:, :])
                act.copy(flat(kd[:, p, 4:8, :]), bank[5][:, :]).then_inc(R["kd_out"], 1)

            def close(t):
                act.wait_ge(R["mm"], t + 1)
                act.wait_ge(stored, t * 16)
                act.copy(y[:, 0:512], bank[4][:, :])
                act.copy(y[:, 512:D], bank[5][:, :]).then_inc(R["y"], 1)

            def step(t, p, i, first=False):
                more = not last(t)
                if more:
                    act.wait_ge(Ss, t * 2)
                    decays(t + 1, 1 - p, i + p)
                if more:
                    level(t + 1, 0)
                    kd_rows(t + 1, 1 - p)
                    level(t + 1, 1)
                    level(t + 1, 2)
                act.wait_ge(R["o_ps"], t + 1)
                act.copy(flat(o[:, 0:4, :]), bank[6][:, :])
                act.copy(flat(o[:, 4:8, :]), bank[7][:, :]).then_inc(R["o_out"], 1)
                if more:
                    level(t + 1, 3)
                    level(t + 1, 4)
                if more:
                    level(t + 1, 5)
                act.wait_ge(R["ogt"], t + 1)
                act.wait_ge(R["mm"], t)
                act.copy(flat(oT[:, 0:4, :]), bank[2][:, :])
                act.copy(flat(oT[:, 4:8, :]), bank[3][:, :]).then_inc(R["oT_out"], 1)
                if not first:
                    close(t - 1)

            decays(0, 0, 0)
            level(0, 0)
            kd_rows(0, 0)
            for n in range(1, 6):
                level(0, n)
            after_first(act, step)
            close(SAMPLE)

        @block.tensor
        def _(pe):
            pe_rows(pe)
            pe.wait_ge(const_in, 32)
            pe.wait_ge(init, 1)
            ident = keep["ident"]

            def diagonal(u, p, i):
                pe.wait_ge(q_in[p], (i + 1) * 16)
                pe.wait_ge(R["kd_out"], u)
                if not (isinstance(u, int) and u < 3):
                    pe.wait_ge(R["y"], u - 2)
                for h in range(H):
                    mm = pe.matmul(bank[4 + h // 4][:, h % 4 * P:(h % 4 + 1) * P], rq[:, p, 1, h, :], rq[:, p, 0, h, :], start=True, stop=True)
                mm.then_inc(R["dq"], 1)

            def kd_transposes(u):
                pe.wait_ge(R["kd"], u + 1)
                pe.wait_ge(R["dg"], u + 1)
                for h in range(H):
                    mm = pe.transpose(bank[4 + h // 4][:, h % 4 * P:(h % 4 + 1) * P], kdT[:, h, :], ident[:, :])
                mm.then_inc(R["kdt"], 1)

            def level(u, n):
                pe.wait_ge(kqs, u * 6 + n + 1)
                if n >= 2:
                    pe.wait_ge(Ac, u * 6 + n - 1)
                else:
                    pe.wait_ge(Ac, u * 6)
                for h in range(H):
                    mm = pe.matmul(bank[n % 2][:, h * CH:(h + 1) * CH], KLv[:, n % 2, h, :], QLv[:, n % 2, h * CH:(h + 1) * CH],
                                   start=True, stop=True)
                mm.then_inc(scs, 1)

            def chunk(t, p, c):
                lo, hi = c * CH, (c + 1) * CH
                if c:
                    pe.wait_ge(Ss, t * 2 + 1)
                elif not last(t):
                    pe.wait_ge(Ss, t * 2)
                else:
                    pe.wait_ge(state_in, 16)
                for h in range(H):
                    mm = pe.matmul(bank[6 + h // 4][lo:hi, h % 4 * P:(h % 4 + 1) * P], qe[:, p, h, lo:hi], St[:, h, :],
                                   start=h % 4 == 0, stop=False, skip_group_check=True)
                mm.then_inc(qSs, 1)
                if not (last(t) and c):
                    for h in range(H):
                        mm = pe.matmul(bank[2 + h // 4][:, h % 4 * P:(h % 4 + 1) * P], kd[lo:hi, p, h, :], rz[lo:hi, p, 0, h, :],
                                       start=True, stop=True)
                    mm.then_inc(kSs, 1)

            PIECES = ((0, 0, KD // 2), (0, KD // 2, KD), (1, 0, KD // 2), (1, KD // 2, KD - 2), (1, KD - 2, KD))

            def project(t, n):
                j, k0, k1 = PIECES[n]
                if n == 0:
                    pe.wait_ge(R["oT_out"], t + 1)
                    if isinstance(t, int) and t + 1 >= SAMPLE:
                        pe.wait_ge(R["y"], t)
                    else:
                        pe.wait_ge(R["kd_out"], t + 3)
                for k in range(k0, k1):
                    mm = pe.matmul(bank[4 + j][:, :], oT[:, k, :], w[:, k, j * 512:(j + 1) * 512], start=k == 0, stop=k == KD - 1)
                if k1 == KD and j:
                    mm.then_inc(R["mm"], 1)

            def step(t, p, i, first=False):
                more = not last(t)
                if more:
                    diagonal(t + 1, 1 - p, i + p)
                pe.wait_ge(z_in[p], (i + 1) * 16)
                pe.wait_ge(R["oT_out"], t)
                pe.wait_ge(R["o_out"], t)
                pe.wait_ge(R["kd_out"], t + 1)
                pe.wait_ge(R["qe"], t + 1)
                chunk(t, p, 0)
                if more:
                    kd_transposes(t + 1)
                    level(t + 1, 0)
                if not first:
                    project(t - 1, 0)
                chunk(t, p, 1)
                pe.wait_ge(Ac, t * 6 + 6)
                for h in range(H):
                    mm = pe.matmul(bank[6 + h // 4][:, h % 4 * P:(h % 4 + 1) * P], A[:, p, h, :], rz[:, p, 0, h, :],
                                   start=False, stop=h % 4 == 3, skip_group_check=True)
                mm.then_inc(R["o_ps"], 1)
                for n in range(1, 4):
                    if more:
                        level(t + 1, n)
                    if not first:
                        project(t - 1, n)
                if more:
                    pe.wait_ge(Ss, t * 2 + 2)
                else:
                    pe.wait_ge(Ss, t * 2 + 1)
                pe.wait_ge(R["og"], t + 1)
                for h in range(H):
                    mm = pe.transpose(bank[2 + h // 4][:, h % 4 * P:(h % 4 + 1) * P], o[:, h, :], ident[:, :])
                mm.then_inc(R["ogt"], 1)
                if more:
                    level(t + 1, 4)
                if not first:
                    project(t - 1, 4)
                if more:
                    level(t + 1, 5)

            diagonal(0, 0, 0)
            kd_transposes(0)
            for n in range(6):
                level(0, n)
            after_first(pe, step)
            for n in range(len(PIECES)):
                project(SAMPLE, n)

        @block.vector
        def _(dve):
            dve_rows(dve)
            dve.memset(KLv[:, :, :, :], 0.0)
            dve.memset(St[:, :, :], 0.0).then_inc(init, 1)
            dve.wait_ge(init, 1)

            def tail(u, p, i):
                dve.wait_ge(q_in[p], (i + 1) * 16)
                dve.wait_ge(R["kdt"], u)
                Gc = rq[:, p, 2, :, :].rearrange("p h (c t) -> p (h c) t", t=CH)
                dve.tensor_tensor(kdT[:, :, :].rearrange("p h (c t) -> p (h c) t", t=CH), Gc[:, :, CH - 1:CH].to_broadcast([P, 2 * H, CH]), Gc,
                                  ALU.subtract).then_inc(R["tail"], 1)

            def differences(u, p, n):
                b = LEVELS[n]
                g = halves(rq[:, p, 2, :, :], b)
                mid = g[:, :, 0, b - 1:b].to_broadcast([P, 512 // b, b])
                dve.tensor_tensor(DL[:, 0, :].rearrange("p (n b) -> p n b", b=b), mid, g[:, :, 0, :], ALU.subtract)
                dve.tensor_tensor(DL[:, 1, :].rearrange("p (n b) -> p n b", b=b), g[:, :, 1, :], mid, ALU.subtract).then_inc(dls, 1)

            def diagonal(u, p):
                dve.wait_ge(R["dq"], u + 1)
                for j in range(2):
                    v = dve.tensor_tensor(A[:, p, 4 * j:4 * j + 4, :], heads4(bank[4 + j]), over_heads(keep["ident"][:, :], 4), ALU.mult)
                v.then_inc(R["dg"], 1)
                dve.wait_ge(R["fin"], u + 1)
                dve.tensor_tensor(kdT[:, :, :], rq[:, p, 1, :, :], kdT[:, :, :], ALU.mult).then_inc(R["kd"], 1)

            def operands(u, p, n):
                b = LEVELS[n]
                dve.wait_ge(els, u * 6 + n + 1)
                if n >= 2:
                    dve.wait_ge(scs, u * 6 + n - 1)
                dve.tensor_tensor(halves(KLv[:, n % 2, :, :], b)[:, :, 0, :], halves(rq[:, p, 1, :, :], b)[:, :, 0, :],
                                  EL[:, n % 2, 0, :].rearrange("p (n b) -> p n b", b=b), ALU.mult)
                dve.tensor_tensor(QLv[:, n % 2, :].rearrange("p (n b) -> p n b", b=b), halves(rq[:, p, 0, :, :], b)[:, :, 1, :],
                                  EL[:, n % 2, 1, :].rearrange("p (n b) -> p n b", b=b), ALU.mult).then_inc(kqs, 1)

            def take(u, p, n):
                b = LEVELS[n]
                dve.wait_ge(scs, u * 6 + n + 1)
                if n:
                    dve.wait_ge(Ac, u * 6 + n)
                dve.memset(hold[:, n:n + 1], 0.0)
                dst = A[:, p, :, :].rearrange("p h (n a b) -> p h n a b", a=2, b=b)[:, :, :, 1, :]
                src = bank[n % 2][:, :].rearrange("p (h n b) -> p h n b", h=H, b=b)
                mask = keep["levels"][:, n, :].bitcast(I32).rearrange("p (n a b) -> p n a b", a=2, b=b)[:, :, 1, :]
                dve.copy_predicated(dst, mask.unsqueeze(1).to_broadcast([P, H, CH // b, b]), src).then_inc(Ac, 1)

            def update(t, p, c):
                if not (last(t) and c):
                    dve.wait_ge(qSs, t * 2 + c + 1)
                    dve.wait_ge(kSs, t * 2 + c + 1)
                    for h in range(H):
                        v = dve.scalar_tensor_tensor(out=St[:, h, :], in0=St[:, h, :], scalar=EG[:, p, h, (c + 1) * CH - 1:(c + 1) * CH],
                                                     in1=bank[2 + h // 4][:, h % 4 * P:(h % 4 + 1) * P], op0=ALU.mult, op1=ALU.add)
                    v.then_inc(Ss, 1)

            def slot(u, p, n):
                operands(u, p, n)
                if n < 5:
                    differences(u, p, n + 1)
                if n:
                    take(u, p, n - 1)

            def squares(t):
                dve.wait_ge(R["o_out"], t + 1)
                dve.tensor_tensor(osq[:, :, :], o[:, :, :], o[:, :, :], ALU.mult).then_inc(R["on"], 1)
                dve.wait_ge(R["on"], t + 1)
                dve.tensor_reduce(os8[:, :], osq[:, :, :], AX, ALU.add).then_inc(R["sum"], 1)
                dve.wait_ge(R["sum"], t + 1)
                dve.tensor_scalar(os8[:, :], os8[:, :], 1.0 / P, EPS, ALU.mult, ALU.add).then_inc(R["os"], 1)

            def gated(t, p):
                dve.wait_ge(R["or"], t + 1)
                dve.tensor_tensor(o[:, :, :], o[:, :, :], bc(or8[:, :], P), ALU.mult).then_inc(R["normed"], 1)
                dve.wait_ge(R["normed"], t + 1)
                dve.wait_ge(R["gate"], t + 1)
                dve.tensor_tensor(o[:, :, :], o[:, :, :], rz[:, p, 1, :, :], ALU.mult).then_inc(R["og"], 1)

            def close(t):
                dve.wait_ge(R["y"], t + 1)
                dve.tensor_tensor_reduce(flat(osq[:, :, :]), y[:, :], y[:, :], 1.0 / D, EPS, ALU.mult, ALU.add, ms[:, :]).then_inc(R["ms"], 1)
                dve.wait_ge(R["rs"], t + 1)
                dve.wait_ge(x_in, (t + 1) * 16)
                dve.scalar_tensor_tensor(out=y[:, :], in0=y[:, :], scalar=rs[:, 0:1], in1=gB[:, cond(t), :],
                                         op0=ALU.mult, op1=ALU.mult).then_inc(R["yn"], 1)
                dve.wait_ge(R["yn"], t + 1)
                dve.tensor_tensor(y[:, :], y[:, :], xt[:, :], ALU.add).then_inc(R["out"], 1)

            def step(t, p, i, first=False):
                u, pu = t + 1, 1 - p
                more = not last(t)
                if more:
                    tail(u, pu, i + p)
                    differences(u, pu, 0)
                take(t, p, 5)
                if more:
                    dve.wait_ge(R["o_ps"], t)
                    diagonal(u, pu)
                    slot(u, pu, 0)
                update(t, p, 0)
                if more:
                    slot(u, pu, 1)
                update(t, p, 1)
                if not (isinstance(t, int) and t < 2):
                    close(t - 2)
                if more:
                    slot(u, pu, 2)
                squares(t)
                if more:
                    slot(u, pu, 3)
                gated(t, p)
                if more:
                    slot(u, pu, 4)
                    slot(u, pu, 5)

            tail(0, 0, 0)
            differences(0, 0, 0)
            diagonal(0, 0)
            for n in range(6):
                slot(0, 0, n)
            after_first(dve, step)
            close(SAMPLE - 1)
            close(SAMPLE)


def program(nc, io):
    scr = {n: nc.dram_tensor("scr_" + n, list(s), F32, kind="Internal").ap() for n, s in (
        ("qkv", (TILES, P, NCT, P)), ("z", (TILES, P, D)), ("ba", (TILES, P, 8)), ("cq", (TILES, P, QL)),
        ("oa", (TILES, P, 512)), ("ob", (TILES, P, 512)), ("x1", (TILES, P, D)), ("qkg", (TILES, P, 3 * D)), ("iz", (TILES, P, 2 * D)))}
    with ExitStack() as ctx:
        keep = {n: ctx.enter_context(nc.sbuf_tensor("k_" + n, list(s), F32)) for n, s in (
            ("ident", (P, P)), ("cums", (P, P)), ("strict", (P, P)), ("blk", (P, P)), ("low1", (P, P)),
            ("levels", (P, 6, P)), ("ones", (P, P)), ("mhalf", (P, 8)), ("lb", (P, 2, KD)),
            ("mA", (P, 2, 2, KD)), ("mB", (P, 2, 2, KD)), ("gg", (P, 2, 2, KD)))}
        even = ExitStack()
        sb, _, sem = stage(nc, even)
        w_even, even_in = sb("w_even", [P, KD, IN_E]), sem("even_in")
        modulation(nc, io, keep, w_even, even_in)
        in_even(nc, io, keep, scr, w_even, even_in)
        even.close()
        delta(nc, io, keep, scr)
        with ExitStack() as kv:
            kT = kv.enter_context(nc.sbuf_tensor("kT", [P, HB, PAST + DEC], F32))
            V = kv.enter_context(nc.sbuf_tensor("V", [P, NT + 1, HB, DV + 1], F32))
            for sample in (False, True):
                keys(nc, io, keep, scr, kT, V, sample)
                attention(nc, io, keep, scr, kT, V, sample)
        with ExitStack() as odd:
            sb, _, sem = stage(nc, odd)
            w_ahead, ahead_in = sb("w_ahead", [P, AHEAD, IN_O]), sem("ahead_in")
            close_even(nc, io, keep, scr, w_ahead, ahead_in)
            in_odd(nc, io, keep, scr, w_ahead, ahead_in)
        hgrn(nc, io, keep, scr)


INS = ("x_prompt x_sample c_prompt c_sample cache_ckv cache_kr state_delta state_conv state_hgrn w_ada b_ada g_pre g_post "
       "w_in_e conv_w a_log dt_bias g_norm_a g_q w_uq g_kv w_ukv w_out_e w_in_o lb_logits g_norm_c w_out_o").split()
OUTS = (("y_prompt", (1, SEQ, D)), ("y_sample", (1, DEC, D)), ("p_delta", (1, 1, HA, DK, DK)), ("p_conv", (1, 1, 3, QKV)),
        ("p_ckv", (1, 1, SEQ, KL)), ("p_kr", (1, 1, SEQ, ROPE)), ("p_hgrn", (1, 1, HC, P, P)),
        ("s_delta", (1, 1, HA, DK, DK)), ("s_conv", (1, 1, 3, QKV)), ("s_ckv", (1, 1, DEC, KL)), ("s_kr", (1, 1, DEC, ROPE)),
        ("s_hgrn", (1, 1, HC, P, P)))


def constants():
    import numpy as np
    a = np.arange(P)
    same = (a[:, None] // CH) == (a[None, :] // CH)
    levels = np.zeros((P, 6, P), np.float32)
    for n, b in enumerate(LEVELS):
        block = (a[:, None] // (2 * b)) == (a[None, :] // (2 * b))
        levels[:, n, :] = block & (a[:, None] // b % 2 == 0) & (a[None, :] // b % 2 == 1)
    half = ROPE // 2
    inv = (np.float32(10000.0) ** (-np.arange(half, dtype=np.float32) / np.float32(half))).astype(np.float32)
    ang = np.arange(TILES * P, dtype=np.float32)[:, None] * inv[None, :]
    cos, sin = np.cos(ang).astype(np.float32), np.sin(ang).astype(np.float32)
    rope = np.concatenate([cos, cos, -sin, sin], axis=1).reshape(TILES, P, 64)
    return {
        "c_ident": np.eye(P, dtype=np.float32),
        "c_cums": (same & (a[:, None] <= a[None, :])).astype(np.float32),
        "c_blk": same.astype(np.float32),
        "c_strict": (same & (a[:, None] > a[None, :])).astype(np.float32),
        "c_low1": np.ascontiguousarray(levels[:, 0, :].T),
        "c_levels": levels,
        "c_rope": rope,
    }


def kernel(**inputs):
    import numpy as np
    import concourse.bacc as bacc
    from concourse.bass_utils import run_bass_kernel_spmd

    nc = bacc.Bacc("TRN2", target_bir_lowering=False, num_devices=1)
    arrays = {n: np.ascontiguousarray(inputs[n]) for n in INS}
    arrays.update(constants())
    io = {n: nc.dram_tensor(n, a.shape, F32, kind="ExternalInput").ap() for n, a in arrays.items()}
    for n, s in OUTS:
        io[n] = nc.dram_tensor(n, s, F32, kind="ExternalOutput").ap()
    program(nc, io)
    r = run_bass_kernel_spmd(nc, [arrays], core_ids=[0])
    return tuple(r.results[0][n] for n, _ in OUTS)
```
